# Optimizing a Trainium2 kernel written in Bass

```python
import math
import jax
import jax.numpy as jnp
from jax import lax
import numpy as np

D_MODEL = 2048
BATCH = 1
SEQ = 256
DEPTH = 1
DEC_BATCH = 8
DEC_SEQ = 4
PAST_LEN = 2048
PAGE_SIZE = 128

RW_HEAD = 64
RW_WIDTH = D_MODEL // 2
RW_HEADS = RW_WIDTH // RW_HEAD
RW_DECAY_RANK = 64
RW_ICLR_RANK = 64
RW_COLS = 3 * RW_WIDTH + RW_DECAY_RANK + RW_ICLR_RANK
RW_SPLITS = (RW_WIDTH, 2 * RW_WIDTH, 3 * RW_WIDTH, 3 * RW_WIDTH + RW_DECAY_RANK)
GN_EPS = 64e-5
ML_HEADS = 4
ML_V_WIDTH = D_MODEL // 2
ML_QK_WIDTH = ML_V_WIDTH // 2
ML_DV = ML_V_WIDTH // ML_HEADS
ML_DQK = ML_QK_WIDTH // ML_HEADS
ML_CHUNK = 64
ML_COLS = 2 * ML_QK_WIDTH + 2 * ML_V_WIDTH + 2 * ML_HEADS
ML_SPLITS = (ML_QK_WIDTH, 2 * ML_QK_WIDTH, 2 * ML_QK_WIDTH + ML_V_WIDTH,
             2 * ML_QK_WIDTH + 2 * ML_V_WIDTH, 2 * ML_QK_WIDTH + 2 * ML_V_WIDTH + ML_HEADS)
POOL_WIDTH = D_MODEL // 2
POOL_WINDOWS = (2, 4, 8, 16)
POOL_GROUPS = len(POOL_WINDOWS)
POOL_GW = POOL_WIDTH // POOL_GROUPS
POOL_BUF = max(POOL_WINDOWS) - 1
N_BRANCH = 3
GATE_COLS = N_BRANCH * D_MODEL
IN_COLS = RW_COLS + ML_COLS + POOL_WIDTH + GATE_COLS
IN_SPLITS = (RW_COLS, RW_COLS + ML_COLS, RW_COLS + ML_COLS + POOL_WIDTH)
MEM_LEN = 256
XA_HEADS = 4
XA_HEAD_DIM = 128
XA_WIDTH = XA_HEADS * XA_HEAD_DIM
MOE_GROUPS = 4
MOE_PER_GROUP = 8
MOE_EXPERTS = MOE_GROUPS * MOE_PER_GROUP
MOE_TOPK = 2
MOE_HIDDEN = D_MODEL // 8
RMS_EPS = 1e-6

kernel_name = "hybrid_rwkv7_mlstm_pool_hmoe_step"

def rmsnorm(x, g):
    xf = x.astype(jnp.float32)
    y = xf * lax.rsqrt(jnp.mean(xf * xf, axis=-1, keepdims=True) + RMS_EPS)
    return (y * g.astype(jnp.float32)).astype(x.dtype)

def rwkv7_mix(u, shift_prev, s_prev, mu, w0, w2, a0, a2, k_k, k_a, r_k, gn_w, gn_b):
    B, L, _ = u.shape
    f32 = jnp.float32
    u_prev = jnp.concatenate([shift_prev[:, None].astype(u.dtype), u[:, :-1]], axis=1)
    us = u + (u_prev - u) * mu
    r, k, v, wd, ad = jnp.split(us, RW_SPLITS, axis=-1)
    log_w = -jax.nn.softplus(-(w0 + jnp.tanh(wd) @ w2).astype(f32)) - 0.5
    decay = jnp.exp(-jnp.exp(log_w))
    a = jax.nn.sigmoid((a0 + ad @ a2).astype(f32))
    hd = lambda t: t.astype(f32).reshape(B, L, RW_HEADS, RW_HEAD)
    r, k, v, decay, a = hd(r), hd(k), hd(v), hd(decay), hd(a)
    kk = k * k_k.astype(f32).reshape(RW_HEADS, RW_HEAD)
    kk = kk / jnp.maximum(jnp.sqrt(jnp.sum(kk * kk, axis=-1, keepdims=True)), 1e-12)
    k = k * (1.0 + (a - 1.0) * k_a.astype(f32).reshape(RW_HEADS, RW_HEAD))
    b = kk * a

    def step(S, inp):
        r_t, w_t, k_t, v_t, kk_t, b_t = inp
        sa = jnp.einsum('bhvk,bhk->bhv', S, kk_t)
        S = S * w_t[:, :, None, :] - sa[..., None] * b_t[:, :, None, :] + v_t[..., None] * k_t[:, :, None, :]
        return S, jnp.einsum('bhvk,bhk->bhv', S, r_t)

    tm = lambda t: jnp.swapaxes(t, 0, 1)
    s_fin, y = lax.scan(step, s_prev.astype(f32), (tm(r), tm(decay), tm(k), tm(v), tm(kk), tm(b)))
    y = tm(y)
    mean = jnp.mean(y, axis=-1, keepdims=True)
    var = jnp.mean(jnp.square(y - mean), axis=-1, keepdims=True)
    y = (y - mean) * lax.rsqrt(var + GN_EPS) * gn_w.astype(f32).reshape(RW_HEADS, RW_HEAD) \
        + gn_b.astype(f32).reshape(RW_HEADS, RW_HEAD)
    y = y + jnp.sum(r * k * r_k.astype(f32).reshape(RW_HEADS, RW_HEAD), axis=-1, keepdims=True) * v
    return y.reshape(B, L, RW_WIDTH).astype(u.dtype), u[:, -1].astype(shift_prev.dtype), s_fin.astype(s_prev.dtype)

def mlstm_mix(u, c_prev, n_prev, m_prev, b_i, b_f, gn_w):
    B, L, _ = u.shape
    f32 = jnp.float32
    q, k, v, o, ig, fg = jnp.split(u.astype(f32), ML_SPLITS, axis=-1)
    q = q.reshape(B, L, ML_HEADS, ML_DQK)
    k = k.reshape(B, L, ML_HEADS, ML_DQK) * (ML_DQK ** -0.5)
    v = v.reshape(B, L, ML_HEADS, ML_DV)
    ig = ig + b_i.astype(f32)
    logf = jax.nn.log_sigmoid(fg + b_f.astype(f32))
    c = math.gcd(L, ML_CHUNK)
    nc = L // c
    ch = lambda t: t.reshape(B, nc, c, ML_HEADS, t.shape[-1]).transpose(1, 0, 3, 2, 4)
    chg = lambda t: t.reshape(B, nc, c, ML_HEADS).transpose(1, 0, 3, 2)
    causal = jnp.tril(jnp.ones((c, c), dtype=bool))

    def step(carry, inp):
        C, n, m = carry
        q_c, k_c, v_c, i_c, lf_c = inp
        bcum = jnp.cumsum(lf_c, axis=-1)
        dlog = jnp.where(causal, bcum[..., :, None] - bcum[..., None, :] + i_c[..., None, :], -jnp.inf)
        inter = bcum + m[..., None]
        m_t = jnp.maximum(inter, jnp.max(dlog, axis=-1))
        wts = jnp.exp(dlog - m_t[..., None]) * jnp.einsum('bhtd,bhsd->bhts', q_c, k_c)
        w_prev = jnp.exp(inter - m_t)
        num = w_prev[..., None] * jnp.einsum('bhtd,bhde->bhte', q_c, C) + jnp.einsum('bhts,bhse->bhte', wts, v_c)
        den = w_prev * jnp.einsum('bhtd,bhd->bht', q_c, n) + jnp.sum(wts, axis=-1)
        h = num / jnp.maximum(jnp.abs(den), jnp.exp(-m_t))[..., None]
        b_last = bcum[..., -1]
        s_log = b_last[..., None] - bcum + i_c
        m_new = jnp.maximum(b_last + m, jnp.max(s_log, axis=-1))
        ws = jnp.exp(s_log - m_new[..., None])
        wp = jnp.exp(b_last + m - m_new)
        C = wp[..., None, None] * C + jnp.einsum('bhs,bhsd,bhse->bhde', ws, k_c, v_c)
        n = wp[..., None] * n + jnp.einsum('bhs,bhsd->bhd', ws, k_c)
        return (C, n, m_new), h

    (c_fin, n_fin, m_fin), h = lax.scan(
        step, (c_prev.astype(f32), n_prev.astype(f32), m_prev.astype(f32)),
        (ch(q), ch(k), ch(v), chg(ig), chg(logf)))
    h = h.transpose(1, 0, 3, 2, 4).reshape(B, L, ML_HEADS, ML_DV)
    h = h * lax.rsqrt(jnp.mean(h * h, axis=-1, keepdims=True) + RMS_EPS) * gn_w.astype(f32).reshape(ML_HEADS, ML_DV)
    out = h * jax.nn.sigmoid(o.reshape(B, L, ML_HEADS, ML_DV))
    return (out.reshape(B, L, ML_V_WIDTH).astype(u.dtype), c_fin.astype(c_prev.dtype),
            n_fin.astype(n_prev.dtype), m_fin.astype(m_prev.dtype))

def pool_mix(u, buf, start, w_grp, scale):
    B, L, W = u.shape
    f32 = jnp.float32
    uf = u.astype(f32)
    z = jnp.concatenate([buf.astype(f32), uf], axis=1)
    cs = jnp.concatenate([jnp.zeros((B, 1, W), f32), jnp.cumsum(z, axis=1)], axis=1)
    pos = start + jnp.arange(L)
    means = []
    for g, win in enumerate(POOL_WINDOWS):
        sl = slice(g * POOL_GW, (g + 1) * POOL_GW)
        hi = cs[:, POOL_BUF + 1:POOL_BUF + 1 + L, sl]
        lo = cs[:, POOL_BUF + 1 - win:POOL_BUF + 1 - win + L, sl]
        cnt = jnp.minimum(win, pos + 1).astype(f32)
        means.append((hi - lo) / cnt[None, :, None])
    d = (jnp.concatenate(means, axis=-1) - uf).reshape(B, L, POOL_GROUPS, POOL_GW)
    out = jnp.einsum('blgc,gcd->blgd', d, w_grp.astype(f32)).reshape(B, L, W) * scale.astype(f32)
    return out.astype(u.dtype), z[:, -POOL_BUF:].astype(buf.dtype)

def memory_kv(mem, g_mem, wk, wv):
    B, M, _ = mem.shape
    mn = rmsnorm(mem, g_mem)
    return ((mn @ wk).reshape(B, M, XA_HEADS, XA_HEAD_DIM), (mn @ wv).reshape(B, M, XA_HEADS, XA_HEAD_DIM))

def cross_attend(xn, mem_k, mem_v, wq, wo):
    B, L, _ = xn.shape
    q = (xn @ wq).reshape(B, L, XA_HEADS, XA_HEAD_DIM)
    s = jnp.einsum('blhd,bmhd->bhlm', q, mem_k).astype(jnp.float32) * (XA_HEAD_DIM ** -0.5)
    p = jax.nn.softmax(s, axis=-1).astype(mem_v.dtype)
    return jnp.einsum('bhlm,bmhd->blhd', p, mem_v).reshape(B, L, XA_WIDTH) @ wo

def hmoe(xn, w_r1, b_r1, w_r2, b_r2, w_g, w_u, w_d):
    B, L, D = xn.shape
    f32 = jnp.float32
    t = xn.reshape(B * L, D)
    lg = (t @ w_r1).astype(f32) + b_r1.astype(f32)
    grp = jnp.argmax(lg, axis=-1)
    p_grp = jnp.take_along_axis(jax.nn.softmax(lg, axis=-1), grp[:, None], axis=-1)
    le = ((t @ w_r2).astype(f32) + b_r2.astype(f32)).reshape(-1, MOE_GROUPS, MOE_PER_GROUP)
    le = jnp.take_along_axis(le, grp[:, None, None], axis=1)[:, 0]
    top_v, top_i = lax.top_k(le, MOE_TOPK)
    gate = jax.nn.softmax(top_v, axis=-1) * p_grp
    eid = grp[:, None] * MOE_PER_GROUP + top_i
    comb = jnp.sum(jax.nn.one_hot(eid, MOE_EXPERTS, dtype=f32) * gate[..., None], axis=1)
    h = jax.nn.silu(jnp.einsum('td,edf->tef', t, w_g)) * jnp.einsum('td,edf->tef', t, w_u)
    h = h * comb.astype(h.dtype)[..., None]
    return jnp.einsum('tef,efd->td', h, w_d).reshape(B, L, D)

def trunk_layer(x, mem_k, mem_v, rw_shift, rw_s, ml_c, ml_n, ml_m, pool_buf, start, lp):
    B, L, _ = x.shape
    xn = rmsnorm(x, lp['g_mix'])
    u = xn @ lp['w_in']
    u_rw, u_ml, u_pool, u_gate = jnp.split(u, IN_SPLITS, axis=-1)
    o_rw, rw_shift, rw_s = rwkv7_mix(u_rw, rw_shift, rw_s, lp['rw_mu'], lp['rw_w0'], lp['rw_w2'], lp['rw_a0'],
                                     lp['rw_a2'], lp['rw_k_k'], lp['rw_k_a'], lp['rw_r_k'], lp['rw_gn_w'], lp['rw_gn_b'])
    o_ml, ml_c, ml_n, ml_m = mlstm_mix(u_ml, ml_c, ml_n, ml_m, lp['ml_b_i'], lp['ml_b_f'], lp['ml_gn_w'])
    o_pool, pool_buf = pool_mix(u_pool, pool_buf, start, lp['pool_w'], lp['pool_scale'])
    g = jax.nn.sigmoid(u_gate.astype(jnp.float32)).astype(x.dtype).reshape(B, L, N_BRANCH, D_MODEL)
    merged = (g[:, :, 0] * (o_rw @ lp['w_up_rwkv']) + g[:, :, 1] * (o_ml @ lp['w_up_mlstm'])
              + g[:, :, 2] * (o_pool @ lp['w_up_pool']))
    x = x + merged @ lp['w_out']
    x = x + cross_attend(rmsnorm(x, lp['g_xa']), mem_k, mem_v, lp['xa_wq'], lp['xa_wo'])
    x = x + hmoe(rmsnorm(x, lp['g_moe']), lp['moe_wr1'], lp['moe_br1'], lp['moe_wr2'], lp['moe_br2'],
                 lp['moe_wg'], lp['moe_wu'], lp['moe_wd'])
    return x, rw_shift, rw_s, ml_c, ml_n, ml_m, pool_buf

def setup_inputs(seed: int = 0) -> dict:
    key = jax.random.key(seed)
    ks = iter(jax.random.split(key, 64))
    f32 = jnp.float32
    nrm = lambda shape, s: s * jax.random.normal(next(ks), shape, f32)
    gain = lambda shape: 1.0 + nrm(shape, 0.02)
    return {
        'x_prompt': nrm((BATCH, SEQ, D_MODEL), 1.0),
        'x_sample': nrm((DEC_BATCH, DEC_SEQ, D_MODEL), 1.0),
        'cache_mem_k': nrm((DEPTH, DEC_BATCH, MEM_LEN, XA_HEADS, XA_HEAD_DIM), 1.0),
        'cache_mem_v': nrm((DEPTH, DEC_BATCH, MEM_LEN, XA_HEADS, XA_HEAD_DIM), 1.0),
        'state_rwkv_s': nrm((DEPTH, DEC_BATCH, RW_HEADS, RW_HEAD, RW_HEAD), 0.1),
        'state_rwkv_shift': nrm((DEPTH, DEC_BATCH, RW_COLS), 1.0),
        'state_mlstm_c': nrm((DEPTH, DEC_BATCH, ML_HEADS, ML_DQK, ML_DV), 0.1),
        'state_mlstm_n': nrm((DEPTH, DEC_BATCH, ML_HEADS, ML_DQK), 0.1),
        'state_mlstm_m': nrm((DEPTH, DEC_BATCH, ML_HEADS), 1.0),
        'state_pool': nrm((DEPTH, DEC_BATCH, POOL_BUF, POOL_WIDTH), 1.0),
        'mem_prompt': nrm((BATCH, MEM_LEN, D_MODEL), 1.0),
        'g_mix': gain((DEPTH, D_MODEL)),
        'w_in': nrm((DEPTH, D_MODEL, IN_COLS), D_MODEL ** -0.5),
        'rw_mu': jax.random.uniform(next(ks), (DEPTH, RW_COLS), f32),
        'rw_w0': jax.random.uniform(next(ks), (DEPTH, RW_WIDTH), f32, minval=-6.0, maxval=-1.0),
        'rw_w2': nrm((DEPTH, RW_DECAY_RANK, RW_WIDTH), 0.1 * RW_DECAY_RANK ** -0.5),
        'rw_a0': nrm((DEPTH, RW_WIDTH), 0.1),
        'rw_a2': nrm((DEPTH, RW_ICLR_RANK, RW_WIDTH), 0.1 * RW_ICLR_RANK ** -0.5),
        'rw_k_k': 0.85 + nrm((DEPTH, RW_WIDTH), 0.02),
        'rw_k_a': gain((DEPTH, RW_WIDTH)),
        'rw_r_k': nrm((DEPTH, RW_WIDTH), 0.1),
        'rw_gn_w': gain((DEPTH, RW_WIDTH)),
        'rw_gn_b': nrm((DEPTH, RW_WIDTH), 0.02),
        'ml_b_i': nrm((DEPTH, ML_HEADS), 0.5),
        'ml_b_f': 3.0 + nrm((DEPTH, ML_HEADS), 0.5),
        'ml_gn_w': gain((DEPTH, ML_V_WIDTH)),
        'pool_w': nrm((DEPTH, POOL_GROUPS, POOL_GW, POOL_GW), POOL_GW ** -0.5),
        'pool_scale': 1.0 + nrm((DEPTH, POOL_WIDTH), 0.1),
        'w_up_rwkv': nrm((DEPTH, RW_WIDTH, D_MODEL), RW_WIDTH ** -0.5),
        'w_up_mlstm': nrm((DEPTH, ML_V_WIDTH, D_MODEL), ML_V_WIDTH ** -0.5),
        'w_up_pool': nrm((DEPTH, POOL_WIDTH, D_MODEL), POOL_WIDTH ** -0.5),
        'w_out': nrm((DEPTH, D_MODEL, D_MODEL), D_MODEL ** -0.5),
        'g_xa': gain((DEPTH, D_MODEL)),
        'g_mem': gain((DEPTH, D_MODEL)),
        'xa_wq': nrm((DEPTH, D_MODEL, XA_WIDTH), D_MODEL ** -0.5),
        'xa_wk': nrm((DEPTH, D_MODEL, XA_WIDTH), D_MODEL ** -0.5),
        'xa_wv': nrm((DEPTH, D_MODEL, XA_WIDTH), D_MODEL ** -0.5),
        'xa_wo': nrm((DEPTH, XA_WIDTH, D_MODEL), XA_WIDTH ** -0.5),
        'g_moe': gain((DEPTH, D_MODEL)),
        'moe_wr1': nrm((DEPTH, D_MODEL, MOE_GROUPS), D_MODEL ** -0.5),
        'moe_br1': nrm((DEPTH, MOE_GROUPS), 0.01),
        'moe_wr2': nrm((DEPTH, D_MODEL, MOE_EXPERTS), D_MODEL ** -0.5),
        'moe_br2': nrm((DEPTH, MOE_EXPERTS), 0.01),
        'moe_wg': nrm((DEPTH, MOE_EXPERTS, D_MODEL, MOE_HIDDEN), D_MODEL ** -0.5),
        'moe_wu': nrm((DEPTH, MOE_EXPERTS, D_MODEL, MOE_HIDDEN), D_MODEL ** -0.5),
        'moe_wd': nrm((DEPTH, MOE_EXPERTS, MOE_HIDDEN, D_MODEL), MOE_HIDDEN ** -0.5),
        'g_final': gain((D_MODEL,)),
    }

def reference(x_prompt, x_sample, cache_mem_k, cache_mem_v, state_rwkv_s, state_rwkv_shift, state_mlstm_c,
              state_mlstm_n, state_mlstm_m, state_pool, mem_prompt, g_mix, w_in, rw_mu, rw_w0, rw_w2, rw_a0, rw_a2,
              rw_k_k, rw_k_a, rw_r_k, rw_gn_w, rw_gn_b, ml_b_i, ml_b_f, ml_gn_w, pool_w, pool_scale, w_up_rwkv,
              w_up_mlstm, w_up_pool, w_out, g_xa, g_mem, xa_wq, xa_wk, xa_wv, xa_wo, g_moe, moe_wr1, moe_br1,
              moe_wr2, moe_br2, moe_wg, moe_wu, moe_wd, g_final):
    def layer_params(l):
        return dict(g_mix=g_mix[l], w_in=w_in[l], rw_mu=rw_mu[l], rw_w0=rw_w0[l], rw_w2=rw_w2[l], rw_a0=rw_a0[l],
                    rw_a2=rw_a2[l], rw_k_k=rw_k_k[l], rw_k_a=rw_k_a[l], rw_r_k=rw_r_k[l], rw_gn_w=rw_gn_w[l],
                    rw_gn_b=rw_gn_b[l], ml_b_i=ml_b_i[l], ml_b_f=ml_b_f[l], ml_gn_w=ml_gn_w[l], pool_w=pool_w[l],
                    pool_scale=pool_scale[l], w_up_rwkv=w_up_rwkv[l], w_up_mlstm=w_up_mlstm[l],
                    w_up_pool=w_up_pool[l], w_out=w_out[l], g_xa=g_xa[l], xa_wq=xa_wq[l], xa_wo=xa_wo[l],
                    g_moe=g_moe[l], moe_wr1=moe_wr1[l], moe_br1=moe_br1[l], moe_wr2=moe_wr2[l],
                    moe_br2=moe_br2[l], moe_wg=moe_wg[l], moe_wu=moe_wu[l], moe_wd=moe_wd[l])

    B = x_prompt.shape[0]
    dt = x_prompt.dtype
    yp = x_prompt
    p_rs, p_sh, p_c, p_n, p_m, p_pl, p_mk, p_mv = [], [], [], [], [], [], [], []
    for l in range(DEPTH):
        lp = layer_params(l)
        mk, mv = memory_kv(mem_prompt, g_mem[l], xa_wk[l], xa_wv[l])
        yp, sh, rs, c, n, m, pl = trunk_layer(
            yp, mk, mv, jnp.zeros((B, RW_COLS), dt), jnp.zeros((B, RW_HEADS, RW_HEAD, RW_HEAD), dt),
            jnp.zeros((B, ML_HEADS, ML_DQK, ML_DV), dt), jnp.zeros((B, ML_HEADS, ML_DQK), dt),
            jnp.zeros((B, ML_HEADS), dt), jnp.zeros((B, POOL_BUF, POOL_WIDTH), dt), 0, lp)
        p_rs.append(rs); p_sh.append(sh); p_c.append(c); p_n.append(n); p_m.append(m); p_pl.append(pl)
        p_mk.append(mk); p_mv.append(mv)
    y_prompt = rmsnorm(yp, g_final)

    ys = x_sample
    s_rs, s_sh, s_c, s_n, s_m, s_pl = [], [], [], [], [], []
    for l in range(DEPTH):
        lp = layer_params(l)
        ys, sh, rs, c, n, m, pl = trunk_layer(
            ys, cache_mem_k[l], cache_mem_v[l], state_rwkv_shift[l], state_rwkv_s[l], state_mlstm_c[l],
            state_mlstm_n[l], state_mlstm_m[l], state_pool[l], PAST_LEN, lp)
        s_rs.append(rs); s_sh.append(sh); s_c.append(c); s_n.append(n); s_m.append(m); s_pl.append(pl)
    y_sample = rmsnorm(ys, g_final)

    return (y_prompt, y_sample,
            jnp.stack(p_rs), jnp.stack(p_sh), jnp.stack(p_c), jnp.stack(p_n), jnp.stack(p_m), jnp.stack(p_pl),
            jnp.stack(p_mk), jnp.stack(p_mv),
            jnp.stack(s_rs), jnp.stack(s_sh), jnp.stack(s_c), jnp.stack(s_n), jnp.stack(s_m), jnp.stack(s_pl))


_drawn_inputs = setup_inputs


def setup_inputs(seed=0):
    import zlib

    import numpy as np

    out = dict(_drawn_inputs(seed))
    spreads = {}
    factors = {'rw_w2': 8.0,
     'rw_k_k': 2.983,
     'rw_k_a': 2.714,
     'rw_gn_w': 3.033,
     'ml_gn_w': 3.767,
     'g_xa': 8.0,
     'g_mem': 2.832,
     'moe_br1': 19.805,
     'moe_br2': 12.648,
     'g_final': 8.077,
     'rw_gn_b': 3.106,
     'g_moe': 5.723}
    for name, (base, spread) in spreads.items():
        noise = np.random.default_rng([zlib.crc32(name.encode()), seed]).standard_normal(out[name].shape)
        drawn = base * np.exp(spread * noise) if base else spread * noise
        out[name] = jnp.asarray(drawn.astype(out[name].dtype))
    for name, factor in factors.items():
        out[name] = (out[name] * factor).astype(out[name].dtype)
    return out
```

```python
from contextlib import ExitStack

import numpy as np
import concourse.bass as bass
from concourse import mybir

F32 = mybir.dt.float32
ALU = mybir.AluOpType
ACT = mybir.ActivationFunctionType
AX = mybir.AxisListType

P = 128
D = 2048
KD = D // P
NPR = 256
NB, NL = 8, 4
NSM = NB * NL
T = NPR + NSM
HALF = D // 2
KH = HALF // P
RWT = 25
XW = 1 + NPR + NB * (1 + NL)
MLH, DQK, DV = 4, 128, 256
BUF = 15
PW = BUF + NPR + NB * (BUF + NL)
PS0 = BUF + NPR
WINDOWS = (2, 4, 8, 16)
MEM = 256
XH = 4
NE = 32
SLOT = 4096
ALPHA = float(np.exp(-0.5))
RMS_EPS, GN_EPS = 1e-6, 64e-5

LEVELS = (1, 2, 4, 8, 16, 32, 64)


def constants():
    s = np.arange(P)[:, None]
    t = np.arange(P)[None, :]
    c = {}
    c["ident"] = (s == t)
    c["lt_le"] = np.concatenate([s < t, s <= t], 1)
    for m in LEVELS:
        c[f"level{m}"] = (s // (2 * m) == t // (2 * m)) & (s // m < t // m)
    c["heads"] = (s // 64 == t // 64)
    c["heads_mean"] = (s // 64 == t // 64) / 64.0
    c["ones"] = np.ones((P, P))
    c["ones_dv"] = np.full((P, P), 1.0 / DV)
    same = (s // NL == t // NL)[:, :NSM] & (s < NSM)
    c["seq_lt_le"] = np.concatenate([same & (s < t)[:, :NSM], same & (s <= t)[:, :NSM]], 1)
    for m in (1, 2):
        c[f"seq_level{m}"] = c[f"level{m}"][:, :NSM] & (s < NSM)
    c["of_seq"] = ((s % NSM) // NL == np.arange(NB)[None, :])
    col = np.arange(T)
    first_ml = (col == 0) | ((col >= NPR) & ((col - NPR) % NL == 0))
    c["run_rw"] = np.tile(~(first_ml | (col == P)), (P, 1))
    c["run_ml"] = np.tile(~first_ml, (P, 1))
    c["restart"] = np.tile(np.where(first_ml, -1e30, 0.0), (P, 1))
    c["head_row"] = (s == (np.arange(MLH * P) // P)[None, :])
    c["inv_count"] = np.tile(np.concatenate([1.0 / np.minimum(w, np.arange(16) + 1) for w in WINDOWS]), (P, 1))
    c["slot_id"] = np.tile(np.arange(64), (P, 1))
    c["expert_id"] = np.tile(np.arange(NE), (P, 1))
    at, o = {}, 0
    for n, a in c.items():
        at[n] = (o, o + a.shape[1])
        o += a.shape[1]
    return np.concatenate([a.astype(np.float32) for a in c.values()], 1), at


CONST, CONST_AT = constants()

PARAMS = [("mu", RWT), ("w0", KH), ("a0", KH), ("k_k", KH), ("k_a", KH), ("r_k", KH), ("gn_w", KH), ("gn_b", KH),
          ("ml_gn", KH), ("pool_scale", KH), ("g_mix", KD), ("g_xa", KD), ("g_mem", KD), ("g_moe", KD), ("g_final", KD)]
PARAM_AT, _o = {}, 0
for _n, _w in PARAMS:
    PARAM_AT[_n] = _o
    _o += _w
NPARAM = _o


class Steps:

    def __init__(self, ctx, nc, name, steps):
        self.sem = ctx.enter_context(nc.semaphore(name))
        self.steps = list(steps)
        assert len(set(self.steps)) == len(self.steps)
        self.place = {s: n + 1 for n, s in enumerate(self.steps)}
        self.n = len(self.steps)
        self.next = 0
        self.lap = 0

    def at(self, step, i=0):
        return (i + self.lap) * self.n + self.place[step]

    def done(self, ins, step):
        assert self.steps[self.next % self.n] == step, (step, self.steps[self.next % self.n])
        self.next += 1
        ins.then_inc(self.sem, 1)


NPAST = RWT * NB + KH * NB * BUF


def program(nc, A, O):
    with ExitStack() as ctx:
        def sb(name, shape, c=ctx):
            return c.enter_context(nc.sbuf_tensor(name, shape, F32))

        def sem(name, c=ctx):
            return c.enter_context(nc.semaphore(name))

        const = sb("const", [P, CONST.shape[1]])
        param = sb("param", [P, NPARAM])
        ring = sb("ring", [P, 4, SLOT])
        xn = sb("xn", [P, KD, T])
        mrg = sb("mrg", [P, KD, T])
        ps = ctx.enter_context(nc.psum_tensor("ps", [P, 8, 512], F32))

        def K(name, rows=P, a=0, b=None, base=0):
            lo, hi = CONST_AT[name]
            return const[base:base + rows, lo + a:(hi if b is None else lo + b)]

        def par(name, i=0):
            if isinstance(i, int):
                return param[:, PARAM_AT[name] + i:PARAM_AT[name] + i + 1]
            return param[:, bass.ds(i + PARAM_AT[name], 1)]

        s_load = sem("s_load")
        with ExitStack() as mix:
            rwx = sb("rwx", [P, RWT, XW], mix)
            o_ml = sb("o_ml", [P, KH, T], mix)
            o_pool = sb("o_pool", [P, KH, T], mix)
            with ExitStack() as c:
                mlu = sb("mlu", [P, 24, T], c)
                poolx = sb("poolx", [P, KH, PW], c)
                gif = sb("gif", [8, T], c)
                stage_project(nc, ctx, A, O, locals())
                stage_mlstm(nc, ctx, A, O, locals())
            stage_rwkv(nc, ctx, A, O, locals())
            stage_merge(nc, ctx, A, O, locals())
        stage_cross(nc, ctx, A, O, locals())
        stage_moe(nc, ctx, A, O, locals())


def stage_project(nc, ctx0, A, O, env):
    ring, xn, mrg, ps, const, param, K, par, rwx, mlu, poolx, gif = (
        env[k] for k in "ring xn mrg ps const param K par rwx mlu poolx gif".split())
    ITER, G = 7, 4
    with ExitStack() as ctx:
        sem = lambda n: ctx.enter_context(nc.semaphore(n))
        sq = ctx.enter_context(nc.sbuf_tensor("sq", [P, 2, T], F32))
        rstd = ctx.enter_context(nc.sbuf_tensor("rstd", [P, T], F32))
        past_in = env["o_ml"][:, :, :].rearrange("p k t -> p (k t)")[:, 0:NPAST]
        loaded, past = sem("p_loaded"), sem("p_past")
        slot = [sem(f"p_slot{s}") for s in range(G)]
        odd = sem("p_odd")
        squared = sem("p_squared")
        rooted = sem("p_rooted")
        summed = sem("p_summed")
        v = Steps(ctx, nc, "p_vec", ["zero", "var", "rstd"] + [f"xn{k}" for k in range(KD)])
        tile_done = sem("p_tile")
        evac = sem("p_evac")
        block = ctx.enter_context(nc.Block())

        @block.sync
        def _(sp):
            sp.dma_start(mrg[:, :, :], A["xT"][:, :, :]).then_inc(loaded, 16)
            sp.dma_start(const[:, :], A["const"][:, :]).then_inc(loaded, 16)
            sp.dma_start(param[:, :], A["param"][:, :]).then_inc(loaded, 16)
            for s in range(G):
                sp.dma_start(ring[:, s, :], A["w_main"][s, :, :]).then_inc(slot[s], 16)
            sp.dma_start(past_in, A["past"][:, :]).then_inc(past, 16)
            with sp.Fori(1, ITER) as i:
                for s in range(G):
                    sp.wait_ge(tile_done, i * 8 - 8 + 2 * s + 2)
                    sp.dma_start(ring[:, s, :], A["w_main"][bass.ds(i * G + s, 1), :, :].rearrange("o p n -> (o p) n")
                                 ).then_inc(slot[s], 16)
            sp.wait_ge(tile_done, 8 * ITER)
            sp.dma_start(ring[:, 0, 0:16 * 136], A["w_odd"][:, :]).then_inc(odd, 16)

        @block.scalar
        def _(act):
            act.wait_ge(loaded, 48)
            for k in range(KD):
                if k >= 2:
                    act.wait_ge(summed, k - 1)
                nc.scalar.activation(sq[:, k % 2, :], mrg[:, k, :], ACT.Square).then_inc(squared, 1)

            act.wait_ge(v.sem, v.at("var"))
            nc.scalar.activation(rstd[:, :], rstd[:, :], ACT.Sqrt).then_inc(rooted, 1)

            def evacuate(outs, b, i, scale=1.0):
                act.wait_ge(tile_done, i * 8 + b + 1)
                for n, (o, lo, hi, seq) in enumerate(outs):
                    src = ps[:, b, lo:hi]
                    if seq:
                        src = src.rearrange("p (b l) -> p b l", l=NL)
                    ins = nc.scalar.activation(o, src, ACT.Copy, scale=scale)
                ins.then_inc(evac, 1)

            def rw_out(j):
                a = rwx[:, bass.ds(j, 1), :].rearrange("p o x -> p (o x)")
                return [(a[:, 1:1 + NPR], 0, NPR, False),
                        (a[:, 1 + NPR:XW].rearrange("p (b l) -> p b l", b=NB)[:, :, 1:1 + NL], NPR, T, True)]
            with act.Fori(0, 3) as i:
                for b in range(8):
                    evacuate(rw_out(i * 8 + b), b, i)
            for i in range(3, 6):
                for b in range(8):
                    evacuate([(mlu[:, (i - 3) * 8 + b, :], 0, T, False)], b, i,
                             DQK ** -0.5 if i == 3 and b >= 4 else 1.0)
            for b in range(8):
                evacuate([(poolx[:, b, BUF:PS0], 0, NPR, False),
                          (poolx[:, b, PS0:PW].rearrange("p (b r) -> p b r", b=NB)[:, :, BUF:BUF + NL], NPR, T, True)],
                         b, 6)
            evacuate([(rwx[:, 24, 1:1 + NPR], 0, NPR, False),
                      (rwx[:, 24, 1 + NPR:XW].rearrange("p (b l) -> p b l", b=NB)[:, :, 1:1 + NL], NPR, T, True)], 0, 7)
            act.wait_ge(tile_done, 58)
            nc.scalar.activation(gif[:, :], ps[0:8, 1, 0:T], ACT.Copy).then_inc(evac, 1)

        @block.vector
        def _(dve):
            nc.vector.memset(rwx[:, :, 0:1], 0.0)
            nc.vector.memset(poolx[:, :, 0:BUF], 0.0)
            dve.wait_ge(past, 16)
            nc.vector.tensor_copy(rwx[:, :, XW - 5 * NB:XW:5], past_in[:, 0:RWT * NB].rearrange("p (t b) -> p t b", b=NB))
            for j in range(KH):
                n = RWT * NB + j * NB * BUF
                ins = nc.vector.tensor_copy(poolx[:, j, PS0:PW].rearrange("p (b r) -> p b r", b=NB)[:, :, 0:BUF],
                                            past_in[:, n:n + NB * BUF].rearrange("p (b r) -> p b r", b=NB))
            v.done(ins, "zero")
            dve.wait_ge(summed, KD)
            v.done(nc.vector.tensor_scalar(rstd[:, :], ps[:, 7, 0:T], 1.0 / D, RMS_EPS, ALU.mult, ALU.add), "var")
            dve.wait_ge(v.sem, v.at("var"))
            dve.wait_ge(rooted, 1)
            v.done(nc.vector.reciprocal(rstd[:, :], rstd[:, :]), "rstd")
            dve.wait_ge(v.sem, v.at("rstd"))
            for k in range(KD):
                v.done(nc.vector.scalar_tensor_tensor(out=xn[:, k, :], in0=mrg[:, k, :], scalar=par("g_mix", k),
                                                      in1=rstd[:, :], op0=ALU.mult, op1=ALU.mult), f"xn{k}")

        @block.tensor
        def _(pe):
            pe.wait_ge(loaded, 48)
            for k in range(KD):
                pe.wait_ge(squared, k + 1)
                nc.tensor.matmul(ps[:, 7, 0:T], K("ones"), sq[:, k % 2, :], start=(k == 0), stop=(k == KD - 1)
                                 ).then_inc(summed, 1)
            pe.wait_ge(v.sem, v.at(f"xn{KD - 1}"))
            w = ring[:, :, :].rearrange("p s (k n) -> p s k n", k=KD)

            def tiles(s, i):
                pe.wait_ge(slot[s], i * 16 + 16)
                for h in range(2):
                    if not (isinstance(i, int) and i == 0):
                        pe.wait_ge(evac, i * 8 - 8 + 2 * s + h + 1)
                    for k in range(KD):
                        ins = nc.tensor.matmul(ps[:, 2 * s + h, 0:T], w[:, s, k, h * P:(h + 1) * P], xn[:, k, :],
                                               start=(k == 0), stop=(k == KD - 1))
                    ins.then_inc(tile_done, 1)
            for s in range(G):
                tiles(s, 0)
            with pe.Fori(1, ITER) as i:
                for s in range(G):
                    tiles(s, i)
            pe.wait_ge(odd, 16)
            wo = ring[:, 0, 0:16 * 136].rearrange("p (k n) -> p k n", k=KD)
            for b, lo, hi in ((0, 0, P), (1, P, 136)):
                pe.wait_ge(evac, 48 + b + 1)
                for k in range(KD):
                    ins = nc.tensor.matmul(ps[0:hi - lo, b, 0:T], wo[:, k, lo:hi], xn[:, k, :],
                                           start=(k == 0), stop=(k == KD - 1))
                ins.then_inc(tile_done, 1)


def stage_mlstm(nc, ctx0, A, O, env):
    ring, xn, mrg, ps, const, param, K, par, rwx, mlu, poolx, gif, o_ml, o_pool = (
        env[k] for k in "ring xn mrg ps const param K par rwx mlu poolx gif o_ml o_pool".split())
    with ExitStack() as ctx:
        sem = lambda n: ctx.enter_context(nc.semaphore(n))
        H = range(MLH)
        cst = ring[:, 0, :].rearrange("p (h b e) -> p h b e", h=2, b=NB)
        vt = ring[:, 1, 0:3072].rearrange("p (c n) -> p c n", c=3)
        kt = ring[:, 1, 3072:3456].rearrange("p (c n) -> p c n", c=3)
        expo = ring[:, 2, 0:416]
        wts = ring[:, 2, 416:832]
        sq = ring[:, 2, 832:1408].rearrange("p (k t) -> p k t", k=2)
        dn = ring[:, 2, 1408:1696]
        qw = ring[:, 2, 1696:1728]
        qn = ring[:, 2, 1728:1760]
        wp = ring[:, 2, 1760:1792]
        win = [ring[:, 2, 1792 + 846 * i:2638 + 846 * i].rearrange("p (k t) -> p k t", k=2) for i in range(2)]
        vx = ring[0:NSM, 3, 0:2048].rearrange("p (b e) -> p b e", b=NB)
        pw = ring[:, 3, 2048:4096].rearrange("p (g k n) -> p g k n", g=4, k=2)
        row = lambda j: mrg[0:4, j, :]
        ig, fx, ln, lf, bcum, g, M, m, emt = (row(j) for j in range(9))
        wprev, ws = ln, fx
        seq = lambda a: a[:, NPR:T].rearrange("p (b l) -> p b l", l=NL)
        cp = [mrg[:, 9 + i, 0:DV] for i in range(2)]
        gt = mrg[:, 11, 0:24]
        nout = mrg[:, 11, 24:60].rearrange("p (h b) -> p h b", h=MLH)
        small = mrg[:, 11, 60:102]
        n_in = small[:, 0:32].rearrange("p (h b) -> p h b", h=MLH)
        b_i, b_f, m_prev = small[0:4, 32:33], small[0:4, 33:34], small[0:4, 34:42]
        pout = mrg[:, 12:16, :].rearrange("p k t -> p (k t)")[:, 0:KH * 9 * BUF]
        pout = pout.rearrange("p (k b r) -> p k b r", k=KH, b=9)
        sout = ctx.enter_context(nc.sbuf_tensor("sout", [P, RWT, 9], F32))

        loaded, pool_w = sem("m_loaded"), sem("m_poolw")
        c_in = [sem(f"m_c{i}") for i in range(2)]
        c_out = [sem(f"m_co{i}") for i in range(2)]
        cp_out = [sem(f"m_cpo{i}") for i in range(2)]
        stored = sem("m_stored")
        scanned = sem("m_inner")
        pe_steps = ["fg"] + [f"vt{c}{e}" for c in range(3) for e in range(2)] + ["gt"]
        for h in H:
            pe_steps += [f"s{h}", f"b{h}", f"k{h}", f"n{h}", f"u{h}"] + [f"d{h}{j}" for j in range(4)] + [f"pool{h}"]
        q = Steps(ctx, nc, "m_pe", pe_steps + [f"q{h}" for h in H])
        dve_steps = ["fx", "ig", "mn", "lf", "bcum", "g", "gmax", "M", "m", "wd", "wl", "sout"]
        for h in H:
            dve_steps += [f"x{h}", f"qw{h}", f"qn{h}", f"w{h}", f"wm{h}", f"k{h}", f"max{h}", f"rec{h}", f"h{h}", f"n{h}"]
            dve_steps += [f"c{h}{j}" for j in range(4)]
        dve_steps += [f"v{h}" for h in H] + ["rs"] + [f"y{k}" for k in range(KH)] + [f"o{k}" for k in range(KH)]
        v = Steps(ctx, nc, "m_dve", dve_steps)
        act_steps = ["sig", "abs", "exp", "ln"] + [f"vt{c}{e}" for c in range(3) for e in range(2)] + ["emt", "wprev", "ws", "gt"]
        for h in H:
            act_steps += [f"wp{h}", f"e{h}", f"abs{h}", f"cp{h}", f"pool{h}"]
        a = Steps(ctx, nc, "m_act", act_steps + [f"sq{h}" for h in H] + ["root"])
        pool_steps = []
        for h in H:
            pool_steps += [f"add{h}{i}" for i in range(h + 1)] + [f"mean{h}", f"first{h}", f"d{h}"]
            if h == 0:
                pool_steps += ["pout"]
            pool_steps += [f"vx{h}"]
        g_ = Steps(ctx, nc, "m_pool", pool_steps)
        def store(sp, h):
            sp.wait_ge(a.sem, a.at(f"cp{h}"))
            sp.dma_start(O["ml_cp"][h, :, :], cp[h % 2]).then_inc(cp_out[h % 2], 16)
            sp.wait_ge(v.sem, v.at(f"c{h}3"))
            sp.dma_start(O["ml_cs"][h, :, :, :], cst[:, h % 2, :, :]).then_inc(c_out[h % 2], 16)

        block = ctx.enter_context(nc.Block())

        @block.sync
        def _(sp):
            sp.dma_start(small, A["ml_small"][:, :]).then_inc(loaded, 16)
            sp.dma_start(pw, A["pool_w"][:, :, :, :]).then_inc(pool_w, 16)
            for h in H:
                if h >= 2:
                    sp.wait_ge(c_out[h % 2], 16)
                sp.dma_start(cst[:, h % 2, :, :], A["c_in"][h, :, :, :]).then_inc(c_in[h % 2], 16)
                if h >= 1:
                    store(sp, h - 1)
            store(sp, MLH - 1)
            sp.wait_ge(v.sem, v.at(f"n{MLH - 1}"))
            sp.dma_start(O["ml_n"][:, :, :], nout).then_inc(stored, 16)
            sp.dma_start(O["ml_m"][:, :], m).then_inc(stored, 16)
            sp.dma_start(O["shift"][:, :, :], sout[:, :, :]).then_inc(stored, 16)
            sp.wait_ge(g_.sem, g_.at("pout"))
            sp.dma_start(O["pool"][:, :, :, :], pout).then_inc(stored, 16)
            sp.wait_ge(stored, 64)
            for i in range(2):
                sp.wait_ge(c_out[i], 32)
                sp.wait_ge(cp_out[i], 32)

        @block.tensor
        def _(pe):
            mm, ident = nc.tensor.matmul, K("ident")
            q.done(mm(ps[0:4, 0, 0:T], const[0:8, CONST_AT["ident"][0] + 4:CONST_AT["ident"][0] + 8], gif[:, :],
                      start=True, stop=True), "fg")
            for c in range(3):
                n = P if c < 2 else NSM
                for e in range(2):
                    b = 1 + 2 * c + e
                    for j in range(4):
                        ins = nc.tensor.transpose(ps[0:n, b, j * P:(j + 1) * P],
                                                  mlu[:, 8 + 4 * e + j, c * P:c * P + n], ident)
                    q.done(ins, f"vt{c}{e}")
            pe.wait_ge(a.sem, a.at("ws"))
            for c in range(3):
                n = P if c < 2 else NSM
                for i, r in enumerate((g, ws)):
                    ins = nc.tensor.transpose(ps[0:n, 7, c * 8 + 4 * i:c * 8 + 4 * i + 4], r[:, c * P:c * P + n],
                                              K("ident", 4, 0, 4))
            q.done(ins, "gt")
            pe.wait_ge(a.sem, a.at("vt21"))
            pe.wait_ge(loaded, 16)
            for h in H:
                qh, kh = mlu[:, h, :], mlu[:, 4 + h, :]
                if h:
                    pe.wait_ge(v.sem, v.at(f"w{h - 1}"))
                    pe.wait_ge(v.sem, v.at(f"c{h - 1}3"))
                else:
                    pe.wait_ge(v.sem, v.at("fx"))
                mm(ps[:, 0, 0:NPR], kh[:, 0:P], qh[:, 0:NPR], start=True, stop=True)
                mm(ps[:, 0, NPR:NPR + P], kh[:, P:NPR], qh[:, P:NPR], start=True, stop=True)
                q.done(mm(ps[0:NSM, 0, 384:416], kh[:, NPR:T], qh[:, NPR:T], start=True, stop=True), f"s{h}")
                sel = const[0:4, CONST_AT["head_row"][0] + h * P:CONST_AT["head_row"][0] + (h + 1) * P]
                if h:
                    pe.wait_ge(v.sem, v.at(f"max{h - 1}"))
                mm(ps[:, 1, 0:T], sel, M, start=True, stop=True)
                mm(ps[:, 3, 0:T], sel, emt, start=True, stop=True)
                q.done(mm(ps[:, 3, T:T + NSM], sel, wprev[:, NPR:T], start=True, stop=True), f"b{h}")
                if h == 0:
                    pe.wait_ge(a.sem, a.at("vt21"))
                for c in range(3):
                    n = P if c < 2 else NSM
                    ins = nc.tensor.transpose(ps[0:n, 6, c * P:(c + 1) * P], kh[:, c * P:c * P + n], ident)
                q.done(ins, f"k{h}")
                pe.wait_ge(v.sem, v.at(f"wm{h}"))
                pe.wait_ge(v.sem, v.at(f"qn{h}"))
                w0, w1, wsm = wts[:, 0:NPR], wts[:, NPR:384], wts[0:NSM, 384:416]
                one = K("ones")
                mm(ps[:, 2, 0:NPR], one, w0, start=True, stop=False)
                mm(ps[:, 2, P:NPR], one, w1, start=False, stop=False)
                mm(ps[:, 2, NPR:T], K("ones", NSM), wsm, start=False, stop=False)
                mm(ps[:, 2, NPR:T], one, qn, start=False, stop=True)
                pe.wait_ge(c_in[h % 2], 16 * (h // 2 + 1))
                for e in range(2):
                    f = h * DV + e * P
                    o = ps[:, 4 + e, :]
                    mm(o[:, 0:NPR], vt[:, 0, f:f + P], w0, start=True, stop=False)
                    mm(o[:, P:NPR], vt[:, 1, f:f + P], w1, start=False, stop=False)
                    mm(o[:, NPR:T], vt[0:NSM, 2, f:f + P], wsm, start=False, stop=False)
                    for b in range(NB):
                        ins = mm(o[:, NPR + NL * b:NPR + NL * b + NL], cst[:, h % 2, b, e * P:(e + 1) * P],
                                 qw[:, NL * b:NL * b + NL], start=False, stop=(b == NB - 1))
                q.done(ins, f"n{h}")
                pe.wait_ge(v.sem, v.at(f"k{h}"))
                if h:
                    pe.wait_ge(v.sem, v.at(f"c{h - 1}3"))
                else:
                    pe.wait_ge(a.sem, a.at("gt"))
                for o, r0, r1 in ((ps[:, 7, 0:DV], vt[:, 0, h * DV:(h + 1) * DV], vt[:, 1, h * DV:(h + 1) * DV]),
                                  (ps[:, 7, DV:DV + 1], K("ones")[:, 0:1], K("ones")[:, 0:1])):
                    mm(o, kt[:, 0, :], r0, start=True, stop=False)
                    mm(o, kt[:, 1, :], r1, start=False, stop=True)
                q.done(mm(ps[:, 7, DV + 1:DV + 1 + NB], kt[0:NSM, 2, :], K("of_seq", NSM), start=True, stop=True), f"u{h}")
                pe.wait_ge(g_.sem, g_.at(f"vx{h}"))
                for j in range(4):
                    if j == 0:
                        pe.wait_ge(v.sem, v.at(f"n{h}"))
                        pe.wait_ge(a.sem, a.at(f"cp{h}"))
                    if j == 1:
                        pe.wait_ge(v.sem, v.at(f"x{h}"))
                    if j >= 2:
                        pe.wait_ge(v.sem, v.at(f"c{h}{j - 2}"))
                    q.done(mm(ps[:, 7 if j % 2 == 0 else 1, :], kt[0:NSM, 2, :], vx[:, 2 * j:2 * j + 2, :], start=True, stop=True),
                           f"d{h}{j}")
                pe.wait_ge(pool_w, 16)
                pe.wait_ge(g_.sem, g_.at(f"d{h}"))
                pe.wait_ge(v.sem, v.at(f"h{h}"))
                for e in range(2):
                    for k in range(2):
                        ins = mm(ps[:, 4 + e, 0:T], pw[:, h, k, e * P:(e + 1) * P], o_pool[:, 2 * h + k, :],
                                 start=(k == 0), stop=(k == 1))
                q.done(ins, f"pool{h}")
                pe.wait_ge(a.sem, a.at(f"pool{h}"))
            for h in H:
                pe.wait_ge(a.sem, a.at(f"sq{h}"))
                if h == 0:
                    pe.wait_ge(v.sem, v.at(f"c{MLH - 1}3"))
                for e in range(2):
                    ins = mm(ps[:, h, 0:T], K("ones_dv"), sq[:, e, :], start=(e == 0), stop=(e == 1))
                q.done(ins, f"q{h}")

        @block.scalar
        def _(act):
            fn = nc.scalar.activation
            a.done(fn(mlu[:, 16:24, :], mlu[:, 16:24, :], ACT.Sigmoid), "sig")
            act.wait_ge(v.sem, v.at("fx"))
            a.done(fn(ln, fx, ACT.Abs), "abs")
            act.wait_ge(a.sem, a.at("abs"))
            a.done(fn(ln, ln, ACT.Exp, scale=-1.0), "exp")
            act.wait_ge(a.sem, a.at("exp"))
            a.done(fn(ln, ln, ACT.Ln, bias=1.0), "ln")
            for c in range(3):
                n = P if c < 2 else NSM
                for e in range(2):
                    act.wait_ge(q.sem, q.at(f"vt{c}{e}"))
                    a.done(fn(vt[0:n, c, e * 512:(e + 1) * 512], ps[0:n, 1 + 2 * c + e, :], ACT.Copy), f"vt{c}{e}")
            act.wait_ge(v.sem, v.at("m"))
            a.done(fn(emt, m, ACT.Exp, scale=-1.0), "emt")
            act.wait_ge(v.sem, v.at("wd"))
            a.done(fn(wprev[:, NPR:T], wprev[:, NPR:T], ACT.Exp), "wprev")
            act.wait_ge(v.sem, v.at("wl"))
            a.done(fn(ws, ws, ACT.Exp), "ws")
            act.wait_ge(q.sem, q.at("gt"))
            fn(gt[:, 0:16], ps[:, 7, 0:16], ACT.Copy)
            a.done(fn(gt[0:NSM, 16:24], ps[0:NSM, 7, 16:24], ACT.Copy), "gt")
            for h in H:
                act.wait_ge(q.sem, q.at(f"b{h}"))
                if h:
                    act.wait_ge(v.sem, v.at(f"c{h - 1}3"))
                a.done(fn(wp, ps[:, 3, T:T + NSM], ACT.Copy), f"wp{h}")
                act.wait_ge(v.sem, v.at(f"x{h}"))
                fn(expo[:, 0:384], expo[:, 0:384], ACT.Exp, scale=-1.0)
                a.done(fn(expo[0:NSM, 384:416], expo[0:NSM, 384:416], ACT.Exp, scale=-1.0), f"e{h}")
                act.wait_ge(q.sem, q.at(f"n{h}"))
                a.done(fn(dn, ps[:, 2, 0:T], ACT.Abs), f"abs{h}")
                act.wait_ge(q.sem, q.at(f"u{h}"))
                if h >= 2:
                    act.wait_ge(cp_out[h % 2], 16)
                a.done(fn(cp[h % 2], ps[:, 7, 0:DV], ACT.Copy), f"cp{h}")
                act.wait_ge(q.sem, q.at(f"pool{h}"))
                for e in range(2):
                    ins = fn(o_pool[:, 2 * h + e, :], ps[:, 4 + e, 0:T], ACT.Copy, scale=par("pool_scale", 2 * h + e))
                a.done(ins, f"pool{h}")
            for h in H:
                if h:
                    act.wait_ge(q.sem, q.at(f"q{h - 1}"))
                act.wait_ge(v.sem, v.at(f"h{h}"))
                a.done(fn(sq, o_ml[:, 2 * h:2 * h + 2, :], ACT.Square), f"sq{h}")
            act.wait_ge(v.sem, v.at("v3"))
            a.done(fn(mrg[:, 0:4, :], mrg[:, 0:4, :], ACT.Sqrt), "root")

        @block.vector
        def _(dve):
            ts, tt, stt = nc.vector.tensor_scalar, nc.vector.tensor_tensor, nc.vector.scalar_tensor_tensor
            dve.wait_ge(loaded, 16)
            dve.wait_ge(q.sem, q.at("fg"))
            v.done(ts(fx, ps[0:4, 0, 0:T], b_f, None, ALU.add), "fx")
            v.done(ts(ig, gif[0:4, :], b_i, None, ALU.add), "ig")
            dve.wait_ge(v.sem, v.at("fx"))
            v.done(ts(lf, fx, 0.0, None, ALU.min), "mn")
            dve.wait_ge(v.sem, v.at("mn"))
            dve.wait_ge(a.sem, a.at("ln"))
            v.done(tt(lf, lf, ln, ALU.subtract), "lf")
            dve.wait_ge(v.sem, v.at("lf"))
            v.done(nc.vector.tensor_tensor_scan(bcum, K("run_ml", 4), lf, 0.0, ALU.mult, ALU.add), "bcum")
            dve.wait_ge(v.sem, v.at("bcum"))
            v.done(tt(g, ig, bcum, ALU.subtract), "g")
            dve.wait_ge(v.sem, v.at("g"))
            nc.vector.tensor_copy(M[:, 1:T], g[:, 1:T])
            ts(M[:, 0:1], g[:, 0:1], 0.0, None, ALU.max)
            v.done(tt(emt[:, 0:NB], seq(g)[:, :, 0], m_prev, ALU.max), "gmax")
            dve.wait_ge(v.sem, v.at("gmax"))
            v.done(nc.vector.tensor_copy(seq(M)[:, :, 0], emt[:, 0:NB]), "M")
            raise_ = v.at("M")
            dve.wait_ge(v.sem, raise_)
            nc.vector.tensor_tensor_scan(M, K("restart", 4), M, 0.0, ALU.add, ALU.max).then_inc(scanned, 1)
            dve.wait_ge(scanned, 1)
            v.done(tt(m, bcum, M, ALU.add), "m")
            v.done(tt(seq(wprev), m_prev.unsqueeze(2).to_broadcast([4, NB, NL]), seq(M), ALU.subtract), "wd")
            ts(ws[:, 0:NPR], g[:, 0:NPR], M[:, NPR - 1:NPR], None, ALU.subtract)
            v.done(tt(seq(ws), seq(g), seq(M)[:, :, NL - 1:NL].to_broadcast([4, NB, NL]), ALU.subtract), "wl")
            v.done(nc.vector.tensor_copy(sout[:, :, :], rwx[:, :, NPR:XW:5]), "sout")
            dve.wait_ge(a.sem, a.at("gt"))
            for h in H:
                dve.wait_ge(q.sem, q.at(f"b{h}"))
                gp = lambda c, n=P: gt[0:n, 8 * c + h:8 * c + h + 1]
                wsp = lambda c, n=P: gt[0:n, 8 * c + 4 + h:8 * c + 5 + h]
                ts(expo[:, 0:NPR], ps[:, 1, 0:NPR], gp(0), 0.0, ALU.subtract, ALU.max)
                ts(expo[:, NPR:384], ps[:, 1, P:NPR], gp(1), 0.0, ALU.subtract, ALU.max)
                v.done(ts(expo[0:NSM, 384:416], ps[0:NSM, 1, NPR:T], gp(2, NSM), 0.0, ALU.subtract, ALU.max), f"x{h}")
                dve.wait_ge(a.sem, a.at(f"wp{h}"))
                v.done(tt(qw, mlu[:, h, NPR:T], wp, ALU.mult), f"qw{h}")
                dve.wait_ge(v.sem, v.at(f"qw{h}"))
                v.done(tt(qn.rearrange("p (b l) -> p b l", l=NL), qw.rearrange("p (b l) -> p b l", l=NL),
                          n_in[:, h, :].unsqueeze(2).to_broadcast([P, NB, NL]), ALU.mult), f"qn{h}")
                dve.wait_ge(a.sem, a.at(f"e{h}"))
                dve.wait_ge(q.sem, q.at(f"s{h}"))
                tt(wts[:, 0:384], ps[:, 0, 0:384], expo[:, 0:384], ALU.mult)
                v.done(tt(wts[0:NSM, 384:416], ps[0:NSM, 0, 384:416], expo[0:NSM, 384:416], ALU.mult), f"w{h}")
                dve.wait_ge(v.sem, v.at(f"w{h}"))
                for c in range(2):
                    tt(wts[:, c * NPR:c * NPR + P], wts[:, c * NPR:c * NPR + P], K("lt_le")[:, P:2 * P], ALU.mult)
                v.done(tt(wts[0:NSM, 384:416], wts[0:NSM, 384:416], K("seq_lt_le", NSM)[:, NSM:2 * NSM], ALU.mult), f"wm{h}")
                dve.wait_ge(q.sem, q.at(f"k{h}"))
                if h:
                    dve.wait_ge(q.sem, q.at(f"d{h - 1}3"))
                ts(kt[:, 0, :], ps[:, 6, 0:P], wsp(0), None, ALU.mult)
                ts(kt[:, 1, :], ps[:, 6, P:2 * P], wsp(1), None, ALU.mult)
                v.done(ts(kt[0:NSM, 2, :], ps[0:NSM, 6, 2 * P:3 * P], wsp(2, NSM), None, ALU.mult), f"k{h}")
                dve.wait_ge(a.sem, a.at(f"abs{h}"))
                v.done(tt(dn, dn, ps[:, 3, 0:T], ALU.max), f"max{h}")
                dve.wait_ge(v.sem, v.at(f"max{h}"))
                v.done(nc.vector.reciprocal(dn, dn), f"rec{h}")
                dve.wait_ge(v.sem, v.at(f"rec{h}"))
                tt(o_ml[:, 2 * h, :], ps[:, 4, 0:T], dn, ALU.mult)
                v.done(tt(o_ml[:, 2 * h + 1, :], ps[:, 5, 0:T], dn, ALU.mult), f"h{h}")
                dve.wait_ge(a.sem, a.at(f"cp{h}"))
                nc.vector.tensor_copy(nout[:, h, 0:1], ps[:, 7, DV:DV + 1])
                tt(nout[:, h, 1:9], n_in[:, h, :], wp.rearrange("p (b l) -> p b l", l=NL)[:, :, NL - 1], ALU.mult).then_inc(scanned, 1)
                dve.wait_ge(scanned, 2 + h)
                v.done(tt(nout[:, h, 1:9], nout[:, h, 1:9], ps[:, 7, DV + 1:DV + 1 + NB], ALU.add), f"n{h}")
                for j in range(4):
                    dve.wait_ge(q.sem, q.at(f"d{h}{j}"))
                    for i in range(2):
                        b = 2 * j + i
                        ins = stt(out=cst[:, h % 2, b, :], in0=cst[:, h % 2, b, :], scalar=wp[:, NL * b + NL - 1:NL * b + NL],
                                  in1=ps[:, 7 if j % 2 == 0 else 1, i * DV:(i + 1) * DV], op0=ALU.mult, op1=ALU.add)
                    v.done(ins, f"c{h}{j}")
            for h in H:
                dve.wait_ge(q.sem, q.at(f"q{h}"))
                v.done(ts(mrg[:, h, :], ps[:, h, 0:T], RMS_EPS, None, ALU.add), f"v{h}")
            dve.wait_ge(a.sem, a.at("root"))
            v.done(nc.vector.reciprocal(mrg[:, 0:4, :], mrg[:, 0:4, :]), "rs")
            dve.wait_ge(v.sem, v.at("rs"))
            for k in range(KH):
                v.done(stt(out=o_ml[:, k, :], in0=o_ml[:, k, :], scalar=par("ml_gn", k), in1=mrg[:, k // 2, :],
                           op0=ALU.mult, op1=ALU.mult), f"y{k}")
            for k in range(KH):
                dve.wait_ge(v.sem, v.at(f"y{k}"))
                v.done(tt(o_ml[:, k, :], o_ml[:, k, :], mlu[:, 16 + k, :], ALU.mult), f"o{k}")

        @block.gpsimd
        def _(pool):
            tt, ts = nc.gpsimd.tensor_tensor, nc.gpsimd.tensor_scalar
            for h in H:
                src, n = poolx[:, 2 * h:2 * h + 2, :], PW
                for i in range(h + 1):
                    o, s = win[i % 2], 1 << i
                    if i:
                        pool.wait_ge(g_.sem, g_.at(f"add{h}{i - 1}"))
                    elif h:
                        pool.wait_ge(g_.sem, g_.at(f"d{h - 1}"))
                    lo = (2 << i) - 1
                    g_.done(tt(o[:, :, lo:PW], src[:, :, lo:PW], src[:, :, lo - s:PW - s], ALU.add), f"add{h}{i}")
                    src = o
                pool.wait_ge(g_.sem, g_.at(f"add{h}{h}"))
                w = WINDOWS[h]
                d = o_pool[:, 2 * h:2 * h + 2, :]
                ts(d[:, :, 0:NPR], src[:, :, BUF:PS0], 1.0 / w, None, ALU.mult)
                for k in range(2):
                    ins = ts(d[:, k, NPR:T].rearrange("p (b l) -> p b l", b=NB),
                             src[:, k, PS0:PW].rearrange("p (b r) -> p b r", b=NB)[:, :, BUF:BUF + NL], 1.0 / w, None, ALU.mult)
                g_.done(ins, f"mean{h}")
                pool.wait_ge(g_.sem, g_.at(f"mean{h}"))
                inv = K("inv_count")[:, 16 * h:16 * h + 16]
                g_.done(tt(d[:, :, 0:16], src[:, :, BUF:BUF + 16], inv.unsqueeze(1).to_broadcast([P, 2, 16]), ALU.mult), f"first{h}")
                pool.wait_ge(g_.sem, g_.at(f"first{h}"))
                x = poolx[:, 2 * h:2 * h + 2, :]
                tt(d[:, :, 0:NPR], d[:, :, 0:NPR], x[:, :, BUF:PS0], ALU.subtract)
                for k in range(2):
                    dd = d[:, k, NPR:T].rearrange("p (b l) -> p b l", b=NB)
                    ins = tt(dd, dd, x[:, k, PS0:PW].rearrange("p (b r) -> p b r", b=NB)[:, :, BUF:BUF + NL], ALU.subtract)
                g_.done(ins, f"d{h}")
                if h == 0:
                    for k in range(KH):
                        nc.gpsimd.tensor_copy(pout[:, k, 0, :], poolx[:, k, PS0 - BUF:PS0])
                        ins = nc.gpsimd.tensor_copy(pout[:, k, 1:9, :], poolx[:, k, PS0:PW].rearrange(
                            "p (b r) -> p b r", b=NB)[:, :, NL:NL + BUF])
                    g_.done(ins, "pout")
                pool.wait_ge(a.sem, a.at("vt21"))
                if h:
                    pool.wait_ge(q.sem, q.at(f"d{h - 1}3"))
                g_.done(tt(vx, vt[0:NSM, 2, h * DV:(h + 1) * DV].unsqueeze(1).to_broadcast([NSM, NB, DV]),
                           K("of_seq", NSM).unsqueeze(2).to_broadcast([NSM, NB, DV]), ALU.mult), f"vx{h}")


def stage_rwkv(nc, ctx0, A, O, env):
    ring, xn, mrg, ps, const, param, K, par, rwx, o_ml, o_pool = (
        env[k] for k in "ring xn mrg ps const param K par rwx o_ml o_pool".split())
    with ExitStack() as ctx:
        sem = lambda n: ctx.enter_context(nc.semaphore(n))
        sb = lambda n, s: ctx.enter_context(nc.sbuf_tensor(n, s, F32))
        H = range(2)
        f = sb("f", [P, 11, T])
        r, k, v_, kk, sg, csm, a_, er, ek, ekap, rkk = (f[:, j, :] for j in range(11))
        kr, kb = sb("kr", [P, 2, T]), sb("kb", [P, 2, T])
        dx = sb("dx", [P, XW])
        lora = sb("lora", [P, T])
        wa = sb("wa", [P, P])
        tok = sb("tok", [P, 3, 3 * P])
        xm = sb("xm", [P, 2, 4, P])
        rhs = sb("rhs", [P, 3, P])
        nsa = sb("nsa", [P, 3, P])
        sk = sb("sk", [NSM, 2, 2, 2, NSM])
        su, st_, sz = (sb(n, [NSM, 2, NSM]) for n in ("su", "st_", "sz"))
        sxm = sb("sxm", [NSM, 2, 2, NSM])
        sts = sb("sts", [P, NB, 64])
        vx, nx = sb("vx", [NSM, NB, P]), sb("nx", [NSM, NB, P])
        s0t = sb("s0t", [64, 2, 64])
        cen, ec, st0, st1 = sb("cen", [P, 2]), sb("ec", [P, 2]), sb("st0", [P, 64]), sb("st1", [P, 64])
        gtmp = sb("gtmp", [P, T])
        half = sb("half", [P, 2 * KH])
        kkm = ring[:, 3, 0:1024].rearrange("p (h c x t) -> p h c x t", h=2, c=2, x=2)
        bbm = ring[:, 3, 1024:2048].rearrange("p (h c x t) -> p h c x t", h=2, c=2, x=2)
        um = ring[:, 3, 2048:2560].rearrange("p (j t) -> p j t", j=4)
        tm = ring[:, 3, 2560:3072].rearrange("p (j t) -> p j t", j=4)
        zm = ring[:, 3, 3072:3584].rearrange("p (j t) -> p j t", j=4)
        gate = ring[:, 3, 3584:3584 + T]
        wtmp = zm.rearrange("p j t -> p (j t)")[0:64, :]
        seq = lambda x: x[:, NPR:T].rearrange("p (b l) -> p b l", l=NL)

        mixed = sem("w_mixed")
        slots = [sem(f"w_slot{s}") for s in range(3)]
        wa_in, st_in, st_out, stp_out = sem("w_wa"), sem("w_stin"), sem("w_stout"), sem("w_stp")
        LV = range(len(LEVELS))
        pe_steps = ["z", "a", "G00", "ss", "U00", "G01", "U01", "tr0", "tr1", "tr2"]
        pe_steps += [f"bk{x}{h}" for x in H for h in H] + ["sk0", "sk1", "w0", "w1"]
        fill_after = {1: "G10", 2: "U10", 4: "G11", 5: "U11"}
        for l in LV:
            pe_steps += [f"z{l}"] + ([] if l == 0 else [f"t{l}", f"u{l}"] if l < 6 else [f"u{l}"])
            if l in fill_after:
                pe_steps += [fill_after[l]]
            if l < 2:
                pe_steps += [f"sz{l}"] + ([f"su{l}"] if l else [])
        pe_steps += ["g0", "gs", "sa0", "sas", "y0", "ys", "s0", "g1", "sa1", "y1", "s1", "ds", "mean", "bonus", "var"]
        q = Steps(ctx, nc, "w_pe", pe_steps)
        dve_steps = ["dx_k", "us_k", "kkr", "dx_r", "us_r", "dx_v", "us_v", "sg", "a", "cs", "cen", "csc", "csm", "ssm",
                     "rec", "kk", "m00", "kap", "rt", "b", "bt", "ka", "kp", "kt", "rkk", "m01"]
        dve_steps += [f"bk{x}{h}" for x in H for h in H] + ["sk0", "sk1", "wm0", "w0", "wm1", "w1"]
        for l in LV:
            dve_steps += ([f"u{l}", f"t{l}"] if l == 0 else [f"t{l}", f"u{l}"] if l < 6 else [f"u{l}"])
            if l < 2:
                dve_steps += ["su0", "st0"] if l == 0 else ["su1"]
            if l == 3:
                dve_steps += ["m10"]
        dve_steps += ["m11", "s0", "s1a", "s1", "ds", "dsp", "ysum", "d", "ve", "grec", "y", "bon", "o"]
        v = Steps(ctx, nc, "w_dve", dve_steps)
        act_steps = ["tz", "ta", "kksq", "root", "G00", "ek", "er", "ekap", "ec", "G01", "tr0", "tr1", "tr2"]
        for l in LV:
            act_steps += ([f"z{l}"] if l else []) + (["sz1"] if l == 1 else [])
            if l in (1, 4):
                act_steps += [fill_after[l]]
        act_steps += ["g0", "gs", "sa0", "sas", "g1", "sa1", "ys", "sq", "groot"]
        a = Steps(ctx, nc, "w_act", act_steps)
        pool_steps = []
        for l in LV:
            pool_steps += [f"x{l}"] + ([f"sx{l}"] if l < 2 else []) + (["vx"] if l == 2 else []) + (["m0"] if l == 3 else [])
        g_ = Steps(ctx, nc, "w_pool", pool_steps + ["nx", "m1"])
        for s_ in (q, v, a, g_):
            s_.lap = 1
        dxd = sem("w_dx")
        carrier = sem("w_carrier")
        block = ctx.enter_context(nc.Block())
        N = KH

        def settled(eng):
            eng.sem_inc(carrier, 1)

        def tile(t, i):
            return t[bass.ds(i, 1), :, :].rearrange("o p n -> (o p) n")

        @block.sync
        def _(sp):
            def load_weights(i, j):
                if j is not None:
                    sp.wait_ge(q.sem, q.at("G11", j))
                    settled(sp)
                for b in H:
                    sp.dma_start(ring[:, b, :], tile(A["w_gate"][b + 1], i)).then_inc(slots[b], 16)
                if j is not None:
                    sp.wait_ge(q.sem, q.at("U11", j))
                    settled(sp)
                sp.dma_start(ring[:, 2, :], tile(A["w_up2"], i)).then_inc(slots[2], 16)

            def load_small(i):
                settled(sp)
                sp.dma_start(wa[:, :], tile(A["w_lora"], i)).then_inc(wa_in, 16)
                sp.dma_start(sts[:, :, :], A["rw_s"][bass.ds(i, 1), :, :, :].rearrange("o p b v -> (o p) b v")).then_inc(st_in, 16)

            def store(i):
                sp.wait_ge(v.sem, v.at("s1", i))
                settled(sp)
                sp.dma_start(tile(O["rw_p"], i), st1[:, :]).then_inc(stp_out, 16)
                sp.wait_ge(v.sem, v.at("dsp", i))
                settled(sp)
                sp.dma_start(O["rw_s"][bass.ds(i, 1), :, :, :].rearrange("o p b v -> (o p) b v"), sts[:, :, :]).then_inc(st_out, 16)
                sp.wait_ge(st_out, i * 16 + 16)
                sp.wait_ge(stp_out, i * 16 + 16)
            load_small(0)
            load_weights(0, None)
            with sp.Fori(0, N - 1) as i:
                load_weights(i + 1, i)
                store(i)
                load_small(i + 1)
            store(N - 1)

        @block.tensor
        def _(pe):
            mm, ident = nc.tensor.matmul, K("ident")
            pe.sem_inc(q.sem, q.n)
            w = [ring[:, s, :].rearrange("p (k n) -> p k n", k=KD) for s in range(3)]
            with pe.Fori(0, N) as i:
                def filler(name, lo, hi):
                    kind, d, b = name[0], int(name[1]), int(name[2])
                    n = KD if kind == "G" else KH
                    bank = 0 if kind == "G" else (1, 7)[b]
                    if lo == 0:
                        if kind == "G":
                            pe.wait_ge(slots[b], i * 16 + 16)
                            last = {"G00": ("G11", i - 1), "G01": ("G00", i), "G10": ("G01", i), "G11": ("G10", i)}[name]
                            pe.wait_ge(a.sem, a.at(*last))
                        else:
                            if d == 0 and b == 0:
                                pe.wait_ge(slots[2], i * 16 + 16)
                            pe.wait_ge(v.sem, v.at(f"m1{b}", i - 1) if d == 0 else v.at(f"m0{b}", i))
                    for t in range(lo, hi):
                        if kind == "G":
                            ins = mm(ps[:, 0, 0:T], w[b][:, t, d * P:(d + 1) * P], xn[:, t, :], start=(t == 0), stop=(t == n - 1))
                        else:
                            src = (o_ml, o_pool)[b]
                            ins = mm(ps[:, bank, 0:T], w[2][:, b * KH + t, d * P:(d + 1) * P], src[:, t, :],
                                     start=(t == 0), stop=(t == n - 1))
                    if hi == n:
                        q.done(ins, name)
                hs = lambda h: slice(64 * h, 64 * h + 64)
                pe.wait_ge(mixed, 2)
                pe.wait_ge(wa_in, i * 16 + 16)
                pe.wait_ge(v.sem, v.at("o", i - 1))
                q.done(mm(ps[:, 2, 0:T], wa[0:64, :], lora[0:64, :], start=True, stop=True), "z")
                q.done(mm(ps[:, 3, 0:T], wa[64:128, :], lora[64:128, :], start=True, stop=True), "a")
                filler("G00", 0, 16)
                pe.wait_ge(a.sem, a.at("kksq", i))
                q.done(mm(ps[:, 4, 0:T], K("heads"), ekap, start=True, stop=True), "ss")
                filler("U00", 0, 8)
                filler("G01", 0, 16)
                filler("U01", 0, 8)
                pe.wait_ge(v.sem, v.at("kt", i))
                for c in range(3):
                    n = P if c < 2 else NSM
                    for j, src in enumerate((v_, kb[:, 0, :], kb[:, 1, :])):
                        ins = nc.tensor.transpose(ps[0:n, (5, 6, 2)[c], j * P:(j + 1) * P], src[:, c * P:c * P + n], ident)
                    q.done(ins, f"tr{c}")
                for x in H:
                    for h in H:
                        b = 3 + 2 * x + h
                        if b == 5:
                            pe.wait_ge(a.sem, a.at("tr1", i))
                        for c in H:
                            ins = mm(ps[:, b, c * 256:(c + 1) * 256], kb[hs(h), x, c * P:(c + 1) * P],
                                     kr[hs(h), :, c * P:(c + 1) * P], start=True, stop=True)
                        q.done(ins, f"bk{x}{h}")
                for h in H:
                    if h == 0:
                        pe.wait_ge(a.sem, a.at("tr2", i))
                    else:
                        pe.wait_ge(v.sem, v.at("bk00", i))
                    settled(pe)
                    for x in H:
                        ins = mm(ps[0:NSM, 2 + h, x * 64:x * 64 + 64], kb[hs(h), x, NPR:T], kr[hs(h), :, NPR:T],
                                 start=True, stop=True)
                    q.done(ins, f"sk{h}")
                pe.wait_ge(st_in, i * 16 + 16)
                for h in H:
                    pe.wait_ge(v.sem, v.at(("bk01", "bk10")[h], i))
                    settled(pe)
                    for y in H:
                        ins = mm(ps[NSM * y:NSM * y + NSM, 4 + h, :], kr[hs(h), y, NPR:T], sts[hs(h), :, :], start=True, stop=True)
                    q.done(ins, f"w{h}")
                for l in LV:
                    pe.wait_ge(g_.sem, g_.at(f"x{l}", i))
                    pe.wait_ge(v.sem, v.at("bk11" if l == 0 else f"t{l - 1}", i))
                    if l:
                        pe.wait_ge(a.sem, a.at(f"z{l - 1}", i)) if l > 1 else None
                    for j in range(4):
                        ins = mm(ps[:, 6, j * P:(j + 1) * P], xm[:, l % 2, j, :], ident if l == 0 else tm[:, j, :],
                                 start=True, stop=True)
                    q.done(ins, f"z{l}")
                    if l == 0:
                        pe.wait_ge(v.sem, v.at("w0", i))
                        pe.wait_ge(g_.sem, g_.at("sx0", i))
                        settled(pe)
                        for h in H:
                            ins = mm(ps[0:NSM, 4, h * NSM:(h + 1) * NSM], sxm[:, 0, h, :], K("ident", NSM)[:, 0:NSM], start=True, stop=True)
                        q.done(ins, "sz0")
                        continue
                    name = fill_after.get(l)
                    full = 16 if name and name[0] == "G" else 8
                    if name:
                        filler(name, 0, full // 2)
                    pe.wait_ge(a.sem, a.at(f"z{l}", i))
                    pe.wait_ge(v.sem, v.at(f"u{l - 1}", i))
                    if l == 1:
                        pe.wait_ge(v.sem, v.at("sk1", i))
                    if l < 6:
                        for j in range(4):
                            ins = mm(ps[:, 2, j * P:(j + 1) * P], um[:, j, :], zm[:, j, :], start=True, stop=True)
                        q.done(ins, f"t{l}")
                    for j in range(4):
                        ins = mm(ps[:, 3, j * P:(j + 1) * P], zm[:, j, :], um[:, j, :], start=True, stop=True)
                    q.done(ins, f"u{l}")
                    if name:
                        filler(name, full // 2, full)
                    if l == 1:
                        pe.wait_ge(g_.sem, g_.at("sx1", i))
                        pe.wait_ge(v.sem, v.at("st0", i))
                        settled(pe)
                        for h in H:
                            ins = mm(ps[0:NSM, 4, h * NSM:(h + 1) * NSM], sxm[:, 1, h, :], st_[:, h, :], start=True, stop=True)
                        q.done(ins, "sz1")
                        pe.wait_ge(a.sem, a.at("sz1", i))
                        pe.wait_ge(v.sem, v.at("w1", i))
                        settled(pe)
                        for h in H:
                            ins = mm(ps[0:NSM, 5, h * NSM:(h + 1) * NSM], sz[:, h, :], su[:, h, :], start=True, stop=True)
                        q.done(ins, "su1")
                vt = lambda c, h, n=P: tok[0:n, c, 64 * h:64 * h + 64]

                pe.wait_ge(v.sem, v.at("su1", i))
                for h in H:
                    ins = mm(ps[:, 4, 64 * h:64 * h + 64], kkm[:, h, 0, 0, :], vt(0, h), start=True, stop=True)
                q.done(ins, "g0")
                for h in H:
                    o = ps[0:NSM, 4, P + 64 * h:P + 64 * h + 64]
                    mm(o, sk[:, h, 0, 0, :], vt(2, h, NSM), start=True, stop=False)
                    ins = mm(o, K("ident", NSM)[:, 0:NSM], s0t[0:NSM, h, :], start=False, stop=True)
                q.done(ins, "gs")
                pe.wait_ge(a.sem, a.at("gs", i))
                pe.wait_ge(v.sem, v.at("u6", i))
                for h in H:
                    ins = mm(ps[:, 5, 64 * h:64 * h + 64], um[:, 2 * h, :], rhs[:, 0, hs(h)], start=True, stop=True)
                q.done(ins, "sa0")
                for h in H:
                    ins = mm(ps[0:NSM, 5, P + 64 * h:P + 64 * h + 64], su[:, h, :], rhs[0:NSM, 2, hs(h)], start=True, stop=True)
                q.done(ins, "sas")
                pe.wait_ge(a.sem, a.at("sas", i))
                for h in H:
                    o = ps[hs(h), 6, 0:P]
                    mm(o, vt(0, h), kkm[:, h, 0, 1, :], start=True, stop=False)
                    ins = mm(o, nsa[:, 0, hs(h)], bbm[:, h, 0, 1, :], start=False, stop=True)
                q.done(ins, "y0")
                for h in H:
                    o = ps[hs(h), 6, NPR:T]
                    mm(o, vt(2, h, NSM), sk[:, h, 0, 1, :], start=True, stop=False)
                    mm(o, nsa[0:NSM, 2, hs(h)], sk[:, h, 1, 1, :], start=False, stop=True)
                for h in H:
                    o = ps[hs(h), 3, NPR:T]
                    ins = mm(o, s0t[NSM:64, h, :], const[NSM:64, CONST_AT["ident"][0] + NSM:CONST_AT["ident"][0] + 64],
                             start=True, stop=True)
                q.done(ins, "ys")
                for h in H:
                    o = ps[hs(h), 2, 0:64]
                    mm(o, tok[:, 0, P + 64 * h:P + 64 * h + 64], vt(0, h), start=True, stop=False)
                    ins = mm(o, tok[:, 0, 2 * P + 64 * h:2 * P + 64 * h + 64], nsa[:, 0, hs(h)], start=False, stop=True)
                q.done(ins, "s0")
                pe.wait_ge(v.sem, v.at("s0", i))
                for h in H:
                    o = ps[:, 4 + h, 0:64]
                    mm(o, kkm[:, h, 1, 0, :], vt(1, h), start=True, stop=False)
                    ins = mm(o, kr[hs(h), 0, P:NPR], st0[hs(h), :], start=False, stop=True)
                q.done(ins, "g1")
                pe.wait_ge(a.sem, a.at("g1", i))
                for h in H:
                    ins = mm(ps[:, 4, P + 64 * h:P + 64 * h + 64], um[:, 2 * h + 1, :], rhs[:, 1, hs(h)], start=True, stop=True)
                q.done(ins, "sa1")
                pe.wait_ge(a.sem, a.at("sa1", i))
                for h in H:
                    o = ps[hs(h), 6, P:NPR]
                    mm(o, vt(1, h), kkm[:, h, 1, 1, :], start=True, stop=False)
                    mm(o, nsa[:, 1, hs(h)], bbm[:, h, 1, 1, :], start=False, stop=False)
                    ins = mm(o, st0[hs(h), :], kr[hs(h), 1, P:NPR], start=False, stop=True)
                q.done(ins, "y1")
                for h in H:
                    o = ps[hs(h), 2, 0:64]
                    mm(o, tok[:, 1, P + 64 * h:P + 64 * h + 64], vt(1, h), start=True, stop=False)
                    ins = mm(o, tok[:, 1, 2 * P + 64 * h:2 * P + 64 * h + 64], nsa[:, 1, hs(h)], start=False, stop=True)
                q.done(ins, "s1")
                pe.wait_ge(g_.sem, g_.at("nx", i))
                for h in H:
                    o = ps[hs(h), 5, :]
                    mm(o, tok[0:NSM, 2, P + 64 * h:P + 64 * h + 64], vx[:, :, hs(h)], start=True, stop=False)
                    ins = mm(o, tok[0:NSM, 2, 2 * P + 64 * h:2 * P + 64 * h + 64], nx[:, :, hs(h)], start=False, stop=True)
                q.done(ins, "ds")
                pe.wait_ge(v.sem, v.at("ysum", i))
                q.done(mm(ps[:, 3, 0:T], K("heads_mean"), sg, start=True, stop=True), "mean")
                q.done(mm(ps[:, 4, 0:T], K("heads"), rkk, start=True, stop=True), "bonus")
                pe.wait_ge(v.sem, v.at("s1", i))
                pe.wait_ge(a.sem, a.at("sq", i))
                q.done(mm(ps[:, 2, 0:T], K("heads_mean"), csm, start=True, stop=True), "var")

        @block.scalar
        def _(act):
            fn = nc.scalar.activation
            act.sem_inc(a.sem, a.n)
            act.wait_ge(mixed, 1)
            fn(lora[0:64, :], lora[0:64, :], ACT.Tanh).then_inc(mixed, 1)
            with act.Fori(0, N) as i:
                act.wait_ge(q.sem, q.at("z", i))
                a.done(fn(sg, ps[:, 2, 0:T], ACT.Tanh, bias=half[:, bass.ds(i, 1)], scale=0.5), "tz")
                act.wait_ge(q.sem, q.at("a", i))
                a.done(fn(a_, ps[:, 3, 0:T], ACT.Tanh, bias=half[:, bass.ds(i + KH, 1)], scale=0.5), "ta")
                act.wait_ge(v.sem, v.at("kkr", i))
                a.done(fn(ekap, kk, ACT.Square), "kksq")
                act.wait_ge(v.sem, v.at("ssm", i))
                a.done(fn(ek, ek, ACT.Sqrt), "root")
                act.wait_ge(q.sem, q.at("G00", i))
                a.done(fn(gate, ps[:, 0, 0:T], ACT.Tanh, scale=0.5), "G00")
                act.wait_ge(v.sem, v.at("kk", i))
                a.done(fn(ek, er, ACT.Exp, scale=ALPHA), "ek")
                act.wait_ge(a.sem, a.at("ek", i))
                a.done(fn(er, er, ACT.Exp, scale=-ALPHA), "er")
                a.done(fn(ekap, csm, ACT.Exp, scale=-ALPHA), "ekap")
                a.done(fn(ec[:, :], cen[:, :], ACT.Exp, scale=-ALPHA), "ec")
                act.wait_ge(q.sem, q.at("G01", i))
                act.wait_ge(v.sem, v.at("m00", i))
                a.done(fn(gate, ps[:, 0, 0:T], ACT.Tanh, scale=0.5), "G01")
                for c in range(3):
                    n = P if c < 2 else NSM
                    act.wait_ge(q.sem, q.at(f"tr{c}", i))
                    a.done(fn(tok[0:n, c, :], ps[0:n, (5, 6, 2)[c], 0:3 * P], ACT.Copy), f"tr{c}")
                for l in range(1, 7):
                    act.wait_ge(q.sem, q.at(f"z{l}", i))
                    act.wait_ge(q.sem, q.at(f"u{l - 1}", i)) if l > 1 else act.wait_ge(v.sem, v.at("w1", i))
                    a.done(fn(zm, ps[:, 6, :].rearrange("p (j t) -> p j t", j=4), ACT.Copy), f"z{l}")
                    if l == 1:
                        act.wait_ge(q.sem, q.at("sz1", i))
                        a.done(fn(sz[:, :, :], ps[0:NSM, 4, 0:64].rearrange("p (h t) -> p h t", h=2), ACT.Copy), "sz1")
                    if l in (1, 4):
                        act.wait_ge(q.sem, q.at(fill_after[l], i))
                        act.wait_ge(v.sem, v.at(("m01", "m10")[l > 1], i))
                        a.done(fn(gate, ps[:, 0, 0:T], ACT.Tanh, scale=0.5), fill_after[l])
                act.wait_ge(q.sem, q.at("gs", i))
                a.done(fn(rhs[:, 0, :], ps[:, 4, 0:P], ACT.Copy), "g0")
                act.wait_ge(q.sem, q.at("gs", i))
                a.done(fn(rhs[0:NSM, 2, :], ps[0:NSM, 4, P:2 * P], ACT.Copy), "gs")
                act.wait_ge(q.sem, q.at("sas", i))
                a.done(fn(nsa[:, 0, :], ps[:, 5, 0:P], ACT.Copy, scale=-1.0), "sa0")
                act.wait_ge(q.sem, q.at("sas", i))
                a.done(fn(nsa[0:NSM, 2, :], ps[0:NSM, 5, P:2 * P], ACT.Copy, scale=-1.0), "sas")
                act.wait_ge(q.sem, q.at("g1", i))
                fn(rhs[:, 1, 0:64], ps[:, 4, 0:64], ACT.Copy)
                a.done(fn(rhs[:, 1, 64:128], ps[:, 5, 0:64], ACT.Copy), "g1")
                act.wait_ge(q.sem, q.at("sa1", i))
                a.done(fn(nsa[:, 1, :], ps[:, 4, P:2 * P], ACT.Copy, scale=-1.0), "sa1")
                act.wait_ge(q.sem, q.at("y1", i))
                act.wait_ge(v.sem, v.at("dsp", i))
                fn(er[:, NPR:T], ps[:, 3, NPR:T], ACT.Copy)
                a.done(fn(sg, ps[:, 6, 0:T], ACT.Copy), "ys")
                act.wait_ge(v.sem, v.at("d", i))
                a.done(fn(csm, ekap, ACT.Square), "sq")
                act.wait_ge(v.sem, v.at("ve", i))
                a.done(fn(ek, ek, ACT.Sqrt), "groot")

        @block.vector
        def _(dve):
            ts, tt, stt = nc.vector.tensor_scalar, nc.vector.tensor_tensor, nc.vector.scalar_tensor_tensor
            dve.sem_inc(v.sem, v.n)
            dxs = dx[:, NPR + 1:XW].rearrange("p (b l) -> p b l", b=NB)[:, :, 0:NL]
            now = lambda x: x[:, 1 + NPR:XW].rearrange("p (b l) -> p b l", b=NB)[:, :, 1:1 + NL]

            def mix(x, out, mu):
                stt(out=out[:, 0:NPR], in0=dx[:, 0:NPR], scalar=mu, in1=x[:, 1:1 + NPR], op0=ALU.mult, op1=ALU.add)
                return stt(out=seq(out), in0=dxs, scalar=mu, in1=now(x), op0=ALU.mult, op1=ALU.add)
            ts(half[:, 0:KH], param[:, PARAM_AT["w0"]:PARAM_AT["w0"] + KH], 0.5, None, ALU.mult)
            ts(half[:, KH:2 * KH], param[:, PARAM_AT["a0"]:PARAM_AT["a0"] + KH], 0.5, None, ALU.mult)
            tt(dx[:, 0:XW - 1], rwx[:, 24, 0:XW - 1], rwx[:, 24, 1:XW], ALU.subtract).then_inc(dxd, 1)
            dve.wait_ge(dxd, 1)
            mix(rwx[:, 24, :], lora, par("mu", 24)).then_inc(mixed, 1)
            dve.wait_ge(mixed, 1)
            with dve.Fori(0, N) as i:
                W = lambda s: dve.wait_ge(v.sem, v.at(s, i))
                WQ = lambda s: dve.wait_ge(q.sem, q.at(s, i))
                WA = lambda s: dve.wait_ge(a.sem, a.at(s, i))
                before = None
                for n, out, off in (("k", k, 8), ("r", r, 0), ("v", v_, 16)):
                    if before:
                        W(before)
                    before = f"us_{n}"
                    x = rwx[:, bass.ds(i + off, 1), :].rearrange("p o x -> p (o x)")
                    v.done(tt(dx[:, 0:XW - 1], x[:, 0:XW - 1], x[:, 1:XW], ALU.subtract), f"dx_{n}")
                    W(f"dx_{n}")
                    v.done(mix(x, out, par("mu", i + off)), f"us_{n}")
                    if n == "k":
                        W("us_k")
                        v.done(ts(kk, k, par("k_k", i), None, ALU.mult), "kkr")
                WA("tz")
                v.done(ts(sg, sg, 0.5, 0.5, ALU.mult, ALU.add), "sg")
                WA("ta")
                v.done(ts(a_, a_, 0.5, 0.5, ALU.mult, ALU.add), "a")
                W("sg")
                v.done(nc.vector.tensor_tensor_scan(er, K("run_rw"), sg, 0.0, ALU.mult, ALU.add), "cs")
                W("cs")
                v.done(nc.vector.tensor_copy(cen[:, :], er[:, 63:NPR:P]), "cen")
                W("cen")
                for c in H:
                    ins = ts(er[:, c * P:(c + 1) * P], er[:, c * P:(c + 1) * P], cen[:, c:c + 1], None, ALU.subtract)
                v.done(ins, "csc")
                W("csc")
                v.done(tt(csm, er, sg, ALU.subtract), "csm")
                WQ("ss")
                v.done(ts(ek, ps[:, 4, 0:T], 1e-24, None, ALU.max), "ssm")
                WA("root")
                v.done(nc.vector.reciprocal(ek, ek), "rec")
                W("rec")
                v.done(tt(kk, kk, ek, ALU.mult), "kk")
                i2 = i * 2

                def merge(d, b):
                    WQ(f"U{d}{b}")
                    WA(f"G{d}{b}")
                    if b == 1:
                        dve.wait_ge(g_.sem, g_.at("m0", i) if d else g_.at("m1", i - 1))
                    o = gtmp[:, :] if b else mrg[:, bass.ds(i2 + d, 1), :].rearrange("p o t -> p (o t)")
                    v.done(stt(out=o, in0=gate, scalar=1.0, in1=ps[:, (1, 7)[b], 0:T], op0=ALU.add, op1=ALU.mult), f"m{d}{b}")
                merge(0, 0)
                WA("ec")
                W("kk")
                v.done(tt(kr[:, 0, :], kk, ekap, ALU.mult), "kap")
                v.done(tt(kr[:, 1, :], r, er, ALU.mult), "rt")
                v.done(tt(rkk, kk, a_, ALU.mult), "b")
                W("b")
                v.done(tt(kb[:, 1, :], rkk, ek, ALU.mult), "bt")
                v.done(ts(a_, a_, 1.0, par("k_a", i), ALU.subtract, ALU.mult), "ka")
                W("ka")
                v.done(stt(out=k, in0=a_, scalar=1.0, in1=k, op0=ALU.add, op1=ALU.mult), "kp")
                W("kp")
                v.done(tt(kb[:, 0, :], k, ek, ALU.mult), "kt")
                v.done(stt(out=rkk, in0=r, scalar=par("r_k", i), in1=k, op0=ALU.mult, op1=ALU.mult), "rkk")
                merge(0, 1)
                for x in H:
                    for h in H:
                        WQ(f"bk{x}{h}")
                        out = (kkm, bbm)[x][:, h, :, :, :].rearrange("p c x t -> p c (x t)")
                        v.done(tt(out, ps[:, 3 + 2 * x + h, :].rearrange("p (c n) -> p c n", c=2),
                                  K("lt_le").unsqueeze(1).to_broadcast([P, 2, 256]), ALU.mult), f"bk{x}{h}")
                for h in H:
                    WQ(f"sk{h}")
                    v.done(tt(sk[:, h, :, :, :].rearrange("p x y t -> p x (y t)"),
                              ps[0:NSM, 2 + h, 0:128].rearrange("p (x n) -> p x n", x=2),
                              K("seq_lt_le", NSM).unsqueeze(1).to_broadcast([NSM, 2, 64]), ALU.mult), f"sk{h}")
                for h in H:
                    WQ(f"w{h}")
                    if h:
                        W("w0")
                    v.done(tt(wtmp.rearrange("p (b n) -> p b n", b=NB), ps[0:64, 4 + h, :].rearrange("p (b n) -> p b n", b=NB),
                              K("of_seq", 64).unsqueeze(2).to_broadcast([64, NB, 64]), ALU.mult), f"wm{h}")
                    W(f"wm{h}")
                    v.done(nc.vector.tensor_reduce(s0t[:, h, :], wtmp.rearrange("p (b n) -> p n b", b=NB), AX.X, ALU.add), f"w{h}")
                j4 = lambda x: x.rearrange("p (j t) -> p j t", j=4)
                h2 = lambda x: x.rearrange("p (h t) -> p h t", h=2)
                for l in LV:
                    if l == 0:
                        one4 = K("ident").unsqueeze(1).to_broadcast([P, 4, P])
                        one2 = K("ident", NSM)[:, 0:NSM].unsqueeze(1).to_broadcast([NSM, 2, NSM])
                        dve.wait_ge(g_.sem, g_.at("sx0", i))
                        v.done(tt(um, one4, xm[:, 0, :, :], ALU.subtract), "u0")
                        WQ("z0")
                        v.done(tt(tm, one4, j4(ps[:, 6, :]), ALU.subtract), "t0")
                        v.done(tt(su[:, :, :], one2, sxm[:, 0, :, :], ALU.subtract), "su0")
                        WQ("sz0")
                        v.done(tt(st_[:, :, :], one2, h2(ps[0:NSM, 4, 0:64]), ALU.subtract), "st0")
                        continue
                    if l < 6:
                        WQ(f"t{l}")
                        v.done(tt(tm, tm, j4(ps[:, 2, :]), ALU.subtract), f"t{l}")
                    WQ(f"u{l}")
                    v.done(tt(um, um, j4(ps[:, 3, :]), ALU.subtract), f"u{l}")
                    if l == 1:
                        WQ("su1")
                        v.done(tt(su[:, :, :], su[:, :, :], h2(ps[0:NSM, 5, 0:64]), ALU.subtract), "su1")
                    if l == 3:
                        merge(1, 0)
                merge(1, 1)
                WQ("s0")
                v.done(ts(st0[:, :], ps[:, 2, 0:64], er[:, P - 1:P], ec[:, 1:2], ALU.mult, ALU.mult), "s0")
                WQ("s1")
                v.done(tt(st1[:, :], ps[:, 2, 0:64], st0[:, :], ALU.add), "s1a")
                W("s1a")
                v.done(ts(st1[:, :], st1[:, :], er[:, NPR - 1:NPR], None, ALU.mult), "s1")
                WQ("ds")
                v.done(tt(sts[:, :, :], sts[:, :, :], ps[:, 5, :].rearrange("p (b n) -> p b n", b=NB), ALU.add), "ds")
                W("ds")
                v.done(tt(sts[:, :, :], sts[:, :, :], seq(er)[:, :, NL - 1:NL].to_broadcast([P, NB, 64]), ALU.mult), "dsp")
                WA("ys")
                v.done(tt(sg[:, NPR:T], sg[:, NPR:T], er[:, NPR:T], ALU.add), "ysum")
                W("ysum")
                WQ("mean")
                v.done(tt(ekap, sg, ps[:, 3, 0:T], ALU.subtract), "d")
                WQ("var")
                v.done(ts(ek, ps[:, 2, 0:T], GN_EPS, None, ALU.add), "ve")
                WA("groot")
                v.done(nc.vector.reciprocal(ek, ek), "grec")
                W("grec")
                v.done(stt(out=ekap, in0=ekap, scalar=par("gn_w", i), in1=ek, op0=ALU.mult, op1=ALU.mult), "y")
                v.done(tt(csm, v_, ps[:, 4, 0:T], ALU.mult), "bon")
                W("bon")
                v.done(stt(out=rwx[:, bass.ds(i, 1), 0:T].rearrange("p o t -> p (o t)"), in0=ekap, scalar=par("gn_b", i),
                           in1=csm, op0=ALU.add, op1=ALU.add), "o")

        @block.gpsimd
        def _(pool):
            tt = nc.gpsimd.tensor_tensor
            pool.sem_inc(g_.sem, g_.n)

            def spread(out, src):
                return tt(out, src.unsqueeze(1).to_broadcast([NSM, NB, P]),
                          K("of_seq", NSM).unsqueeze(2).to_broadcast([NSM, NB, P]), ALU.mult)
            with pool.Fori(0, N) as i:
                bb = bbm[:, :, :, 0, :].rearrange("p h c t -> p (h c) t")
                for l in LV:
                    if l == 0:
                        pool.wait_ge(v.sem, v.at("bk11", i))
                    if l >= 2:
                        pool.wait_ge(q.sem, q.at(f"z{l - 2}", i))
                        if l == 2:
                            pool.wait_ge(v.sem, v.at("u0", i))
                    g_.done(tt(xm[:, l % 2, :, :], bb, K(f"level{LEVELS[l]}").unsqueeze(1).to_broadcast([P, 4, P]), ALU.mult), f"x{l}")
                    if l < 2:
                        if l == 0:
                            pool.wait_ge(v.sem, v.at("sk1", i))
                        g_.done(tt(sxm[:, l, :, :], sk[:, :, 1, 0, :],
                                   K(f"seq_level{LEVELS[l]}", NSM).unsqueeze(1).to_broadcast([NSM, 2, NSM]), ALU.mult), f"sx{l}")
                    if l == 2:
                        pool.wait_ge(a.sem, a.at("tr2", i))
                        g_.done(spread(vx[:, :, :], tok[0:NSM, 2, 0:P]), "vx")
                    if l == 3:
                        pool.wait_ge(v.sem, v.at("m01", i))
                        m = mrg[:, bass.ds(i * 2, 1), :].rearrange("p o t -> p (o t)")
                        g_.done(tt(m, m, gtmp[:, :], ALU.add), "m0")
                pool.wait_ge(a.sem, a.at("sas", i))
                g_.done(spread(nx[:, :, :], nsa[0:NSM, 2, :]), "nx")
                pool.wait_ge(v.sem, v.at("m11", i))
                m = mrg[:, bass.ds(i * 2 + 1, 1), :].rearrange("p o t -> p (o t)")
                g_.done(tt(m, m, gtmp[:, :], ALU.add), "m1")


class Norm:

    def __init__(self, nc, ctx, name, src, out, gain, bank, width, tmp):
        self.nc, self.src, self.out, self.gain, self.bank, self.width = nc, src, out, gain, bank, width
        self.sq, self.rstd = tmp[:, 0:2, 0:width], tmp[:, 2, 0:width]
        new = lambda n: ctx.enter_context(nc.semaphore(f"{name}_{n}"))
        self.squared = new("squared")
        self.summed = new("summed")
        self.mean, self.rooted = new("mean"), new("root")
        self.inverse = new("inverse")
        self.done = new("done")

    def act(self, act):
        for k in range(KD):
            if k >= 2:
                act.wait_ge(self.summed, k - 1)
            self.nc.scalar.activation(self.sq[:, k % 2, :], self.src[:, k, :], ACT.Square).then_inc(self.squared, 1)
        act.wait_ge(self.mean, 1)
        self.nc.scalar.activation(self.rstd, self.rstd, ACT.Sqrt).then_inc(self.rooted, 1)

    def pe(self, pe, ps, ones):
        for k in range(KD):
            pe.wait_ge(self.squared, k + 1)
            self.nc.tensor.matmul(ps[:, self.bank, 0:self.width], ones, self.sq[:, k % 2, :], start=(k == 0),
                                  stop=(k == KD - 1)).then_inc(self.summed, 1)

    def dve(self, dve, ps):
        dve.wait_ge(self.summed, KD)
        self.nc.vector.tensor_scalar(self.rstd, ps[:, self.bank, 0:self.width], 1.0 / D, RMS_EPS, ALU.mult, ALU.add
                                     ).then_inc(self.mean, 1)
        dve.wait_ge(self.rooted, 1)
        self.nc.vector.reciprocal(self.rstd, self.rstd).then_inc(self.inverse, 1)
        dve.wait_ge(self.inverse, 1)
        for k in range(KD):
            self.nc.vector.scalar_tensor_tensor(out=self.out[:, k, :], in0=self.src[:, k, :], scalar=self.gain(k),
                                                in1=self.rstd, op0=ALU.mult, op1=ALU.mult).then_inc(self.done, 1)


def stage_merge(nc, ctx0, A, O, env):
    ring, xn, mrg, ps, const, K, par, rwx = (env[k] for k in "ring xn mrg ps const K par rwx".split())
    res = xn
    with ExitStack() as ctx:
        sem = lambda n: ctx.enter_context(nc.semaphore(n))
        gate = ctx.enter_context(nc.sbuf_tensor("gate", [P, 2, T], F32))
        up = ctx.enter_context(nc.sbuf_tensor("up", [P, 2, T], F32))
        slots = [sem(f"g_slot{s}") for s in range(4)]
        oslots = [sem(f"g_oslot{s}") for s in range(4)]
        again = sem("g_again")
        N = KH // 2
        q = Steps(ctx, nc, "g_pe", [f"{x}{d}" for d in range(4) for x in "GU"])
        a = Steps(ctx, nc, "g_act", [f"G{d}" for d in range(4)])
        v = Steps(ctx, nc, "g_dve", [f"{x}{d}" for d in range(4) for x in "um"])
        for s_ in (q, a, v):
            s_.lap = 1
        q2 = Steps(ctx, nc, "g_pe2", [f"o{b}" for b in range(8)])
        v2 = Steps(ctx, nc, "g_dve2", [f"o{b}" for b in range(8)])
        block = ctx.enter_context(nc.Block())

        def tile(t, i):
            return t[bass.ds(i, 1), :, :].rearrange("o p n -> (o p) n")

        @block.sync
        def _(sp):
            with sp.Fori(0, N) as i:
                for s in range(2):
                    sp.wait_ge(q.sem, q.at(f"G{2 * s + 1}", i - 1))
                    sp.dma_start(ring[:, 2 * s, :], tile(A["w_gate"][0], i * 2 + s)).then_inc(slots[2 * s], 16)
                    sp.wait_ge(q.sem, q.at(f"U{2 * s + 1}", i - 1))
                    sp.dma_start(ring[:, 2 * s + 1, 0:2048], tile(A["w_up_rw"], i * 2 + s)).then_inc(slots[2 * s + 1], 16)
            sp.wait_ge(q.sem, q.at("G3", N - 1))
            sp.dma_start(res[:, :, :], A["xT"][:, :, :]).then_inc(again, 16)
            for u in range(8):
                if u < 4:
                    sp.wait_ge(q.sem, q.at(f"{'GU'[u % 2]}{2 * (u // 2) + 1}", N - 1))
                else:
                    sp.wait_ge(q2.sem, q2.at(f"o{2 * (u - 4) + 1}"))
                sp.dma_start(ring[:, u % 4, :], A["w_out"][u, :, :]).then_inc(oslots[u % 4], 16)

        @block.tensor
        def _(pe):
            mm = nc.tensor.matmul
            pe.sem_inc(q.sem, q.n)
            with pe.Fori(0, N) as i:
                for d in range(4):
                    s, c = 2 * (d // 2), (d % 2) * P
                    wg = ring[:, s, :].rearrange("p (k n) -> p k n", k=KD)
                    wu = ring[:, s + 1, 0:2048].rearrange("p (k n) -> p k n", k=KH)
                    if d % 2 == 0:
                        pe.wait_ge(slots[s], i * 16 + 16)
                    pe.wait_ge(a.sem, a.at(f"G{d - 2}", i) if d >= 2 else a.at(f"G{d + 2}", i - 1))
                    for k in range(KD):
                        ins = mm(ps[:, d % 2, 0:T], wg[:, k, c:c + P], xn[:, k, :], start=(k == 0), stop=(k == KD - 1))
                    q.done(ins, f"G{d}")
                    if d % 2 == 0:
                        pe.wait_ge(slots[s + 1], i * 16 + 16)
                    pe.wait_ge(v.sem, v.at(f"u{d - 2}", i) if d >= 2 else v.at(f"u{d + 2}", i - 1))
                    for k in range(KH):
                        ins = mm(ps[:, 2 + d % 2, 0:T], wu[:, k, c:c + P], rwx[:, k, 0:T], start=(k == 0), stop=(k == KH - 1))
                    q.done(ins, f"U{d}")
            pe.wait_ge(v.sem, v.at("m3", N - 1))
            for j in range(KD):
                s = (j // 2) % 4
                w = ring[:, s, :].rearrange("p (k n) -> p k n", k=KD)
                pe.wait_ge(oslots[s], 16 * (j // 8 + 1))
                if j >= 4:
                    pe.wait_ge(v2.sem, v2.at(f"o{(j - 4) % 8}", (j - 4) // 8))
                for k in range(KD):
                    ins = mm(ps[:, 4 + j % 4, 0:T], w[:, k, (j % 2) * P:(j % 2 + 1) * P], mrg[:, k, :],
                             start=(k == 0), stop=(k == KD - 1))
                q2.done(ins, f"o{j % 8}")

        @block.scalar
        def _(act):
            act.sem_inc(a.sem, a.n)
            with act.Fori(0, N) as i:
                for d in range(4):
                    act.wait_ge(q.sem, q.at(f"G{d}", i))
                    act.wait_ge(v.sem, v.at(f"u{d - 2}", i) if d >= 2 else v.at(f"u{d + 2}", i - 1))
                    a.done(nc.scalar.activation(gate[:, d % 2, :], ps[:, d % 2, 0:T], ACT.Sigmoid), f"G{d}")

        @block.vector
        def _(dve):
            dve.sem_inc(v.sem, v.n)
            with dve.Fori(0, N) as i:
                for d in range(4):
                    dve.wait_ge(q.sem, q.at(f"U{d}", i))
                    dve.wait_ge(a.sem, a.at(f"G{d}", i))
                    dve.wait_ge(v.sem, v.at(f"m{d - 2}", i) if d >= 2 else v.at(f"m{d + 2}", i - 1))
                    v.done(nc.vector.tensor_tensor(up[:, d % 2, :], gate[:, d % 2, :], ps[:, 2 + d % 2, 0:T], ALU.mult), f"u{d}")
                    dve.wait_ge(v.sem, v.at(f"u{d}", i))
                    m = mrg[:, bass.ds(i * 4 + d, 1), :].rearrange("p o t -> p (o t)")
                    v.done(nc.vector.scalar_tensor_tensor(out=m, in0=m, scalar=0.5, in1=up[:, d % 2, :],
                                                          op0=ALU.mult, op1=ALU.add), f"m{d}")
            dve.wait_ge(again, 16)
            for j in range(KD):
                dve.wait_ge(q2.sem, q2.at(f"o{j % 8}", j // 8))
                v2.done(nc.vector.tensor_tensor(res[:, j, :], res[:, j, :], ps[:, 4 + j % 4, 0:T], ALU.add), f"o{j % 8}")


def stage_cross(nc, ctx0, A, O, env):
    ring, res, xn, ps, const, K, par = (env[k] for k in "ring xn mrg ps const K par".split())
    with ExitStack() as ctx:
        sem = lambda n: ctx.enter_context(nc.semaphore(n))
        sb = lambda n, s: ctx.enter_context(nc.sbuf_tensor(n, s, F32))
        kc = sb("kc", [P, XH, NB, MEM])
        mem = sb("mem", [P, KD, MEM])
        vc = [sb("vc", [P, NB, XH, P]),
              mem[:, :, :].rearrange("p k m -> p (k m)").rearrange("p (b h d) -> p b h d", b=NB, h=XH)]
        mkt = sb("mkt", [P, XH, MEM])
        mv = sb("mv", [P, 2, XH * P])
        qt = sb("qt", [P, XH, T])
        ot = sb("ot", [P, XH, T])
        tmp, tmp2 = sb("ntmp", [P, 3, T]), sb("ntmp2", [P, 3, T])
        sT = sb("sT", [P, 2, P])
        pr = sb("pr", [P, 2, MEM])
        pt = sb("pt", [P, 2, 2, P])
        mx, sm = sb("mx", [P, 9]), sb("sm", [P, 9])
        scale = float(P) ** -0.5
        nm = Norm(nc, ctx, "xm", mem, mem, lambda k: par("g_mem", k), 7, MEM, tmp)
        nx_ = Norm(nc, ctx, "xx", res, xn, lambda k: par("g_xa", k), 6, T, tmp2)
        memory, kc_in, vc_in = sem("x_memory"), sem("x_kc"), sem("x_vc")
        vc_in1 = sem("x_vc1")
        slots = [sem(f"x_slot{s}") for s in range(4)]
        stored = sem("x_stored")
        order = [(h, c) for h in range(XH) for c in range(2)] + [None]
        J = range(9)
        pe_steps = [f"k{h}" for h in range(XH)] + [f"v{j}" for j in range(4)] + [f"q{h}" for h in range(XH)] + ["sT"]
        pe_steps += ["s0"] + sum([([f"s{j + 1}"] if j < 8 else []) + [f"t{j}", f"o{j}"] for j in J], [])
        q = Steps(ctx, nc, "x_pe", pe_steps + [f"w{j}" for j in range(KD)])
        a = Steps(ctx, nc, "x_act", [f"k{h}" for h in range(XH)] + [f"v{m}" for m in range(2)] + [f"q{h}" for h in range(XH)]
                  + ["sT"] + sum([[f"e{j}", f"t{j}", f"o{j}"] for j in J], []))
        v = Steps(ctx, nc, "x_dve", sum([[f"mx{j}", f"nb{j}", f"r{j}", f"p{j}"] for j in J], []) + [f"w{j}" for j in range(KD)])
        block = ctx.enter_context(nc.Block())

        @block.sync
        def _(sp):
            sp.dma_start(mem[:, :, :], A["memT"][:, :, :]).then_inc(memory, 16)
            for s, n in enumerate(("w_xk", "w_xv")):
                for u in range(2):
                    sp.dma_start(ring[:, 2 * s + u, :], A[n][u, :, :]).then_inc(slots[2 * s + u], 16)
            sp.dma_start(kc[:, :, :, :], A["kc"][:, :, :, :]).then_inc(kc_in, 16)
            for u in range(2):
                sp.wait_ge(q.sem, q.at(f"k{2 * u + 1}"))
                sp.dma_start(ring[:, u, :], A["w_xq"][u, :, :]).then_inc(slots[u], 16)
            sp.dma_start(vc[0][:, :, :, :], A["vc"][:, 0, :, :, :]).then_inc(vc_in, 16)
            sp.wait_ge(q.sem, q.at("v3"))
            sp.dma_start(vc[1], A["vc"][:, 1, :, :, :]).then_inc(vc_in1, 16)
            for u in range(2):
                sp.wait_ge(q.sem, q.at(f"v{2 * u + 1}"))
                sp.dma_start(ring[:, 2 + u, :], A["w_xo"][u, :, :]).then_inc(slots[2 + u], 16)
            sp.wait_ge(a.sem, a.at("v1"))
            sp.dma_start(O["mk"][:, :, :], mkt[:, :, :]).then_inc(stored, 16)
            sp.dma_start(O["mv"][:, :, :], mv[:, :, :]).then_inc(stored, 16)
            sp.wait_ge(stored, 32)

        @block.tensor
        def _(pe):
            mm, ident = nc.tensor.matmul, K("ident")
            w = [ring[:, s, :].rearrange("p (k n) -> p k n", k=KD) for s in range(4)]
            nm.pe(pe, ps, K("ones"))
            nx_.pe(pe, ps, K("ones"))
            for h in range(XH):
                if h % 2 == 0:
                    pe.wait_ge(slots[h // 2], 16)
                for k in range(KD):
                    if h == 0:
                        pe.wait_ge(nm.done, k + 1)
                    ins = mm(ps[:, h, 0:MEM], w[h // 2][:, k, (h % 2) * P:(h % 2 + 1) * P], mem[:, k, :],
                             start=(k == 0), stop=(k == KD - 1))
                q.done(ins, f"k{h}")
            for u in range(2):
                pe.wait_ge(slots[2 + u], 16)
                for m in range(2):
                    for k in range(KD):
                        ins = mm(ps[:, 4 + m, u * 256:(u + 1) * 256], mem[:, k, m * P:(m + 1) * P], w[2 + u][:, k, :],
                                 start=(k == 0), stop=(k == KD - 1))
                    q.done(ins, f"v{2 * u + m}")
            for h in range(XH):
                if h % 2 == 0:
                    pe.wait_ge(slots[h // 2], 32)
                pe.wait_ge(a.sem, a.at(f"k{h}"))
                for k in range(KD):
                    if h == 0:
                        pe.wait_ge(nx_.done, k + 1)
                    ins = mm(ps[:, h, 0:T], w[h // 2][:, k, (h % 2) * P:(h % 2 + 1) * P], xn[:, k, :],
                             start=(k == 0), stop=(k == KD - 1))
                q.done(ins, f"q{h}")
            pe.wait_ge(kc_in, 16)
            pe.wait_ge(nm.mean, 1)
            pe.wait_ge(a.sem, a.at(f"q{XH - 1}"))
            for m in range(2):
                for h in range(XH):
                    for b in range(NB):
                        n = m * P + h * NSM + b * NL
                        ins = mm(ps[:, 7, n:n + NL], kc[:, h, b, m * P:(m + 1) * P], qt[:, h, NPR + b * NL:NPR + (b + 1) * NL],
                                 start=True, stop=True)
            q.done(ins, "sT")

            def scores(j):
                if j >= 2:
                    pe.wait_ge(a.sem, a.at(f"e{j - 2}"))
                if order[j] is None:
                    pe.wait_ge(a.sem, a.at("sT"))
                    for m in range(2):
                        ins = nc.tensor.transpose(ps[:, j % 2, m * P:(m + 1) * P], sT[:, m, :], ident)
                else:
                    h, c = order[j]
                    ins = mm(ps[:, j % 2, 0:MEM], qt[:, h, c * P:(c + 1) * P], mkt[:, h, :], start=True, stop=True)
                q.done(ins, f"s{j}")
            scores(0)
            for j in J:
                if j < 8:
                    scores(j + 1)
                pe.wait_ge(v.sem, v.at(f"p{j}"))
                if j >= 2:
                    pe.wait_ge(a.sem, a.at(f"t{j - 2}"))
                for m in range(2):
                    ins = nc.tensor.transpose(ps[:, 2 + j % 2, m * P:(m + 1) * P], pr[:, j % 2, m * P:(m + 1) * P], ident)
                q.done(ins, f"t{j}")
                pe.wait_ge(a.sem, a.at(f"t{j}"))
                if j >= 2:
                    pe.wait_ge(a.sem, a.at(f"o{j - 2}"))
                o = ps[:, 4 + j % 2, 0:P]
                if order[j] is None:
                    pe.wait_ge(vc_in, 16)
                    pe.wait_ge(vc_in1, 16)
                    for h in range(XH):
                        for b in range(NB):
                            n = h * NSM + b * NL
                            for m in range(2):
                                ins = mm(o[:, n:n + NL], vc[m][:, b, h, :], pt[:, j % 2, m, n:n + NL], start=(m == 0), stop=(m == 1))
                else:
                    h, c = order[j]
                    for m in range(2):
                        ins = mm(o, mv[:, m, h * P:(h + 1) * P], pt[:, j % 2, m, :], start=(m == 0), stop=(m == 1))
                q.done(ins, f"o{j}")
            pe.wait_ge(a.sem, a.at("o8"))
            for j in range(KD):
                u, c = j // 8, (j % 8) * P
                wo = ring[:, 2 + u, :].rearrange("p (k n) -> p k n", k=XH)
                pe.wait_ge(slots[2 + u], 32)
                if j >= 4:
                    pe.wait_ge(v.sem, v.at(f"w{j - 4}"))
                for k in range(XH):
                    ins = mm(ps[:, j % 4, 0:T], wo[:, k, c:c + P], ot[:, k, :], start=(k == 0), stop=(k == XH - 1))
                q.done(ins, f"w{j}")

        @block.scalar
        def _(act):
            fn = nc.scalar.activation
            act.wait_ge(memory, 16)
            nm.act(act)
            nx_.act(act)
            for h in range(XH):
                act.wait_ge(q.sem, q.at(f"k{h}"))
                a.done(fn(mkt[:, h, :], ps[:, h, 0:MEM], ACT.Copy), f"k{h}")
            for m in range(2):
                act.wait_ge(q.sem, q.at(f"v{2 + m}"))
                a.done(fn(mv[:, m, :], ps[:, 4 + m, :], ACT.Copy), f"v{m}")
            for h in range(XH):
                act.wait_ge(q.sem, q.at(f"q{h}"))
                a.done(fn(qt[:, h, :], ps[:, h, 0:T], ACT.Copy), f"q{h}")
            act.wait_ge(q.sem, q.at("sT"))
            a.done(fn(sT[:, :, :], ps[:, 7, 0:2 * P].rearrange("p (m n) -> p m n", m=2), ACT.Copy), "sT")
            for j in J:
                act.wait_ge(v.sem, v.at(f"nb{j}"))
                if j >= 2:
                    act.wait_ge(q.sem, q.at(f"t{j - 2}"))
                a.done(fn(pr[:, j % 2, :], ps[:, j % 2, 0:MEM], ACT.Exp, bias=mx[:, j:j + 1], scale=scale,
                          accum_out=sm[:, j:j + 1]), f"e{j}")
                act.wait_ge(q.sem, q.at(f"t{j}"))
                if j >= 2:
                    act.wait_ge(q.sem, q.at(f"o{j - 2}"))
                a.done(fn(pt[:, j % 2, :, :], ps[:, 2 + j % 2, 0:2 * P].rearrange("p (m n) -> p m n", m=2), ACT.Copy), f"t{j}")
                act.wait_ge(q.sem, q.at(f"o{j}"))
                if order[j] is None:
                    ins = fn(ot[:, :, NPR:T], ps[:, 4 + j % 2, 0:P].rearrange("p (h n) -> p h n", h=XH), ACT.Copy)
                else:
                    h, c = order[j]
                    ins = fn(ot[:, h, c * P:(c + 1) * P], ps[:, 4 + j % 2, 0:P], ACT.Copy)
                a.done(ins, f"o{j}")

        @block.vector
        def _(dve):
            nm.dve(dve, ps)
            nx_.dve(dve, ps)
            for j in J:
                dve.wait_ge(q.sem, q.at(f"s{j}"))
                v.done(nc.vector.tensor_reduce(mx[:, j:j + 1], ps[:, j % 2, 0:MEM], AX.X, ALU.max), f"mx{j}")
                dve.wait_ge(v.sem, v.at(f"mx{j}"))
                v.done(nc.vector.tensor_scalar(mx[:, j:j + 1], mx[:, j:j + 1], -scale, None, ALU.mult), f"nb{j}")
                dve.wait_ge(a.sem, a.at(f"e{j}"))
                v.done(nc.vector.reciprocal(sm[:, j:j + 1], sm[:, j:j + 1]), f"r{j}")
                dve.wait_ge(v.sem, v.at(f"r{j}"))
                v.done(nc.vector.tensor_scalar(pr[:, j % 2, :], pr[:, j % 2, :], sm[:, j:j + 1], None, ALU.mult), f"p{j}")
            for j in range(KD):
                dve.wait_ge(q.sem, q.at(f"w{j}"))
                v.done(nc.vector.tensor_tensor(res[:, j, :], res[:, j, :], ps[:, j % 4, 0:T], ALU.add), f"w{j}")


def stage_moe(nc, ctx0, A, O, env):
    ring, res, xn, ps, const, K, par = (env[k] for k in "ring xn mrg ps const K par".split())
    C, CAP, ROUNDS, PAIRS = 3, 64, -(-T // 64), NE // 2
    NF = 2
    rows = [P, P, NSM]
    with ExitStack() as ctx:
        sem = lambda n: ctx.enter_context(nc.semaphore(n))
        sb = lambda n, s, t=F32: ctx.enter_context(nc.sbuf_tensor(n, s, t))
        ring2 = sb("ring2", [P, 2, SLOT])
        x2t = sb("x2t", [P, C, D])
        tmp = sb("etmp", [P, 3, T])
        wr, br = sb("wr", [P, KD, 36]), sb("br", [P, 36])
        L = sb("L", [P, C, 36])
        ex, pen, gsum = sb("ex", [P, C, 4]), sb("pen", [P, C, 4]), sb("gsum", [P, C, 1])
        top, first = sb("top", [P, C, 2]), sb("first", [P, C, 2])
        gates, score = sb("gates", [P, C, 2]), sb("score", [P, C, NE])
        pick = [sb(f"pick{n}", [P, C, NE]) for n in range(2)]
        sel, rank = sb("sel", [P, C, NE]), sb("rank", [P, C, NE])
        comb = sb("comb", [P, C, ROUNDS * NE])
        pos = sb("pos", [P, C, ROUNDS * NE])
        count, over = sb("count", [P, 1]), sb("over", [P, ROUNDS - 1])
        turns_f, turns = sb("turns_f", [P, 1]), sb("turns", [P, 1], mybir.dt.int32)
        put = sb("put", [P, C, 2 * CAP])
        take = sb("take", [P, C, 2 * CAP])
        takeT = sb("takeT", [P, T])
        xg = sb("xg", [P, KD, 2 * CAP])
        sg, h = sb("sg", [P, 2, NF, CAP]), sb("h", [P, 2, NF, CAP])
        y = sb("y", [P, D])

        nm = Norm(nc, ctx, "en", res, xn, lambda k: par("g_moe", k), 7, T, tmp)
        nf = Norm(nc, ctx, "ef", res, xn, lambda k: par("g_final", k), 7, T, tmp)
        wr_in, stored = sem("e_wr"), sem("e_stored")
        last_pe, last = sem("e_last_pe"), sem("e_last")
        slot = [sem(f"e_slot{s}") for s in range(6)]
        ready = [ring[:, s, :] for s in range(4)] + [ring2[:, s, :] for s in range(2)]
        transposes = [(c, g) for c in range(C) for g in range(4)]
        qr = Steps(ctx, nc, "e_pe0", [f"r{c}" for c in range(C)] + [f"x{c}{g}" for c, g in transposes]
                   + [f"rank{c}" for c in range(C)] + ["count"])
        ar = Steps(ctx, nc, "e_act0", [f"x{c}{g}" for c, g in transposes] + ["ex", "e2"])
        router = (["zero"] + [f"r{c}" for c in range(C)] + ["gmax", "gdiff", "gsum", "pg", "geq", "gidx", "gfirst", "gone", "pen", "le"]
                  + sum([[f"top{n}", f"eq{n}", f"idx{n}", f"first{n}", f"one{n}"] + (["le2"] if n == 0 else []) for n in range(2)], [])
                  + ["dv", "e2p", "g1", "g1p", "g2", "sel", "c0"] + ["comb"] + [f"rank{c}" for c in range(C)]
                  + ["pos0", "pos1"] + ["pos"] + ["count", "over", "osum", "turns"])
        vr = Steps(ctx, nc, "e_dve0", router)
        q = Steps(ctx, nc, "e_pe", [f"x{g}" for g in range(4)] + ["u0", "u1"] + [f"s{k}" for k in range(KD)] + ["t", "d0", "d1"])
        a = Steps(ctx, nc, "e_act", [f"x{g}" for g in range(4)] + ["g0", "g1", "t", "y"])
        v = Steps(ctx, nc, "e_dve", ["sel", "m0", "h0", "m1", "h1"] + [f"s{k}" for k in range(KD)])
        for s_ in (q, a, v):
            s_.lap = 1
        block = ctx.enter_context(nc.Block())

        def turn_count(eng):
            eng.wait_ge(vr.sem, vr.at("turns"))
            return eng.value_load(turns[0:1, 0:1], min_val=PAIRS, max_val=PAIRS * ROUNDS)

        @block.sync
        def _(sp):
            def load(j, i):
                for u in range(2):
                    if i is not None:
                        sp.wait_ge(q.sem, q.at(f"u{u}", i - 1))
                    for n, w in enumerate(("w_eg", "w_eu")):
                        sp.dma_start(ready[2 * u + n], A[w][bass.ds(j * 2 + u, 1), :, :].rearrange("o p n -> (o p) n")
                                     ).then_inc(slot[2 * u + n], 16)
                for u in range(2):
                    if i is not None:
                        sp.wait_ge(q.sem, q.at(f"d{u}", i - 1))
                    sp.dma_start(ready[4 + u], A["w_ed"][bass.ds(j * 2 + u, 1), :, :].rearrange("o p n -> (o p) n")
                                 ).then_inc(slot[4 + u], 16)
            sp.dma_start(wr[:, :, :], A["w_router"][:, :, :]).then_inc(wr_in, 16)
            sp.dma_start(br[:, :], A["b_router"][:, :]).then_inc(wr_in, 16)
            load(0, None)
            with sp.Fori(1, turn_count(sp)) as i:
                load(i % PAIRS, i)
            sp.wait_ge(nf.done, KD)
            sp.dma_start(O["y"][:, :, :], xn[:, :, :]).then_inc(stored, 16)
            sp.wait_ge(stored, 16)

        @block.tensor
        def _(pe):
            mm, ident = nc.tensor.matmul, K("ident")
            nm.pe(pe, ps, K("ones"))
            pe.wait_ge(wr_in, 32)
            for c in range(C):
                for k in range(KD):
                    if c == 0:
                        pe.wait_ge(nm.done, k + 1)
                    ins = mm(ps[0:rows[c], c, 0:36], xn[:, k, c * P:c * P + rows[c]], wr[:, k, :],
                             start=(k == 0), stop=(k == KD - 1))
                qr.done(ins, f"r{c}")
            for n, (c, g) in enumerate(transposes):
                if n >= 2:
                    pe.wait_ge(ar.sem, ar.at("x%d%d" % transposes[n - 2]))
                for k in range(4):
                    ins = nc.tensor.transpose(ps[0:rows[c], 4 + n % 2, k * P:(k + 1) * P],
                                              xn[:, g * 4 + k, c * P:c * P + rows[c]], ident)
                qr.done(ins, f"x{c}{g}")
            pe.wait_ge(vr.sem, vr.at("sel"))
            earlier, ones = K("lt_le", b=P), K("ones")
            for c in range(C):
                for e in range(c + 1):
                    left = (earlier if e == c else ones)[0:rows[e], 0:rows[c]]
                    ins = mm(ps[0:rows[c], c, 0:NE], left, sel[0:rows[e], e, :], start=(e == 0), stop=(e == c))
                qr.done(ins, f"rank{c}")
            for e in range(C):
                ins = mm(ps[:, 3, 0:NE], ones[0:rows[e], :], sel[0:rows[e], e, :], start=(e == 0), stop=(e == C - 1))
            qr.done(ins, "count")
            pe.wait_ge(ar.sem, ar.at("x23"))

            def scatter(k, i):
                if k >= 2:
                    pe.wait_ge(v.sem, v.at(f"s{k - 2}", i + 1))
                q.done(mm(ps[:, k % 2, 0:T], y[:, k * P:(k + 1) * P], takeT[:, :], start=True, stop=True), f"s{k}")

            total = turn_count(pe)
            pe.sem_inc(q.sem, q.n)
            with pe.Fori(0, total) as i:
                pe.wait_ge(v.sem, v.at("sel", i))
                pe.wait_ge(v.sem, v.at(f"s{KD - 1}", i - 1))
                for g in range(4):
                    if g >= 2:
                        pe.wait_ge(a.sem, a.at(f"x{g - 2}", i))
                    for k in range(4 * g, 4 * g + 4):
                        for c in range(C):
                            ins = mm(ps[:, g % 2, (k % 4) * P:(k % 4 + 1) * P], x2t[0:rows[c], c, k * P:(k + 1) * P],
                                     put[0:rows[c], c, :], start=(c == 0), stop=(c == C - 1))
                    q.done(ins, f"x{g}")
                for u in range(2):
                    pe.wait_ge(a.sem, a.at("x3", i))
                    pe.wait_ge(slot[2 * u], i * 16 + 16)
                    pe.wait_ge(slot[2 * u + 1], i * 16 + 16)
                    pe.wait_ge(a.sem, a.at("t", i - 1))
                    for n in range(2):
                        w = ready[2 * u + n].rearrange("p (k f) -> p k f", k=KD)
                        for f in range(NF):
                            for k in range(KD):
                                ins = mm(ps[:, 2 + u, (n * NF + f) * CAP:(n * NF + f + 1) * CAP], w[:, k, f * P:(f + 1) * P],
                                         xg[:, k, u * CAP:(u + 1) * CAP], start=(k == 0), stop=(k == KD - 1))
                    q.done(ins, f"u{u}")
                pe.wait_ge(a.sem, a.at("y", i - 1))
                pe.wait_ge(a.sem, a.at("x3", i))
                for k in range(KD):
                    scatter(k, i - 1)
                pe.wait_ge(v.sem, v.at("h1", i))
                for c in range(C):
                    ins = nc.tensor.transpose(ps[:, 2, c * P:c * P + rows[c]], take[0:rows[c], c, :],
                                              K("ident", rows[c], 0, rows[c]))
                q.done(ins, "t")
                for u in range(2):
                    pe.wait_ge(slot[4 + u], i * 16 + 16)
                    w = ready[4 + u].rearrange("p (f d) -> p f d", f=NF)
                    for n in range(4):
                        for f in range(NF):
                            ins = mm(ps[u * CAP:(u + 1) * CAP, 4 + n, :], h[:, u, f, :], w[:, f, n * 512:(n + 1) * 512],
                                     start=(f == 0), stop=(f == NF - 1))
                    q.done(ins, f"d{u}")
            pe.wait_ge(v.sem, v.at(f"s{KD - 1}", total - 1))
            pe.wait_ge(a.sem, a.at("y", total - 1))
            for k in range(KD):
                if k >= 2:
                    pe.wait_ge(last, k - 1)
                mm(ps[:, k % 2, 0:T], y[:, k * P:(k + 1) * P], takeT[:, :], start=True, stop=True).then_inc(last_pe, 1)
            nf.pe(pe, ps, K("ones"))

        @block.scalar
        def _(act):
            fn = nc.scalar.activation
            nm.act(act)
            for n, (c, g) in enumerate(transposes):
                act.wait_ge(qr.sem, qr.at(f"x{c}{g}"))
                ar.done(fn(x2t[0:rows[c], c, g * 512:(g + 1) * 512], ps[0:rows[c], 4 + n % 2, :], ACT.Copy), f"x{c}{g}")
            act.wait_ge(vr.sem, vr.at("gdiff"))
            ar.done(fn(ex[:, :, :], ex[:, :, :], ACT.Exp), "ex")
            act.wait_ge(vr.sem, vr.at("dv"))
            ar.done(fn(gates[:, :, 1:2], gates[:, :, 1:2], ACT.Exp), "e2")
            total = turn_count(act)
            act.sem_inc(a.sem, a.n)
            with act.Fori(0, total) as i:
                for g in range(4):
                    act.wait_ge(q.sem, q.at(f"x{g}", i))
                    act.wait_ge(q.sem, q.at("u1", i - 1))
                    a.done(fn(xg[:, 4 * g:4 * g + 4, :].rearrange("p k s -> p (k s)"), ps[:, g % 2, :], ACT.Copy), f"x{g}")
                for u in range(2):
                    act.wait_ge(q.sem, q.at(f"u{u}", i))
                    act.wait_ge(v.sem, v.at(f"h{u}", i - 1))
                    a.done(fn(sg[:, u, :, :].rearrange("p f s -> p (f s)"), ps[:, 2 + u, 0:NF * CAP], ACT.Sigmoid), f"g{u}")
                act.wait_ge(q.sem, q.at("t", i))
                a.done(fn(takeT[:, :], ps[:, 2, 0:T], ACT.Copy), "t")
                act.wait_ge(q.sem, q.at("d1", i))
                for n in range(4):
                    ins = fn(y[:, n * 512:(n + 1) * 512], ps[:, 4 + n, :], ACT.Copy)
                a.done(ins, "y")
            act.wait_ge(last, KD)
            nf.act(act)

        @block.vector
        def _(dve):
            tt, ts, stt = nc.vector.tensor_tensor, nc.vector.tensor_scalar, nc.vector.scalar_tensor_tensor
            red = nc.vector.tensor_reduce

            def then(ins, step):
                vr.done(ins, step)
                dve.wait_ge(vr.sem, vr.at(step))
            nc.vector.memset(y[:, :], 0.0)
            nc.vector.memset(takeT[:, :], 0.0)
            nc.vector.memset(put[:, :, :], 0.0)
            nc.vector.memset(take[:, :, :], 0.0)
            then(nc.vector.memset(L[:, :, :], 0.0), "zero")
            nm.dve(dve, ps)
            dve.wait_ge(wr_in, 32)
            for c in range(C):
                dve.wait_ge(qr.sem, qr.at(f"r{c}"))
                then(tt(L[0:rows[c], c, :], ps[0:rows[c], c, 0:36], br[0:rows[c], :], ALU.add), f"r{c}")
            wide = lambda t, n: t.to_broadcast([P, C, n])
            number = K("expert_id").unsqueeze(1)
            lg = L[:, :, 0:4]
            then(red(top[:, :, 0:1], lg, AX.X, ALU.max), "gmax")
            then(tt(ex[:, :, :], lg, wide(top[:, :, 0:1], 4), ALU.subtract), "gdiff")
            dve.wait_ge(ar.sem, ar.at("ex"))
            then(red(gsum[:, :, :], ex[:, :, :], AX.X, ALU.add), "gsum")
            then(nc.vector.reciprocal(gsum[:, :, :], gsum[:, :, :]), "pg")
            then(tt(pen[:, :, :], lg, wide(top[:, :, 0:1], 4), ALU.is_ge), "geq")
            then(stt(out=pen[:, :, :], in0=pen[:, :, :], scalar=-1000.0, in1=number[:, :, 0:4].to_broadcast([P, C, 4]),
                     op0=ALU.mult, op1=ALU.add), "gidx")
            then(red(first[:, :, 0:1], pen[:, :, :], AX.X, ALU.min), "gfirst")
            then(tt(pen[:, :, :], pen[:, :, :], wide(first[:, :, 0:1], 4), ALU.is_equal), "gone")
            then(ts(pen[:, :, :], pen[:, :, :], 1e30, -1e30, ALU.mult, ALU.add), "pen")
            by_group = lambda t: t.rearrange("p c (g e) -> p c g e", g=4)
            for c in range(C):
                ins = tt(by_group(L[:, :, 4:36])[:, c], by_group(L[:, :, 4:36])[:, c],
                         pen[:, c, :].unsqueeze(2).to_broadcast([P, 4, 8]), ALU.add)
            then(ins, "le")
            le = L[:, :, 4:36]
            for n in range(2):
                then(red(top[:, :, n:n + 1], le, AX.X, ALU.max), f"top{n}")
                then(tt(score[:, :, :], le, wide(top[:, :, n:n + 1], NE), ALU.is_ge), f"eq{n}")
                then(stt(out=score[:, :, :], in0=score[:, :, :], scalar=-1000.0, in1=number.to_broadcast([P, C, NE]),
                         op0=ALU.mult, op1=ALU.add), f"idx{n}")
                then(red(first[:, :, n:n + 1], score[:, :, :], AX.X, ALU.min), f"first{n}")
                then(tt(pick[n][:, :, :], score[:, :, :], wide(first[:, :, n:n + 1], NE), ALU.is_equal), f"one{n}")
                if n == 0:
                    then(stt(out=le, in0=pick[0][:, :, :], scalar=-2e30, in1=le, op0=ALU.mult, op1=ALU.add), "le2")
            then(tt(gates[:, :, 1:2], top[:, :, 1:2], top[:, :, 0:1], ALU.subtract), "dv")
            dve.wait_ge(ar.sem, ar.at("e2"))
            then(ts(gates[:, :, 0:1], gates[:, :, 1:2], 1.0, None, ALU.add), "e2p")
            then(nc.vector.reciprocal(gates[:, :, 0:1], gates[:, :, 0:1]), "g1")
            then(tt(gates[:, :, 0:1], gates[:, :, 0:1], gsum[:, :, :], ALU.mult), "g1p")
            then(tt(gates[:, :, 1:2], gates[:, :, 1:2], gates[:, :, 0:1], ALU.mult), "g2")
            then(tt(sel[:, :, :], pick[0][:, :, :], pick[1][:, :, :], ALU.add), "sel")
            tt(pick[0][:, :, :], pick[0][:, :, :], wide(gates[:, :, 0:1], NE), ALU.mult)
            then(tt(pick[1][:, :, :], pick[1][:, :, :], wide(gates[:, :, 1:2], NE), ALU.mult), "c0")
            for r in range(ROUNDS):
                ins = tt(comb[:, :, r * NE:(r + 1) * NE], pick[0][:, :, :], pick[1][:, :, :], ALU.add)
            then(ins, "comb")
            for c in range(C):
                dve.wait_ge(qr.sem, qr.at(f"rank{c}"))
                ins = nc.vector.tensor_copy(rank[0:rows[c], c, :], ps[0:rows[c], c, 0:NE])
                then(ins, f"rank{c}")
            for c in range(C):
                ins = stt(out=rank[0:rows[c], c, :], in0=rank[0:rows[c], c, :], scalar=1.0, in1=sel[0:rows[c], c, :],
                          op0=ALU.add, op1=ALU.mult)
            then(ins, "pos0")
            for c in range(C):
                ins = ts(rank[0:rows[c], c, :], rank[0:rows[c], c, :], -1.0, None, ALU.add)
            then(ins, "pos1")
            for c in range(C):
                for r in range(ROUNDS):
                    ins = ts(pos[0:rows[c], c, r * NE:(r + 1) * NE], rank[0:rows[c], c, :], float(-r * CAP), None, ALU.add)
            then(ins, "pos")
            dve.wait_ge(qr.sem, qr.at("count"))
            then(red(count[:, :], ps[:, 3, 0:NE], AX.X, ALU.max), "count")
            for r in range(1, ROUNDS):
                ins = ts(over[:, r - 1:r], count[:, :], float(r * CAP), float(PAIRS), ALU.is_gt, ALU.mult)
            then(ins, "over")
            then(red(turns_f[:, :], over[:, :], AX.X, ALU.add), "osum")
            then(ts(turns[:, :], turns_f[:, :], float(PAIRS), None, ALU.add), "turns")

            total = turn_count(dve)
            dve.sem_inc(v.sem, v.n)
            with dve.Fori(0, total) as i:
                dve.wait_ge(q.sem, q.at("t", i - 1))
                for c in range(C):
                    for u in range(2):
                        at = lambda t: t[0:rows[c], c, bass.ds(i * 2 + u, 1)]
                        o = slice(u * CAP, (u + 1) * CAP)
                        ts(put[0:rows[c], c, o], K("slot_id", rows[c]), at(pos), None, ALU.is_equal)
                        ins = ts(take[0:rows[c], c, o], K("slot_id", rows[c]), at(pos), at(comb), ALU.is_equal, ALU.mult)
                v.done(ins, "sel")
                for u in range(2):
                    dve.wait_ge(a.sem, a.at(f"g{u}", i))
                    dve.wait_ge(q.sem, q.at(f"d{u}", i - 1))
                    half = lambda n: ps[:, 2 + u, n * NF * CAP:(n + 1) * NF * CAP]
                    flat = lambda t: t[:, u, :, :].rearrange("p f s -> p (f s)")
                    v.done(tt(flat(sg), flat(sg), half(0), ALU.mult), f"m{u}")
                    dve.wait_ge(v.sem, v.at(f"m{u}", i))
                    v.done(tt(flat(h), flat(sg), half(1), ALU.mult), f"h{u}")
                for k in range(KD):
                    dve.wait_ge(q.sem, q.at(f"s{k}", i))
                    v.done(tt(res[:, k, :], res[:, k, :], ps[:, k % 2, 0:T], ALU.add), f"s{k}")
            dve.wait_ge(v.sem, v.at(f"s{KD - 1}", total - 1))
            for k in range(KD):
                dve.wait_ge(last_pe, k + 1)
                tt(res[:, k, :], res[:, k, :], ps[:, k % 2, 0:T], ALU.add).then_inc(last, 1)
            dve.wait_ge(last, KD)
            nf.dve(dve, ps)



def feature_cols(a):
    a = np.asarray(a)
    f = a.shape[-1]
    lead = a.shape[:-1]
    a = a.reshape(*lead, f // P, P)
    return np.ascontiguousarray(np.moveaxis(np.moveaxis(a, -1, 0), -1, 1))


def weight_units(w, width=256):
    k, n = w.shape
    return np.ascontiguousarray(w.reshape(k // P, P, n // width, width).transpose(2, 1, 0, 3)).reshape(n // width, P, -1)


def lay_out(i):
    g = {n: np.asarray(v) for n, v in i.items()}
    w = g["w_in"][0]
    x = np.concatenate([g["x_prompt"][0], g["x_sample"].reshape(NSM, D)], 0)
    a = {"const": CONST, "xT": feature_cols(x)}
    vec = dict(mu="rw_mu", w0="rw_w0", a0="rw_a0", k_k="rw_k_k", k_a="rw_k_a", r_k="rw_r_k", gn_w="rw_gn_w",
               gn_b="rw_gn_b", ml_gn="ml_gn_w", pool_scale="pool_scale", g_mix="g_mix", g_xa="g_xa", g_mem="g_mem",
               g_moe="g_moe", g_final="g_final")
    a["param"] = np.concatenate([g[vec[n]].reshape(-1, P).T for n, _ in PARAMS], 1)
    a["w_main"] = weight_units(np.concatenate([w[:, 0:3072], w[:, 3200:6272], w[:, 6280:7304]], 1))
    a["w_odd"] = weight_units(np.concatenate([w[:, 3072:3200], w[:, 6272:6280]], 1), 136)[0]
    a["past"] = np.concatenate([feature_cols(g["state_rwkv_shift"][0]).reshape(P, -1),
                                feature_cols(g["state_pool"][0]).reshape(P, -1)], 1)
    small = np.zeros((P, 42), np.float32)
    small[:, 0:32] = g["state_mlstm_n"][0].transpose(2, 1, 0).reshape(P, 32)
    small[0:4, 32], small[0:4, 33] = g["ml_b_i"][0], g["ml_b_f"][0]
    small[0:4, 34:42] = g["state_mlstm_m"][0].T
    a["ml_small"] = small
    pairs = lambda w: weight_units(w)
    a["w_gate"] = np.stack([pairs(w[:, 7304 + b * D:7304 + (b + 1) * D]) for b in range(3)])
    a["w_up_rw"] = weight_units(g["w_up_rwkv"][0])
    a["w_out"] = weight_units(g["w_out"][0])
    a["memT"] = feature_cols(g["mem_prompt"][0])
    a["w_xk"], a["w_xv"], a["w_xq"] = (weight_units(g[n][0]) for n in ("xa_wk", "xa_wv", "xa_wq"))
    a["w_xo"] = weight_units(g["xa_wo"][0], 1024)
    a["w_router"] = feature_cols(np.concatenate([g["moe_wr1"][0], g["moe_wr2"][0]], 1).T)
    a["b_router"] = np.tile(np.concatenate([g["moe_br1"][0], g["moe_br2"][0]]), (P, 1))
    for n, m in (("w_eg", "moe_wg"), ("w_eu", "moe_wu"), ("w_ed", "moe_wd")):
        e, k, f = g[m][0].shape
        a[n] = g[m][0].reshape(e, k // P, P, f).transpose(0, 2, 1, 3).reshape(e, P, -1)
    a["kc"] = g["cache_mem_k"][0].transpose(3, 2, 0, 1)
    a["vc"] = g["cache_mem_v"][0].reshape(NB, 2, P, XH, P).transpose(2, 1, 0, 3, 4)
    a["w_up2"] = np.concatenate([pairs(g["w_up_mlstm"][0]), pairs(g["w_up_pool"][0])], 2)
    a["w_lora"] = np.concatenate([g["rw_w2"][0], g["rw_a2"][0]], 0).reshape(P, KH, P).transpose(1, 0, 2)
    a["rw_s"] = g["state_rwkv_s"][0].reshape(NB, KH, 2, 64, 64).transpose(1, 2, 4, 0, 3).reshape(KH, P, NB, 64)
    a["pool_w"] = g["pool_w"][0].reshape(4, 2, P, 256).transpose(2, 0, 1, 3)
    a["c_in"] = g["state_mlstm_c"][0].transpose(1, 2, 0, 3)
    return {n: np.ascontiguousarray(v) for n, v in a.items()}


OUTS = {"y": (P, KD, T), "mk": (P, XH, MEM), "mv": (P, 2, XH * P), "rw_p": (KH, P, 64), "rw_s": (KH, P, NB, 64), "ml_n": (P, MLH, 9), "ml_m": (MLH, T), "shift": (P, RWT, 9), "pool": (P, KH, 9, BUF), "ml_cp": (MLH, P, DV),
        "ml_cs": (MLH, P, NB, DV)}


def feature_rows(a):
    a = np.moveaxis(a, (0, 1), (-1, -2))
    return np.ascontiguousarray(a).reshape(*a.shape[:-2], -1)


def give_back(o):
    shift = feature_rows(o["shift"])
    pool = feature_rows(o["pool"])
    n = o["ml_n"].transpose(2, 1, 0)
    m = o["ml_m"]
    mk = o["mk"].transpose(2, 1, 0)[None, None]
    mv = o["mv"].transpose(1, 0, 2).reshape(1, 1, MEM, XH, P)
    rw_p = o["rw_p"].reshape(KH, 2, 64, 64).transpose(0, 1, 3, 2).reshape(1, 1, 16, 64, 64)
    rw_s = o["rw_s"].reshape(KH, 2, 64, NB, 64).transpose(3, 0, 1, 4, 2).reshape(1, NB, 16, 64, 64)
    y = feature_rows(o["y"])
    return (y[None, 0:NPR], y[NPR:T].reshape(NB, NL, D), rw_p, shift[None, 0:1], o["ml_cp"][None, None], n[None, 0:1], m[:, NPR - 1][None, None], pool[None, 0:1],
            mk, mv, rw_s, shift[None, 1:9], o["ml_cs"].transpose(2, 0, 1, 3)[None], n[None, 1:9],
            np.ascontiguousarray(m[:, NPR + NL - 1::NL].T)[None], pool[None, 1:9])


def kernel(**inputs):
    import concourse.bacc as bacc
    from concourse.bass_utils import run_bass_kernel_spmd

    nc = bacc.Bacc("TRN2", target_bir_lowering=False, num_devices=1)
    arrays = lay_out(inputs)
    A = {n: nc.dram_tensor(f"in_{n}", a.shape, F32, kind="ExternalInput").ap() for n, a in arrays.items()}
    O = {n: nc.dram_tensor(f"out_{n}", s, F32, kind="ExternalOutput").ap() for n, s in OUTS.items()}
    program(nc, A, O)
    r = run_bass_kernel_spmd(nc, [{f"in_{n}": a for n, a in arrays.items()}], core_ids=[0])
    return give_back({n: r.results[0][f"out_{n}"] for n in OUTS})
```

```python
from contextlib import ExitStack

import numpy as np
import concourse.bass as bass
from concourse import mybir

F32 = mybir.dt.float32
F32R = mybir.dt.float32r
ALU = mybir.AluOpType
ACT = mybir.ActivationFunctionType
AX = mybir.AxisListType

P = 128
D = 2048
KD = D // P
NPR = 256
NB, NL = 8, 4
NSM = NB * NL
T = NPR + NSM
HALF = D // 2
KH = HALF // P
RWT = 25
XW = 1 + NPR + NB * (1 + NL)
MLH, DQK, DV = 4, 128, 256
BUF = 15
PW = BUF + NPR + NB * (BUF + NL)
PS0 = BUF + NPR
WINDOWS = (2, 4, 8, 16)
MEM = 256
XH = 4
NE = 32
SLOT = 4096
ALPHA = float(np.exp(-0.5))
RMS_EPS, GN_EPS = 1e-6, 64e-5

LEVELS = (1, 2, 4, 8, 16, 32, 64)


def constants():
    s = np.arange(P)[:, None]
    t = np.arange(P)[None, :]
    c = {}
    c["ident"] = (s == t)
    c["lt_le"] = np.concatenate([s < t, s <= t], 1)
    for m in LEVELS:
        c[f"level{m}"] = (s // (2 * m) == t // (2 * m)) & (s // m < t // m)
    c["heads"] = (s // 64 == t // 64)
    c["heads_mean"] = (s // 64 == t // 64) / 64.0
    c["ones"] = np.ones((P, P))
    c["ones_dv"] = np.full((P, P), 1.0 / DV)
    same = (s // NL == t // NL)[:, :NSM] & (s < NSM)
    c["seq_lt_le"] = np.concatenate([same & (s < t)[:, :NSM], same & (s <= t)[:, :NSM]], 1)
    for m in (1, 2):
        c[f"seq_level{m}"] = c[f"level{m}"][:, :NSM] & (s < NSM)
    c["of_seq"] = ((s % NSM) // NL == np.arange(NB)[None, :])
    col = np.arange(T)
    first_ml = (col == 0) | ((col >= NPR) & ((col - NPR) % NL == 0))
    c["run_rw"] = np.tile(~(first_ml | (col == P)), (P, 1))
    c["run_ml"] = np.tile(~first_ml, (P, 1))
    c["restart"] = np.tile(np.where(first_ml, -1e30, 0.0), (P, 1))
    c["head_row"] = (s == (np.arange(MLH * P) // P)[None, :])
    c["inv_count"] = np.tile(np.concatenate([1.0 / np.minimum(w, np.arange(16) + 1) for w in WINDOWS]), (P, 1))
    c["slot_id"] = np.tile(np.arange(64), (P, 1))
    c["expert_id"] = np.tile(np.arange(NE), (P, 1))
    at, o = {}, 0
    for n, a in c.items():
        at[n] = (o, o + a.shape[1])
        o += a.shape[1]
    return np.concatenate([a.astype(np.float32) for a in c.values()], 1), at


CONST, CONST_AT = constants()

PARAMS = [("mu", RWT), ("w0", KH), ("a0", KH), ("k_k", KH), ("k_a", KH), ("r_k", KH), ("gn_w", KH), ("gn_b", KH),
          ("ml_gn", KH), ("pool_scale", KH), ("g_mix", KD), ("g_xa", KD), ("g_mem", KD), ("g_moe", KD), ("g_final", KD)]
PARAM_AT, _o = {}, 0
for _n, _w in PARAMS:
    PARAM_AT[_n] = _o
    _o += _w
NPARAM = _o


class Steps:

    def __init__(self, ctx, nc, name, steps):
        self.sem = ctx.enter_context(nc.semaphore(name))
        self.steps = list(steps)
        assert len(set(self.steps)) == len(self.steps)
        self.place = {s: n + 1 for n, s in enumerate(self.steps)}
        self.n = len(self.steps)
        self.next = 0
        self.lap = 0

    def at(self, step, i=0):
        return (i + self.lap) * self.n + self.place[step]

    def done(self, ins, step):
        assert self.steps[self.next % self.n] == step, (step, self.steps[self.next % self.n])
        self.next += 1
        ins.then_inc(self.sem, 1)

    def left_out(self, eng, step, i):
        assert self.steps[self.next % self.n] == step
        eng.wait_ge(self.sem, self.at(step, i) - 1)
        self.next += 1
        eng.sem_inc(self.sem, 1)


NPAST = RWT * NB + KH * NB * BUF


def program(nc, A, O):
    with ExitStack() as ctx:
        at = {}

        def sb(name, shape, c=ctx):
            at[name] = -(-nc.sbuf_base // 32) * 32
            return c.enter_context(nc.sbuf_tensor(name, shape, F32))

        def rounded(name, shape, over, words=0):
            return nc.alloc_sbuf_tensor_at(name, shape, F32R, offset=at[over] + 4 * words)

        def sem(name, c=ctx):
            return c.enter_context(nc.semaphore(name))

        const = sb("const", [P, CONST.shape[1]])
        param = sb("param", [P, NPARAM])
        ring = sb("ring", [P, 4, SLOT])
        xn = sb("xn", [P, KD, T])
        mrg = sb("mrg", [P, KD, T])
        ps = ctx.enter_context(nc.psum_tensor("ps", [P, 8, 512], F32))

        def K(name, rows=P, a=0, b=None, base=0):
            lo, hi = CONST_AT[name]
            return const[base:base + rows, lo + a:(hi if b is None else lo + b)]

        def par(name, i=0):
            if isinstance(i, int):
                return param[:, PARAM_AT[name] + i:PARAM_AT[name] + i + 1]
            return param[:, bass.ds(i + PARAM_AT[name], 1)]

        s_load = sem("s_load")
        with ExitStack() as mix:
            rwx = sb("rwx", [P, RWT, XW], mix)
            o_ml = sb("o_ml", [P, KH, T], mix)
            o_pool = sb("o_pool", [P, KH, T], mix)
            with ExitStack() as c:
                mlu = sb("mlu", [P, 24, T], c)
                poolx = sb("poolx", [P, KH, PW], c)
                gif = sb("gif", [8, T], c)
                stage_project(nc, ctx, A, O, locals())
                stage_mlstm(nc, ctx, A, O, locals())
            stage_rwkv(nc, ctx, A, O, locals())
            stage_merge(nc, ctx, A, O, locals())
        stage_cross(nc, ctx, A, O, locals())
        stage_moe(nc, ctx, A, O, locals())


def stage_project(nc, ctx0, A, O, env):
    ring, xn, mrg, ps, const, param, K, par, rwx, mlu, poolx, gif, o_ml, o_pool, rounded = (
        env[k] for k in "ring xn mrg ps const param K par rwx mlu poolx gif o_ml o_pool rounded".split())
    ITER, G = 7, 4
    TILES = 2 * (ITER * G + 1)
    with ExitStack() as ctx:
        sem = lambda n: ctx.enter_context(nc.semaphore(n))
        sq = ctx.enter_context(nc.sbuf_tensor("sq", [P, 2, T], F32))
        rstd = ctx.enter_context(nc.sbuf_tensor("rstd", [P, T], F32))
        one = ctx.enter_context(nc.sbuf_tensor("one", [P, P], F32))
        past_in = mlu[:, 19:24, :].rearrange("p k t -> p (k t)")[:, 0:NPAST]
        low = lambda k: (o_ml, o_pool)[k // KH][:, k % KH, :]
        high = rounded("w_high", [P, 2, KD, P], "mrg")
        w_parts = rounded("w_rest", [P, G, SLOT], "ring")
        columns = lambda w, n: w[:, :, :].rearrange("p s (k n) -> p s k n", k=KD)[:, n // 2 % G, :, (n % 2) * P:(n % 2 + 1) * P]
        weights, w_rest = lambda n: columns(ring, n), lambda n: columns(w_parts, n)
        x_h, x_l = rounded("x_high", [P, KD, T], "xn"), rounded("x_rest", [P, KD, T], "o_ml")
        loaded, past, constants_in = sem("p_loaded"), sem("p_past"), sem("p_const")
        x_in = [sem(f"p_x{n}") for n in range(4)]
        slot = [sem(f"p_slot{s}") for s in range(G)]
        squared = sem("p_squared")
        rooted = sem("p_rooted")
        x_high = sem("p_x_high")
        summed = sem("p_summed")
        x_rest = sem("p_x_rest")
        v = Steps(ctx, nc, "p_vec", ["var", "rstd"] + [f"xn{k}" for k in range(KD)])
        w_high = sem("p_w_high")
        w_low = sem("p_w_low")
        high_used = sem("p_high_used")
        tile_done = sem("p_tile")
        evac = sem("p_evac")
        one_set = sem("p_one")
        carried = sem("p_carried")
        block = ctx.enter_context(nc.Block())

        @block.sync
        def _(sp):
            for n in range(4):
                sp.dma_start(mrg[:, 4 * n:4 * n + 4, :], A["xT"][:, 4 * n:4 * n + 4, :]).then_inc(x_in[n], 16)
            sp.dma_start(param[:, :], A["param"][:, :]).then_inc(loaded, 16)
            for s in range(G):
                sp.dma_start(ring[:, s, :], A["w_main"][s, :, :]).then_inc(slot[s], 16)
            sp.dma_start(const[:, :], A["const"][:, :]).then_inc(constants_in, 16)
            sp.dma_start(past_in, A["past"][:, :]).then_inc(past, 16)
            with sp.Fori(1, ITER) as i:
                for s in range(G):
                    sp.wait_ge(tile_done, i * 8 - 8 + 2 * s + 2)
                    sp.dma_start(ring[:, s, :], A["w_main"][bass.ds(i * G + s, 1), :, :].rearrange("o p n -> (o p) n")
                                 ).then_inc(slot[s], 16)
            sp.wait_ge(constants_in, 16)
            sp.wait_ge(tile_done, 8 * ITER - 6)
            sp.dma_start(ring[:, 0, :], A["w_main"][ITER * G, :, :]).then_inc(slot[0], 16)

        @block.scalar
        def _(act):
            for k in range(KD):
                if k % 4 == 0:
                    act.wait_ge(x_in[k // 4], 16)
                if k >= 2:
                    act.wait_ge(summed, k - 1)
                nc.scalar.activation(sq[:, k % 2, :], mrg[:, k, :], ACT.Square).then_inc(squared, 1)
            act.wait_ge(v.sem, v.at("var"))
            nc.scalar.activation(rstd[:, :], rstd[:, :], ACT.Sqrt).then_inc(rooted, 1)
            def split(n, i):
                if n % 2 == 0:
                    act.wait_ge(slot[n // 2 % G], i * 16 + 16 * (n // 8 + 1))
                if not (isinstance(i, int) and i == 0 and n < 2):
                    act.wait_ge(w_low, i * 8 + n - 1)
                    act.wait_ge(high_used, i * 8 + n - 1)
                nc.scalar.activation(high[:, n % 2, :, :], weights(n), ACT.Copy).then_inc(w_high, 1)

            def evacuate(outs, b, i, scale=1.0):
                act.wait_ge(tile_done, i * 8 + b + 1)
                for o, lo, hi, seq in outs:
                    src = ps[:, b, lo:hi]
                    if seq:
                        src = src.rearrange("p (b l) -> p b l", l=NL)
                    ins = nc.scalar.activation(o, src, ACT.Copy, scale=scale)
                ins.then_inc(evac, 1)

            def rw_out(a):
                return [(a[:, 1:1 + NPR], 0, NPR, False),
                        (a[:, 1 + NPR:XW].rearrange("p (b l) -> p b l", b=NB)[:, :, 1:1 + NL], NPR, T, True)]
            for k in range(KD):
                act.wait_ge(v.sem, v.at(f"xn{k}"))
                nc.scalar.activation(x_h[:, k, :], low(k), ACT.Copy).then_inc(x_high, 1)
                if k in (7, 14):
                    split((7, 14).index(k), 0)
            with act.Fori(0, 3) as i:
                for b in range(8):
                    split(b + 2, i)
                    evacuate(rw_out(rwx[:, bass.ds(i * 8 + b, 1), :].rearrange("p o x -> p (o x)")), b, i)
            for i in range(3, 6):
                if i == 5:
                    act.wait_ge(carried, 1)
                for b in range(8):
                    split(b + 2, i)
                    evacuate([(mlu[:, (i - 3) * 8 + b, :], 0, T, False)], b, i,
                             DQK ** -0.5 if i == 3 and b >= 4 else 1.0)
            for b in range(8):
                split(b + 2, 6)
                evacuate([(poolx[:, b, BUF:PS0], 0, NPR, False),
                          (poolx[:, b, PS0:PW].rearrange("p (b r) -> p b r", b=NB)[:, :, BUF:BUF + NL], NPR, T, True)],
                         b, 6)
            evacuate(rw_out(rwx[:, 24, :]), 0, 7)
            act.wait_ge(tile_done, TILES)
            nc.scalar.activation(gif[:, :], ps[0:8, 1, 0:T], ACT.Copy).then_inc(evac, 1)

        @block.vector
        def _(dve):
            dve.wait_ge(summed, KD)
            v.done(nc.vector.tensor_scalar(rstd[:, :], ps[:, 7, 0:T], 1.0 / D, RMS_EPS, ALU.mult, ALU.add), "var")
            dve.wait_ge(v.sem, v.at("var"))
            dve.wait_ge(rooted, 1)
            v.done(nc.vector.reciprocal(rstd[:, :], rstd[:, :]), "rstd")
            dve.wait_ge(v.sem, v.at("rstd"))
            dve.wait_ge(loaded, 16)
            for n in range(4):
                dve.wait_ge(x_in[n], 16)
            for k in range(KD):
                v.done(nc.vector.scalar_tensor_tensor(out=low(k), in0=mrg[:, k, :], scalar=par("g_mix", k),
                                                      in1=rstd[:, :], op0=ALU.mult, op1=ALU.mult), f"xn{k}")

            def rest(n, i):
                dve.wait_ge(w_high, i * 8 + n + 1)
                nc.vector.tensor_tensor(w_rest(n), weights(n), high[:, n % 2, :, :], ALU.subtract).then_inc(w_low, 1)
            with dve.Fori(0, ITER) as i:
                for n in range(8):
                    rest(n, i)
            for n in range(2):
                rest(n, ITER)
            dve.wait_ge(tile_done, TILES)
            nc.vector.tensor_tensor(xn[:, 0:KH, :], x_h[:, 0:KH, :], x_l[:, 0:KH, :], ALU.add)

        @block.gpsimd
        def _(pool):
            nc.gpsimd.memset(one[:, :], 1.0).then_inc(one_set, 1)
            nc.gpsimd.memset(rwx[:, :, 0:1], 0.0)
            nc.gpsimd.memset(poolx[:, :, 0:BUF], 0.0)
            for k in range(KD):
                pool.wait_ge(x_high, k + 1)
                nc.gpsimd.tensor_tensor(x_l[:, k, :], low(k), x_h[:, k, :], ALU.subtract).then_inc(x_rest, 1)
            pool.wait_ge(past, 16)
            nc.gpsimd.tensor_copy(rwx[:, :, XW - 5 * NB:XW:5], past_in[:, 0:RWT * NB].rearrange("p (t b) -> p t b", b=NB))
            for j in range(KH):
                n = RWT * NB + j * NB * BUF
                ins = nc.gpsimd.tensor_copy(poolx[:, j, PS0:PW].rearrange("p (b r) -> p b r", b=NB)[:, :, 0:BUF],
                                            past_in[:, n:n + NB * BUF].rearrange("p (b r) -> p b r", b=NB))
            ins.then_inc(carried, 1)
            pool.wait_ge(tile_done, TILES)
            nc.gpsimd.tensor_tensor(xn[:, KH:KD, :], x_h[:, KH:KD, :], x_l[:, KH:KD, :], ALU.add)

        @block.tensor
        def _(pe):
            mm = nc.tensor.matmul
            pe.wait_ge(one_set, 1)
            for k in range(KD):
                pe.wait_ge(squared, k + 1)
                mm(ps[:, 7, 0:T], one[:, :], sq[:, k % 2, :], start=(k == 0), stop=(k == KD - 1)).then_inc(summed, 1)

            def tile(n, i):
                pe.wait_ge(w_high, i * 8 + n + 1)
                if not (isinstance(i, int) and i == 0):
                    pe.wait_ge(evac, i * 8 - 8 + n + 1)
                for k in range(KD):
                    if isinstance(i, int) and i == n == 0:
                        pe.wait_ge(x_high, k + 1)
                        pe.wait_ge(x_rest, k + 1)
                    mm(ps[:, n, 0:T], high[:, n % 2, k, :], x_h[:, k, :], start=(k == 0), stop=False)
                    ins = mm(ps[:, n, 0:T], high[:, n % 2, k, :], x_l[:, k, :], start=False, stop=False)
                ins.then_inc(high_used, 1)
                pe.wait_ge(w_low, i * 8 + n + 1)
                for k in range(KD):
                    ins = mm(ps[:, n, 0:T], w_rest(n)[:, k, :], x_h[:, k, :], start=False,
                             stop=(k == KD - 1))
                ins.then_inc(tile_done, 1)
            for n in range(8):
                tile(n, 0)
            with pe.Fori(1, ITER) as i:
                for n in range(8):
                    tile(n, i)
            for n in range(2):
                tile(n, ITER)


def stage_mlstm(nc, ctx0, A, O, env):
    ring, xn, mrg, ps, const, param, K, par, rwx, mlu, poolx, gif, o_ml, o_pool = (
        env[k] for k in "ring xn mrg ps const param K par rwx mlu poolx gif o_ml o_pool".split())
    with ExitStack() as ctx:
        sem = lambda n: ctx.enter_context(nc.semaphore(n))
        H = range(MLH)
        cst = ring[:, 0, :].rearrange("p (h b e) -> p h b e", h=2, b=NB)
        vt = ring[:, 1, 0:3072].rearrange("p (c n) -> p c n", c=3)
        kt = ring[:, 1, 3072:3456].rearrange("p (c n) -> p c n", c=3)
        expo = ring[:, 2, 0:416]
        wts = ring[:, 2, 416:832]
        sq = ring[:, 2, 832:1408].rearrange("p (k t) -> p k t", k=2)
        dn = ring[:, 2, 1408:1696]
        qw = ring[:, 2, 1696:1728]
        qn = ring[:, 2, 1728:1760]
        wp = ring[:, 2, 1760:1792]
        win = [ring[:, 2, 1792 + 846 * i:2638 + 846 * i].rearrange("p (k t) -> p k t", k=2) for i in range(2)]
        vx = ring[0:NSM, 3, 0:2048].rearrange("p (b e) -> p b e", b=NB)
        pw = ring[:, 3, 2048:4096].rearrange("p (g k n) -> p g k n", g=4, k=2)
        row = lambda j: mrg[0:4, j, :]
        ig, fx, ln, lf, bcum, g, M, m, emt = (row(j) for j in range(9))
        wprev, ws = ln, fx
        seq = lambda a: a[:, NPR:T].rearrange("p (b l) -> p b l", l=NL)
        cp = [mrg[:, 9 + i, 0:DV] for i in range(2)]
        gt = mrg[:, 11, 0:24]
        nout = mrg[:, 11, 24:60].rearrange("p (h b) -> p h b", h=MLH)
        small = mrg[:, 11, 60:102]
        n_in = small[:, 0:32].rearrange("p (h b) -> p h b", h=MLH)
        b_i, b_f, m_prev = small[0:4, 32:33], small[0:4, 33:34], small[0:4, 34:42]
        pout = mrg[:, 12:16, :].rearrange("p k t -> p (k t)")[:, 0:KH * 9 * BUF]
        pout = pout.rearrange("p (k b r) -> p k b r", k=KH, b=9)
        sout = ctx.enter_context(nc.sbuf_tensor("sout", [P, RWT, 9], F32))

        loaded, pool_w = sem("m_loaded"), sem("m_poolw")
        c_in = [sem(f"m_c{i}") for i in range(2)]
        c_out = [sem(f"m_co{i}") for i in range(2)]
        cp_out = [sem(f"m_cpo{i}") for i in range(2)]
        stored = sem("m_stored")
        scanned = sem("m_inner")
        pe_steps = ["fg"] + [f"vt{c}{e}" for c in range(3) for e in range(2)] + ["gt"]
        for h in H:
            pe_steps += [f"s{h}", f"b{h}", f"k{h}", f"n{h}", f"u{h}"] + [f"d{h}{j}" for j in range(4)] + [f"pool{h}"]
        q = Steps(ctx, nc, "m_pe", pe_steps + [f"q{h}" for h in H])
        dve_steps = ["fx", "ig", "mn", "lf", "bcum", "g", "gmax", "M", "m", "wd", "wl", "sout"]
        for h in H:
            dve_steps += [f"x{h}", f"qw{h}", f"qn{h}", f"w{h}", f"wm{h}", f"k{h}", f"max{h}", f"rec{h}", f"h{h}", f"n{h}"]
            dve_steps += [f"c{h}{j}" for j in range(4)]
        dve_steps += [f"v{h}" for h in H] + ["rs"] + [f"y{k}" for k in range(KH)] + [f"o{k}" for k in range(KH)]
        v = Steps(ctx, nc, "m_dve", dve_steps)
        act_steps = ["sig", "abs", "exp", "ln"] + [f"vt{c}{e}" for c in range(3) for e in range(2)] + ["emt", "wprev", "ws", "gt"]
        for h in H:
            act_steps += [f"wp{h}", f"e{h}", f"abs{h}", f"cp{h}", f"pool{h}"]
        a = Steps(ctx, nc, "m_act", act_steps + [f"sq{h}" for h in H] + ["root"])
        pool_steps = []
        for h in H:
            pool_steps += [f"add{h}{i}" for i in range(h + 1)] + [f"mean{h}", f"first{h}", f"d{h}"]
            if h == 0:
                pool_steps += ["pout"]
            pool_steps += [f"vx{h}"]
        g_ = Steps(ctx, nc, "m_pool", pool_steps)
        def store(sp, h):
            sp.wait_ge(a.sem, a.at(f"cp{h}"))
            sp.dma_start(O["ml_cp"][h, :, :], cp[h % 2]).then_inc(cp_out[h % 2], 16)
            sp.wait_ge(v.sem, v.at(f"c{h}3"))
            sp.dma_start(O["ml_cs"][h, :, :, :], cst[:, h % 2, :, :]).then_inc(c_out[h % 2], 16)

        block = ctx.enter_context(nc.Block())

        @block.sync
        def _(sp):
            sp.dma_start(small, A["ml_small"][:, :]).then_inc(loaded, 16)
            sp.dma_start(pw, A["pool_w"][:, :, :, :]).then_inc(pool_w, 16)
            for h in H:
                if h >= 2:
                    sp.wait_ge(c_out[h % 2], 16)
                sp.dma_start(cst[:, h % 2, :, :], A["c_in"][h, :, :, :]).then_inc(c_in[h % 2], 16)
                if h >= 1:
                    store(sp, h - 1)
            store(sp, MLH - 1)
            sp.wait_ge(v.sem, v.at(f"n{MLH - 1}"))
            sp.dma_start(O["ml_n"][:, :, :], nout).then_inc(stored, 16)
            sp.dma_start(O["ml_m"][:, :], m).then_inc(stored, 16)
            sp.dma_start(O["shift"][:, :, :], sout[:, :, :]).then_inc(stored, 16)
            sp.wait_ge(g_.sem, g_.at("pout"))
            sp.dma_start(O["pool"][:, :, :, :], pout).then_inc(stored, 16)
            sp.wait_ge(stored, 64)
            for i in range(2):
                sp.wait_ge(c_out[i], 32)
                sp.wait_ge(cp_out[i], 32)

        @block.tensor
        def _(pe):
            mm, ident = nc.tensor.matmul, K("ident")
            q.done(mm(ps[0:4, 0, 0:T], const[0:8, CONST_AT["ident"][0] + 4:CONST_AT["ident"][0] + 8], gif[:, :],
                      start=True, stop=True), "fg")
            for c in range(3):
                n = P if c < 2 else NSM
                for e in range(2):
                    b = 1 + 2 * c + e
                    for j in range(4):
                        ins = nc.tensor.transpose(ps[0:n, b, j * P:(j + 1) * P],
                                                  mlu[:, 8 + 4 * e + j, c * P:c * P + n], ident)
                    q.done(ins, f"vt{c}{e}")
            pe.wait_ge(a.sem, a.at("ws"))
            for c in range(3):
                n = P if c < 2 else NSM
                for i, r in enumerate((g, ws)):
                    ins = nc.tensor.transpose(ps[0:n, 7, c * 8 + 4 * i:c * 8 + 4 * i + 4], r[:, c * P:c * P + n],
                                              K("ident", 4, 0, 4))
            q.done(ins, "gt")
            pe.wait_ge(a.sem, a.at("vt21"))
            pe.wait_ge(loaded, 16)
            for h in H:
                qh, kh = mlu[:, h, :], mlu[:, 4 + h, :]
                if h:
                    pe.wait_ge(v.sem, v.at(f"w{h - 1}"))
                    pe.wait_ge(v.sem, v.at(f"c{h - 1}3"))
                else:
                    pe.wait_ge(v.sem, v.at("fx"))
                mm(ps[:, 0, 0:NPR], kh[:, 0:P], qh[:, 0:NPR], start=True, stop=True)
                mm(ps[:, 0, NPR:NPR + P], kh[:, P:NPR], qh[:, P:NPR], start=True, stop=True)
                q.done(mm(ps[0:NSM, 0, 384:416], kh[:, NPR:T], qh[:, NPR:T], start=True, stop=True), f"s{h}")
                sel = const[0:4, CONST_AT["head_row"][0] + h * P:CONST_AT["head_row"][0] + (h + 1) * P]
                if h:
                    pe.wait_ge(v.sem, v.at(f"max{h - 1}"))
                mm(ps[:, 1, 0:T], sel, M, start=True, stop=True)
                mm(ps[:, 3, 0:T], sel, emt, start=True, stop=True)
                q.done(mm(ps[:, 3, T:T + NSM], sel, wprev[:, NPR:T], start=True, stop=True), f"b{h}")
                if h == 0:
                    pe.wait_ge(a.sem, a.at("vt21"))
                for c in range(3):
                    n = P if c < 2 else NSM
                    ins = nc.tensor.transpose(ps[0:n, 6, c * P:(c + 1) * P], kh[:, c * P:c * P + n], ident)
                q.done(ins, f"k{h}")
                pe.wait_ge(v.sem, v.at(f"wm{h}"))
                pe.wait_ge(v.sem, v.at(f"qn{h}"))
                w0, w1, wsm = wts[:, 0:NPR], wts[:, NPR:384], wts[0:NSM, 384:416]
                one = K("ones")
                mm(ps[:, 2, 0:NPR], one, w0, start=True, stop=False)
                mm(ps[:, 2, P:NPR], one, w1, start=False, stop=False)
                mm(ps[:, 2, NPR:T], K("ones", NSM), wsm, start=False, stop=False)
                mm(ps[:, 2, NPR:T], one, qn, start=False, stop=True)
                pe.wait_ge(c_in[h % 2], 16 * (h // 2 + 1))
                for e in range(2):
                    f = h * DV + e * P
                    o = ps[:, 4 + e, :]
                    mm(o[:, 0:NPR], vt[:, 0, f:f + P], w0, start=True, stop=False)
                    mm(o[:, P:NPR], vt[:, 1, f:f + P], w1, start=False, stop=False)
                    mm(o[:, NPR:T], vt[0:NSM, 2, f:f + P], wsm, start=False, stop=False)
                    for b in range(NB):
                        ins = mm(o[:, NPR + NL * b:NPR + NL * b + NL], cst[:, h % 2, b, e * P:(e + 1) * P],
                                 qw[:, NL * b:NL * b + NL], start=False, stop=(b == NB - 1))
                q.done(ins, f"n{h}")
                pe.wait_ge(v.sem, v.at(f"k{h}"))
                if h:
                    pe.wait_ge(v.sem, v.at(f"c{h - 1}3"))
                else:
                    pe.wait_ge(a.sem, a.at("gt"))
                for o, r0, r1 in ((ps[:, 7, 0:DV], vt[:, 0, h * DV:(h + 1) * DV], vt[:, 1, h * DV:(h + 1) * DV]),
                                  (ps[:, 7, DV:DV + 1], K("ones")[:, 0:1], K("ones")[:, 0:1])):
                    mm(o, kt[:, 0, :], r0, start=True, stop=False)
                    mm(o, kt[:, 1, :], r1, start=False, stop=True)
                q.done(mm(ps[:, 7, DV + 1:DV + 1 + NB], kt[0:NSM, 2, :], K("of_seq", NSM), start=True, stop=True), f"u{h}")
                pe.wait_ge(g_.sem, g_.at(f"vx{h}"))
                for j in range(4):
                    if j == 0:
                        pe.wait_ge(v.sem, v.at(f"n{h}"))
                        pe.wait_ge(a.sem, a.at(f"cp{h}"))
                    if j == 1:
                        pe.wait_ge(v.sem, v.at(f"x{h}"))
                    if j >= 2:
                        pe.wait_ge(v.sem, v.at(f"c{h}{j - 2}"))
                    q.done(mm(ps[:, 7 if j % 2 == 0 else 1, :], kt[0:NSM, 2, :], vx[:, 2 * j:2 * j + 2, :], start=True, stop=True),
                           f"d{h}{j}")
                pe.wait_ge(pool_w, 16)
                pe.wait_ge(g_.sem, g_.at(f"d{h}"))
                pe.wait_ge(v.sem, v.at(f"h{h}"))
                for e in range(2):
                    for k in range(2):
                        ins = mm(ps[:, 4 + e, 0:T], pw[:, h, k, e * P:(e + 1) * P], o_pool[:, 2 * h + k, :],
                                 start=(k == 0), stop=(k == 1))
                q.done(ins, f"pool{h}")
                pe.wait_ge(a.sem, a.at(f"pool{h}"))
            for h in H:
                pe.wait_ge(a.sem, a.at(f"sq{h}"))
                if h == 0:
                    pe.wait_ge(v.sem, v.at(f"c{MLH - 1}3"))
                for e in range(2):
                    ins = mm(ps[:, h, 0:T], K("ones_dv"), sq[:, e, :], start=(e == 0), stop=(e == 1))
                q.done(ins, f"q{h}")

        @block.scalar
        def _(act):
            fn = nc.scalar.activation
            a.done(fn(mlu[:, 16:24, :], mlu[:, 16:24, :], ACT.Sigmoid), "sig")
            act.wait_ge(v.sem, v.at("fx"))
            a.done(fn(ln, fx, ACT.Abs), "abs")
            act.wait_ge(a.sem, a.at("abs"))
            a.done(fn(ln, ln, ACT.Exp, scale=-1.0), "exp")
            act.wait_ge(a.sem, a.at("exp"))
            a.done(fn(ln, ln, ACT.Ln, bias=1.0), "ln")
            for c in range(3):
                n = P if c < 2 else NSM
                for e in range(2):
                    act.wait_ge(q.sem, q.at(f"vt{c}{e}"))
                    a.done(fn(vt[0:n, c, e * 512:(e + 1) * 512], ps[0:n, 1 + 2 * c + e, :], ACT.Copy), f"vt{c}{e}")
            act.wait_ge(v.sem, v.at("m"))
            a.done(fn(emt, m, ACT.Exp, scale=-1.0), "emt")
            act.wait_ge(v.sem, v.at("wd"))
            a.done(fn(wprev[:, NPR:T], wprev[:, NPR:T], ACT.Exp), "wprev")
            act.wait_ge(v.sem, v.at("wl"))
            a.done(fn(ws, ws, ACT.Exp), "ws")
            act.wait_ge(q.sem, q.at("gt"))
            fn(gt[:, 0:16], ps[:, 7, 0:16], ACT.Copy)
            a.done(fn(gt[0:NSM, 16:24], ps[0:NSM, 7, 16:24], ACT.Copy), "gt")
            for h in H:
                act.wait_ge(q.sem, q.at(f"b{h}"))
                if h:
                    act.wait_ge(v.sem, v.at(f"c{h - 1}3"))
                a.done(fn(wp, ps[:, 3, T:T + NSM], ACT.Copy), f"wp{h}")
                act.wait_ge(v.sem, v.at(f"x{h}"))
                fn(expo[:, 0:384], expo[:, 0:384], ACT.Exp, scale=-1.0)
                a.done(fn(expo[0:NSM, 384:416], expo[0:NSM, 384:416], ACT.Exp, scale=-1.0), f"e{h}")
                act.wait_ge(q.sem, q.at(f"n{h}"))
                a.done(fn(dn, ps[:, 2, 0:T], ACT.Abs), f"abs{h}")
                act.wait_ge(q.sem, q.at(f"u{h}"))
                if h >= 2:
                    act.wait_ge(cp_out[h % 2], 16)
                a.done(fn(cp[h % 2], ps[:, 7, 0:DV], ACT.Copy), f"cp{h}")
                act.wait_ge(q.sem, q.at(f"pool{h}"))
                for e in range(2):
                    ins = fn(o_pool[:, 2 * h + e, :], ps[:, 4 + e, 0:T], ACT.Copy, scale=par("pool_scale", 2 * h + e))
                a.done(ins, f"pool{h}")
            for h in H:
                if h:
                    act.wait_ge(q.sem, q.at(f"q{h - 1}"))
                act.wait_ge(v.sem, v.at(f"h{h}"))
                a.done(fn(sq, o_ml[:, 2 * h:2 * h + 2, :], ACT.Square), f"sq{h}")
            act.wait_ge(v.sem, v.at("v3"))
            a.done(fn(mrg[:, 0:4, :], mrg[:, 0:4, :], ACT.Sqrt), "root")

        @block.vector
        def _(dve):
            ts, tt, stt = nc.vector.tensor_scalar, nc.vector.tensor_tensor, nc.vector.scalar_tensor_tensor
            dve.wait_ge(loaded, 16)
            dve.wait_ge(q.sem, q.at("fg"))
            v.done(ts(fx, ps[0:4, 0, 0:T], b_f, None, ALU.add), "fx")
            v.done(ts(ig, gif[0:4, :], b_i, None, ALU.add), "ig")
            dve.wait_ge(v.sem, v.at("fx"))
            v.done(ts(lf, fx, 0.0, None, ALU.min), "mn")
            dve.wait_ge(v.sem, v.at("mn"))
            dve.wait_ge(a.sem, a.at("ln"))
            v.done(tt(lf, lf, ln, ALU.subtract), "lf")
            dve.wait_ge(v.sem, v.at("lf"))
            v.done(nc.vector.tensor_tensor_scan(bcum, K("run_ml", 4), lf, 0.0, ALU.mult, ALU.add), "bcum")
            dve.wait_ge(v.sem, v.at("bcum"))
            v.done(tt(g, ig, bcum, ALU.subtract), "g")
            dve.wait_ge(v.sem, v.at("g"))
            nc.vector.tensor_copy(M[:, 1:T], g[:, 1:T])
            ts(M[:, 0:1], g[:, 0:1], 0.0, None, ALU.max)
            v.done(tt(emt[:, 0:NB], seq(g)[:, :, 0], m_prev, ALU.max), "gmax")
            dve.wait_ge(v.sem, v.at("gmax"))
            v.done(nc.vector.tensor_copy(seq(M)[:, :, 0], emt[:, 0:NB]), "M")
            raise_ = v.at("M")
            dve.wait_ge(v.sem, raise_)
            nc.vector.tensor_tensor_scan(M, K("restart", 4), M, 0.0, ALU.add, ALU.max).then_inc(scanned, 1)
            dve.wait_ge(scanned, 1)
            v.done(tt(m, bcum, M, ALU.add), "m")
            v.done(tt(seq(wprev), m_prev.unsqueeze(2).to_broadcast([4, NB, NL]), seq(M), ALU.subtract), "wd")
            ts(ws[:, 0:NPR], g[:, 0:NPR], M[:, NPR - 1:NPR], None, ALU.subtract)
            v.done(tt(seq(ws), seq(g), seq(M)[:, :, NL - 1:NL].to_broadcast([4, NB, NL]), ALU.subtract), "wl")
            v.done(nc.vector.tensor_copy(sout[:, :, :], rwx[:, :, NPR:XW:5]), "sout")
            dve.wait_ge(a.sem, a.at("gt"))
            for h in H:
                dve.wait_ge(q.sem, q.at(f"b{h}"))
                gp = lambda c, n=P: gt[0:n, 8 * c + h:8 * c + h + 1]
                wsp = lambda c, n=P: gt[0:n, 8 * c + 4 + h:8 * c + 5 + h]
                ts(expo[:, 0:NPR], ps[:, 1, 0:NPR], gp(0), 0.0, ALU.subtract, ALU.max)
                ts(expo[:, NPR:384], ps[:, 1, P:NPR], gp(1), 0.0, ALU.subtract, ALU.max)
                v.done(ts(expo[0:NSM, 384:416], ps[0:NSM, 1, NPR:T], gp(2, NSM), 0.0, ALU.subtract, ALU.max), f"x{h}")
                dve.wait_ge(a.sem, a.at(f"wp{h}"))
                v.done(tt(qw, mlu[:, h, NPR:T], wp, ALU.mult), f"qw{h}")
                dve.wait_ge(v.sem, v.at(f"qw{h}"))
                v.done(tt(qn.rearrange("p (b l) -> p b l", l=NL), qw.rearrange("p (b l) -> p b l", l=NL),
                          n_in[:, h, :].unsqueeze(2).to_broadcast([P, NB, NL]), ALU.mult), f"qn{h}")
                dve.wait_ge(a.sem, a.at(f"e{h}"))
                dve.wait_ge(q.sem, q.at(f"s{h}"))
                tt(wts[:, 0:384], ps[:, 0, 0:384], expo[:, 0:384], ALU.mult)
                v.done(tt(wts[0:NSM, 384:416], ps[0:NSM, 0, 384:416], expo[0:NSM, 384:416], ALU.mult), f"w{h}")
                dve.wait_ge(v.sem, v.at(f"w{h}"))
                for c in range(2):
                    tt(wts[:, c * NPR:c * NPR + P], wts[:, c * NPR:c * NPR + P], K("lt_le")[:, P:2 * P], ALU.mult)
                v.done(tt(wts[0:NSM, 384:416], wts[0:NSM, 384:416], K("seq_lt_le", NSM)[:, NSM:2 * NSM], ALU.mult), f"wm{h}")
                dve.wait_ge(q.sem, q.at(f"k{h}"))
                if h:
                    dve.wait_ge(q.sem, q.at(f"d{h - 1}3"))
                ts(kt[:, 0, :], ps[:, 6, 0:P], wsp(0), None, ALU.mult)
                ts(kt[:, 1, :], ps[:, 6, P:2 * P], wsp(1), None, ALU.mult)
                v.done(ts(kt[0:NSM, 2, :], ps[0:NSM, 6, 2 * P:3 * P], wsp(2, NSM), None, ALU.mult), f"k{h}")
                dve.wait_ge(a.sem, a.at(f"abs{h}"))
                v.done(tt(dn, dn, ps[:, 3, 0:T], ALU.max), f"max{h}")
                dve.wait_ge(v.sem, v.at(f"max{h}"))
                v.done(nc.vector.reciprocal(dn, dn), f"rec{h}")
                dve.wait_ge(v.sem, v.at(f"rec{h}"))
                tt(o_ml[:, 2 * h, :], ps[:, 4, 0:T], dn, ALU.mult)
                v.done(tt(o_ml[:, 2 * h + 1, :], ps[:, 5, 0:T], dn, ALU.mult), f"h{h}")
                dve.wait_ge(a.sem, a.at(f"cp{h}"))
                nc.vector.tensor_copy(nout[:, h, 0:1], ps[:, 7, DV:DV + 1])
                tt(nout[:, h, 1:9], n_in[:, h, :], wp.rearrange("p (b l) -> p b l", l=NL)[:, :, NL - 1], ALU.mult).then_inc(scanned, 1)
                dve.wait_ge(scanned, 2 + h)
                v.done(tt(nout[:, h, 1:9], nout[:, h, 1:9], ps[:, 7, DV + 1:DV + 1 + NB], ALU.add), f"n{h}")
                for j in range(4):
                    dve.wait_ge(q.sem, q.at(f"d{h}{j}"))
                    for i in range(2):
                        b = 2 * j + i
                        ins = stt(out=cst[:, h % 2, b, :], in0=cst[:, h % 2, b, :], scalar=wp[:, NL * b + NL - 1:NL * b + NL],
                                  in1=ps[:, 7 if j % 2 == 0 else 1, i * DV:(i + 1) * DV], op0=ALU.mult, op1=ALU.add)
                    v.done(ins, f"c{h}{j}")
            for h in H:
                dve.wait_ge(q.sem, q.at(f"q{h}"))
                v.done(ts(mrg[:, h, :], ps[:, h, 0:T], RMS_EPS, None, ALU.add), f"v{h}")
            dve.wait_ge(a.sem, a.at("root"))
            v.done(nc.vector.reciprocal(mrg[:, 0:4, :], mrg[:, 0:4, :]), "rs")
            dve.wait_ge(v.sem, v.at("rs"))
            for k in range(KH):
                v.done(stt(out=o_ml[:, k, :], in0=o_ml[:, k, :], scalar=par("ml_gn", k), in1=mrg[:, k // 2, :],
                           op0=ALU.mult, op1=ALU.mult), f"y{k}")
            for k in range(KH):
                dve.wait_ge(v.sem, v.at(f"y{k}"))
                v.done(tt(o_ml[:, k, :], o_ml[:, k, :], mlu[:, 16 + k, :], ALU.mult), f"o{k}")

        @block.gpsimd
        def _(pool):
            tt, ts = nc.gpsimd.tensor_tensor, nc.gpsimd.tensor_scalar
            for h in H:
                src, n = poolx[:, 2 * h:2 * h + 2, :], PW
                for i in range(h + 1):
                    o, s = win[i % 2], 1 << i
                    if i:
                        pool.wait_ge(g_.sem, g_.at(f"add{h}{i - 1}"))
                    elif h:
                        pool.wait_ge(g_.sem, g_.at(f"d{h - 1}"))
                    lo = (2 << i) - 1
                    g_.done(tt(o[:, :, lo:PW], src[:, :, lo:PW], src[:, :, lo - s:PW - s], ALU.add), f"add{h}{i}")
                    src = o
                pool.wait_ge(g_.sem, g_.at(f"add{h}{h}"))
                w = WINDOWS[h]
                d = o_pool[:, 2 * h:2 * h + 2, :]
                ts(d[:, :, 0:NPR], src[:, :, BUF:PS0], 1.0 / w, None, ALU.mult)
                for k in range(2):
                    ins = ts(d[:, k, NPR:T].rearrange("p (b l) -> p b l", b=NB),
                             src[:, k, PS0:PW].rearrange("p (b r) -> p b r", b=NB)[:, :, BUF:BUF + NL], 1.0 / w, None, ALU.mult)
                g_.done(ins, f"mean{h}")
                pool.wait_ge(g_.sem, g_.at(f"mean{h}"))
                inv = K("inv_count")[:, 16 * h:16 * h + 16]
                g_.done(tt(d[:, :, 0:16], src[:, :, BUF:BUF + 16], inv.unsqueeze(1).to_broadcast([P, 2, 16]), ALU.mult), f"first{h}")
                pool.wait_ge(g_.sem, g_.at(f"first{h}"))
                x = poolx[:, 2 * h:2 * h + 2, :]
                tt(d[:, :, 0:NPR], d[:, :, 0:NPR], x[:, :, BUF:PS0], ALU.subtract)
                for k in range(2):
                    dd = d[:, k, NPR:T].rearrange("p (b l) -> p b l", b=NB)
                    ins = tt(dd, dd, x[:, k, PS0:PW].rearrange("p (b r) -> p b r", b=NB)[:, :, BUF:BUF + NL], ALU.subtract)
                g_.done(ins, f"d{h}")
                if h == 0:
                    for k in range(KH):
                        nc.gpsimd.tensor_copy(pout[:, k, 0, :], poolx[:, k, PS0 - BUF:PS0])
                        ins = nc.gpsimd.tensor_copy(pout[:, k, 1:9, :], poolx[:, k, PS0:PW].rearrange(
                            "p (b r) -> p b r", b=NB)[:, :, NL:NL + BUF])
                    g_.done(ins, "pout")
                pool.wait_ge(a.sem, a.at("vt21"))
                if h:
                    pool.wait_ge(q.sem, q.at(f"d{h - 1}3"))
                g_.done(tt(vx, vt[0:NSM, 2, h * DV:(h + 1) * DV].unsqueeze(1).to_broadcast([NSM, NB, DV]),
                           K("of_seq", NSM).unsqueeze(2).to_broadcast([NSM, NB, DV]), ALU.mult), f"vx{h}")


def stage_rwkv(nc, ctx0, A, O, env):
    ring, xn, mrg, ps, const, param, K, par, rwx, o_ml, o_pool = (
        env[k] for k in "ring xn mrg ps const param K par rwx o_ml o_pool".split())
    with ExitStack() as ctx:
        sem = lambda n: ctx.enter_context(nc.semaphore(n))
        sb = lambda n, s: ctx.enter_context(nc.sbuf_tensor(n, s, F32))
        H = range(2)
        f = sb("f", [P, 11, T])
        r, k, v_, kk, sg, csm, a_, er, ek, ekap, rkk = (f[:, j, :] for j in range(11))
        kr, kb = sb("kr", [P, 2, T]), sb("kb", [P, 2, T])
        dx = sb("dx", [P, XW])
        lora = sb("lora", [P, T])
        wa = sb("wa", [P, P])
        tok = sb("tok", [P, 3, 3 * P])
        xm = sb("xm", [P, 2, 4, P])
        rhs = sb("rhs", [P, 3, P])
        nsa = sb("nsa", [P, 3, P])
        sk = sb("sk", [NSM, 2, 2, 2, NSM])
        su, st_, sz = (sb(n, [NSM, 2, NSM]) for n in ("su", "st_", "sz"))
        sxm = sb("sxm", [NSM, 2, 2, NSM])
        sts = sb("sts", [P, NB, 64])
        vx, nx = sb("vx", [NSM, NB, P]), sb("nx", [NSM, NB, P])
        s0t = sb("s0t", [64, 2, 64])
        cen, ec, st0, st1 = sb("cen", [P, 2]), sb("ec", [P, 2]), sb("st0", [P, 64]), sb("st1", [P, 64])
        gtmp = sb("gtmp", [P, T])
        half = sb("half", [P, 2 * KH])
        kkm = ring[:, 3, 0:1024].rearrange("p (h c x t) -> p h c x t", h=2, c=2, x=2)
        bbm = ring[:, 3, 1024:2048].rearrange("p (h c x t) -> p h c x t", h=2, c=2, x=2)
        um = ring[:, 3, 2048:2560].rearrange("p (j t) -> p j t", j=4)
        tm = ring[:, 3, 2560:3072].rearrange("p (j t) -> p j t", j=4)
        zm = ring[:, 3, 3072:3584].rearrange("p (j t) -> p j t", j=4)
        gate = ring[:, 3, 3584:3584 + T]
        wtmp = zm.rearrange("p j t -> p (j t)")[0:64, :]
        seq = lambda x: x[:, NPR:T].rearrange("p (b l) -> p b l", l=NL)

        mixed = sem("w_mixed")
        slots = [sem(f"w_slot{s}") for s in range(3)]
        wa_in, st_in, st_out, stp_out = sem("w_wa"), sem("w_stin"), sem("w_stout"), sem("w_stp")
        LV = range(len(LEVELS))
        pe_steps = ["G00", "z", "a", "ss", "U00", "G01", "U01", "tr0", "tr1", "tr2"]
        pe_steps += [f"bk{x}{h}" for x in H for h in H] + ["sk0", "sk1", "w0", "w1"]
        fill_after = {1: "G10", 2: "U10", 4: "G11"}
        for l in LV:
            pe_steps += [f"z{l}"] + ([] if l == 0 else [f"t{l}", f"u{l}"] if l < 6 else [f"u{l}"])
            if l in fill_after:
                pe_steps += [fill_after[l]]
            if l < 2:
                pe_steps += [f"sz{l}"] + ([f"su{l}"] if l else [])
        pe_steps += ["g0", "gs", "sa0", "sas", "y0", "ys", "s0", "g1", "sa1", "U11", "y1", "s1", "ds", "mean", "bonus", "var"]
        q = Steps(ctx, nc, "w_pe", pe_steps)
        dve_steps = ["dx_k", "us_k", "kkr", "dx_r", "us_r", "dx_v", "us_v", "sg", "a", "cs", "cen", "csc", "csm", "ssm",
                     "rec", "kk", "m00", "kap", "rt", "b", "bt", "ka", "kp", "kt", "rkk", "m01"]
        dve_steps += [f"bk{x}{h}" for x in H for h in H] + ["sk0", "sk1", "wm0", "w0", "wm1", "w1"]
        for l in LV:
            dve_steps += ([f"u{l}", f"t{l}"] if l == 0 else [f"t{l}", f"u{l}"] if l < 6 else [f"u{l}"])
            if l < 2:
                dve_steps += ["su0", "st0"] if l == 0 else ["su1"]
            if l == 3:
                dve_steps += ["m10"]
        dve_steps += ["s0", "s1a", "s1", "ds", "dsp", "m11", "ysum", "d", "ve", "grec", "y", "bon", "o"]
        v = Steps(ctx, nc, "w_dve", dve_steps)
        act_steps = ["tz", "ta", "kksq", "root", "G00", "ek", "er", "ekap", "ec", "G01", "tr0", "tr1", "tr2"]
        for l in LV:
            act_steps += ([f"z{l}"] if l else []) + (["sz1"] if l == 1 else [])
            if l in (1, 4):
                act_steps += [fill_after[l]]
        act_steps += ["g0", "gs", "sa0", "sas", "g1", "sa1", "ys", "sq", "groot"]
        a = Steps(ctx, nc, "w_act", act_steps)
        pool_steps = []
        for l in LV:
            pool_steps += [f"x{l}"] + ([f"sx{l}"] if l < 2 else []) + (["vx"] if l == 2 else []) + (["m0"] if l == 3 else [])
        g_ = Steps(ctx, nc, "w_pool", pool_steps + ["nx", "m1"])
        for s_ in (q, v, a, g_):
            s_.lap = 1
        dxd = sem("w_dx")
        carrier = sem("w_carrier")
        block = ctx.enter_context(nc.Block())
        N = KH

        def settled(eng):
            eng.sem_inc(carrier, 1)

        def tile(t, i):
            return t[bass.ds(i, 1), :, :].rearrange("o p n -> (o p) n")

        @block.sync
        def _(sp):
            def load_weights(i, j):
                if j is not None:
                    sp.wait_ge(q.sem, q.at("G11", j))
                    settled(sp)
                for b in H:
                    sp.dma_start(ring[:, b, :], tile(A["w_gate"][b + 1], i)).then_inc(slots[b], 16)
                if j is not None:
                    sp.wait_ge(q.sem, q.at("U11", j))
                    settled(sp)
                sp.dma_start(ring[:, 2, :], tile(A["w_up2"], i)).then_inc(slots[2], 16)

            def load_small(i):
                settled(sp)
                sp.dma_start(wa[:, :], tile(A["w_lora"], i)).then_inc(wa_in, 16)
                sp.dma_start(sts[:, :, :], A["rw_s"][bass.ds(i, 1), :, :, :].rearrange("o p b v -> (o p) b v")).then_inc(st_in, 16)

            def store(i):
                sp.wait_ge(v.sem, v.at("s1", i))
                settled(sp)
                sp.dma_start(tile(O["rw_p"], i), st1[:, :]).then_inc(stp_out, 16)
                sp.wait_ge(v.sem, v.at("dsp", i))
                settled(sp)
                sp.dma_start(O["rw_s"][bass.ds(i, 1), :, :, :].rearrange("o p b v -> (o p) b v"), sts[:, :, :]).then_inc(st_out, 16)
                sp.wait_ge(st_out, i * 16 + 16)
                sp.wait_ge(stp_out, i * 16 + 16)
            load_small(0)
            load_weights(0, None)
            with sp.Fori(0, N - 1) as i:
                load_weights(i + 1, i)
                store(i)
                load_small(i + 1)
            store(N - 1)

        @block.tensor
        def _(pe):
            mm, ident = nc.tensor.matmul, K("ident")
            pe.sem_inc(q.sem, q.n)
            w = [ring[:, s, :].rearrange("p (k n) -> p k n", k=KD) for s in range(3)]
            with pe.Fori(0, N) as i:
                def filler(name, lo, hi):
                    kind, d, b = name[0], int(name[1]), int(name[2])
                    n = KD if kind == "G" else KH
                    bank = 0 if kind == "G" else (1, 7)[b]
                    if lo == 0:
                        if kind == "G":
                            pe.wait_ge(slots[b], i * 16 + 16)
                            last = {"G00": ("G11", i - 1), "G01": ("G00", i), "G10": ("G01", i), "G11": ("G10", i)}[name]
                            pe.wait_ge(a.sem, a.at(*last))
                        else:
                            if d == 0 and b == 0:
                                pe.wait_ge(slots[2], i * 16 + 16)
                            pe.wait_ge(v.sem, v.at(f"m1{b}", i - 1) if d == 0 else v.at(f"m0{b}", i))
                    for t in range(lo, hi):
                        if kind == "G":
                            ins = mm(ps[:, 0, 0:T], w[b][:, t, d * P:(d + 1) * P], xn[:, t, :], start=(t == 0), stop=(t == n - 1))
                        else:
                            src = (o_ml, o_pool)[b]
                            ins = mm(ps[:, bank, 0:T], w[2][:, b * KH + t, d * P:(d + 1) * P], src[:, t, :],
                                     start=(t == 0), stop=(t == n - 1))
                    if hi == n:
                        q.done(ins, name)
                hs = lambda h: slice(64 * h, 64 * h + 64)
                filler("G00", 0, 16)
                pe.wait_ge(mixed, 2)
                pe.wait_ge(wa_in, i * 16 + 16)
                pe.wait_ge(v.sem, v.at("o", i - 1))
                q.done(mm(ps[:, 2, 0:T], wa[0:64, :], lora[0:64, :], start=True, stop=True), "z")
                q.done(mm(ps[:, 3, 0:T], wa[64:128, :], lora[64:128, :], start=True, stop=True), "a")
                pe.wait_ge(a.sem, a.at("kksq", i))
                q.done(mm(ps[:, 4, 0:T], K("heads"), ekap, start=True, stop=True), "ss")
                filler("U00", 0, 8)
                filler("G01", 0, 16)
                filler("U01", 0, 8)
                pe.wait_ge(v.sem, v.at("kt", i))
                for c in range(3):
                    n = P if c < 2 else NSM
                    for j, src in enumerate((v_, kb[:, 0, :], kb[:, 1, :])):
                        ins = nc.tensor.transpose(ps[0:n, (5, 6, 2)[c], j * P:(j + 1) * P], src[:, c * P:c * P + n], ident)
                    q.done(ins, f"tr{c}")
                for x in H:
                    for h in H:
                        b = 3 + 2 * x + h
                        if b == 5:
                            pe.wait_ge(a.sem, a.at("tr1", i))
                        for c in H:
                            ins = mm(ps[:, b, c * 256:(c + 1) * 256], kb[hs(h), x, c * P:(c + 1) * P],
                                     kr[hs(h), :, c * P:(c + 1) * P], start=True, stop=True)
                        q.done(ins, f"bk{x}{h}")
                for h in H:
                    if h == 0:
                        pe.wait_ge(a.sem, a.at("tr2", i))
                    else:
                        pe.wait_ge(v.sem, v.at("bk00", i))
                    settled(pe)
                    for x in H:
                        ins = mm(ps[0:NSM, 2 + h, x * 64:x * 64 + 64], kb[hs(h), x, NPR:T], kr[hs(h), :, NPR:T],
                                 start=True, stop=True)
                    q.done(ins, f"sk{h}")
                pe.wait_ge(st_in, i * 16 + 16)
                for h in H:
                    pe.wait_ge(v.sem, v.at(("bk01", "bk10")[h], i))
                    settled(pe)
                    for y in H:
                        ins = mm(ps[NSM * y:NSM * y + NSM, 4 + h, :], kr[hs(h), y, NPR:T], sts[hs(h), :, :], start=True, stop=True)
                    q.done(ins, f"w{h}")
                for l in LV:
                    pe.wait_ge(g_.sem, g_.at(f"x{l}", i))
                    pe.wait_ge(v.sem, v.at("bk11" if l == 0 else f"t{l - 1}", i))
                    if l:
                        pe.wait_ge(a.sem, a.at(f"z{l - 1}", i)) if l > 1 else None
                    for j in range(4):
                        ins = mm(ps[:, 6, j * P:(j + 1) * P], xm[:, l % 2, j, :], ident if l == 0 else tm[:, j, :],
                                 start=True, stop=True)
                    q.done(ins, f"z{l}")
                    if l == 0:
                        pe.wait_ge(v.sem, v.at("w0", i))
                        pe.wait_ge(g_.sem, g_.at("sx0", i))
                        settled(pe)
                        for h in H:
                            ins = mm(ps[0:NSM, 4, h * NSM:(h + 1) * NSM], sxm[:, 0, h, :], K("ident", NSM)[:, 0:NSM], start=True, stop=True)
                        q.done(ins, "sz0")
                        continue
                    name = fill_after.get(l)
                    full = 16 if name and name[0] == "G" else 8
                    if name:
                        filler(name, 0, full // 2)
                    pe.wait_ge(a.sem, a.at(f"z{l}", i))
                    pe.wait_ge(v.sem, v.at(f"u{l - 1}", i))
                    if l == 1:
                        pe.wait_ge(v.sem, v.at("sk1", i))
                    if l < 6:
                        for j in range(4):
                            ins = mm(ps[:, 2, j * P:(j + 1) * P], um[:, j, :], zm[:, j, :], start=True, stop=True)
                        q.done(ins, f"t{l}")
                    for j in range(4):
                        ins = mm(ps[:, 3, j * P:(j + 1) * P], zm[:, j, :], um[:, j, :], start=True, stop=True)
                    q.done(ins, f"u{l}")
                    if name:
                        filler(name, full // 2, full)
                    if l == 1:
                        pe.wait_ge(g_.sem, g_.at("sx1", i))
                        pe.wait_ge(v.sem, v.at("st0", i))
                        settled(pe)
                        for h in H:
                            ins = mm(ps[0:NSM, 4, h * NSM:(h + 1) * NSM], sxm[:, 1, h, :], st_[:, h, :], start=True, stop=True)
                        q.done(ins, "sz1")
                        pe.wait_ge(a.sem, a.at("sz1", i))
                        pe.wait_ge(v.sem, v.at("w1", i))
                        settled(pe)
                        for h in H:
                            ins = mm(ps[0:NSM, 5, h * NSM:(h + 1) * NSM], sz[:, h, :], su[:, h, :], start=True, stop=True)
                        q.done(ins, "su1")
                vt = lambda c, h, n=P: tok[0:n, c, 64 * h:64 * h + 64]

                pe.wait_ge(v.sem, v.at("su1", i))
                for h in H:
                    ins = mm(ps[:, 4, 64 * h:64 * h + 64], kkm[:, h, 0, 0, :], vt(0, h), start=True, stop=True)
                q.done(ins, "g0")
                for h in H:
                    o = ps[0:NSM, 4, P + 64 * h:P + 64 * h + 64]
                    mm(o, sk[:, h, 0, 0, :], vt(2, h, NSM), start=True, stop=False)
                    ins = mm(o, K("ident", NSM)[:, 0:NSM], s0t[0:NSM, h, :], start=False, stop=True)
                q.done(ins, "gs")
                filler("U11", 0, 2)
                pe.wait_ge(a.sem, a.at("gs", i))
                pe.wait_ge(v.sem, v.at("u6", i))
                for h in H:
                    ins = mm(ps[:, 5, 64 * h:64 * h + 64], um[:, 2 * h, :], rhs[:, 0, hs(h)], start=True, stop=True)
                q.done(ins, "sa0")
                for h in H:
                    ins = mm(ps[0:NSM, 5, P + 64 * h:P + 64 * h + 64], su[:, h, :], rhs[0:NSM, 2, hs(h)], start=True, stop=True)
                q.done(ins, "sas")
                pe.wait_ge(a.sem, a.at("sas", i))
                for h in H:
                    o = ps[hs(h), 6, 0:P]
                    mm(o, vt(0, h), kkm[:, h, 0, 1, :], start=True, stop=False)
                    ins = mm(o, nsa[:, 0, hs(h)], bbm[:, h, 0, 1, :], start=False, stop=True)
                q.done(ins, "y0")
                for h in H:
                    o = ps[hs(h), 6, NPR:T]
                    mm(o, vt(2, h, NSM), sk[:, h, 0, 1, :], start=True, stop=False)
                    mm(o, nsa[0:NSM, 2, hs(h)], sk[:, h, 1, 1, :], start=False, stop=True)
                for h in H:
                    o = ps[hs(h), 3, NPR:T]
                    ins = mm(o, s0t[NSM:64, h, :], const[NSM:64, CONST_AT["ident"][0] + NSM:CONST_AT["ident"][0] + 64],
                             start=True, stop=True)
                q.done(ins, "ys")
                for h in H:
                    o = ps[hs(h), 2, 0:64]
                    mm(o, tok[:, 0, P + 64 * h:P + 64 * h + 64], vt(0, h), start=True, stop=False)
                    ins = mm(o, tok[:, 0, 2 * P + 64 * h:2 * P + 64 * h + 64], nsa[:, 0, hs(h)], start=False, stop=True)
                q.done(ins, "s0")
                filler("U11", 2, 4)
                pe.wait_ge(v.sem, v.at("s0", i))
                for h in H:
                    o = ps[:, 4 + h, 0:64]
                    mm(o, kkm[:, h, 1, 0, :], vt(1, h), start=True, stop=False)
                    ins = mm(o, kr[hs(h), 0, P:NPR], st0[hs(h), :], start=False, stop=True)
                q.done(ins, "g1")
                filler("U11", 4, 6)
                pe.wait_ge(a.sem, a.at("g1", i))
                for h in H:
                    ins = mm(ps[:, 4, P + 64 * h:P + 64 * h + 64], um[:, 2 * h + 1, :], rhs[:, 1, hs(h)], start=True, stop=True)
                q.done(ins, "sa1")
                filler("U11", 6, 8)
                pe.wait_ge(a.sem, a.at("sa1", i))
                for h in H:
                    o = ps[hs(h), 6, P:NPR]
                    mm(o, vt(1, h), kkm[:, h, 1, 1, :], start=True, stop=False)
                    mm(o, nsa[:, 1, hs(h)], bbm[:, h, 1, 1, :], start=False, stop=False)
                    ins = mm(o, st0[hs(h), :], kr[hs(h), 1, P:NPR], start=False, stop=True)
                q.done(ins, "y1")
                for h in H:
                    o = ps[hs(h), 2, 0:64]
                    mm(o, tok[:, 1, P + 64 * h:P + 64 * h + 64], vt(1, h), start=True, stop=False)
                    ins = mm(o, tok[:, 1, 2 * P + 64 * h:2 * P + 64 * h + 64], nsa[:, 1, hs(h)], start=False, stop=True)
                q.done(ins, "s1")
                pe.wait_ge(g_.sem, g_.at("nx", i))
                for h in H:
                    o = ps[hs(h), 5, :]
                    mm(o, tok[0:NSM, 2, P + 64 * h:P + 64 * h + 64], vx[:, :, hs(h)], start=True, stop=False)
                    ins = mm(o, tok[0:NSM, 2, 2 * P + 64 * h:2 * P + 64 * h + 64], nx[:, :, hs(h)], start=False, stop=True)
                q.done(ins, "ds")
                pe.wait_ge(v.sem, v.at("ysum", i))
                q.done(mm(ps[:, 3, 0:T], K("heads_mean"), sg, start=True, stop=True), "mean")
                q.done(mm(ps[:, 4, 0:T], K("heads"), rkk, start=True, stop=True), "bonus")
                pe.wait_ge(v.sem, v.at("s1", i))
                pe.wait_ge(a.sem, a.at("sq", i))
                q.done(mm(ps[:, 2, 0:T], K("heads_mean"), csm, start=True, stop=True), "var")

        @block.scalar
        def _(act):
            fn = nc.scalar.activation
            act.sem_inc(a.sem, a.n)
            act.wait_ge(mixed, 1)
            fn(lora[0:64, :], lora[0:64, :], ACT.Tanh).then_inc(mixed, 1)
            with act.Fori(0, N) as i:
                act.wait_ge(q.sem, q.at("z", i))
                a.done(fn(sg, ps[:, 2, 0:T], ACT.Tanh, bias=half[:, bass.ds(i, 1)], scale=0.5), "tz")
                act.wait_ge(q.sem, q.at("a", i))
                a.done(fn(a_, ps[:, 3, 0:T], ACT.Tanh, bias=half[:, bass.ds(i + KH, 1)], scale=0.5), "ta")
                act.wait_ge(v.sem, v.at("kkr", i))
                a.done(fn(ekap, kk, ACT.Square), "kksq")
                act.wait_ge(v.sem, v.at("ssm", i))
                a.done(fn(ek, ek, ACT.Sqrt), "root")
                act.wait_ge(q.sem, q.at("G00", i))
                a.done(fn(gate, ps[:, 0, 0:T], ACT.Tanh, scale=0.5), "G00")
                act.wait_ge(v.sem, v.at("kk", i))
                a.done(fn(ek, er, ACT.Exp, scale=ALPHA), "ek")
                act.wait_ge(a.sem, a.at("ek", i))
                a.done(fn(er, er, ACT.Exp, scale=-ALPHA), "er")
                a.done(fn(ekap, csm, ACT.Exp, scale=-ALPHA), "ekap")
                a.done(fn(ec[:, :], cen[:, :], ACT.Exp, scale=-ALPHA), "ec")
                act.wait_ge(q.sem, q.at("G01", i))
                act.wait_ge(v.sem, v.at("m00", i))
                a.done(fn(gate, ps[:, 0, 0:T], ACT.Tanh, scale=0.5), "G01")
                for c in range(3):
                    n = P if c < 2 else NSM
                    act.wait_ge(q.sem, q.at(f"tr{c}", i))
                    a.done(fn(tok[0:n, c, :], ps[0:n, (5, 6, 2)[c], 0:3 * P], ACT.Copy), f"tr{c}")
                for l in range(1, 7):
                    act.wait_ge(q.sem, q.at(f"z{l}", i))
                    act.wait_ge(q.sem, q.at(f"u{l - 1}", i)) if l > 1 else act.wait_ge(v.sem, v.at("w1", i))
                    a.done(fn(zm, ps[:, 6, :].rearrange("p (j t) -> p j t", j=4), ACT.Copy), f"z{l}")
                    if l == 1:
                        act.wait_ge(q.sem, q.at("sz1", i))
                        a.done(fn(sz[:, :, :], ps[0:NSM, 4, 0:64].rearrange("p (h t) -> p h t", h=2), ACT.Copy), "sz1")
                    if l in (1, 4):
                        act.wait_ge(q.sem, q.at(fill_after[l], i))
                        act.wait_ge(v.sem, v.at(("m01", "m10")[l > 1], i))
                        a.done(fn(gate, ps[:, 0, 0:T], ACT.Tanh, scale=0.5), fill_after[l])
                act.wait_ge(q.sem, q.at("gs", i))
                a.done(fn(rhs[:, 0, :], ps[:, 4, 0:P], ACT.Copy), "g0")
                act.wait_ge(q.sem, q.at("gs", i))
                a.done(fn(rhs[0:NSM, 2, :], ps[0:NSM, 4, P:2 * P], ACT.Copy), "gs")
                act.wait_ge(q.sem, q.at("sas", i))
                a.done(fn(nsa[:, 0, :], ps[:, 5, 0:P], ACT.Copy, scale=-1.0), "sa0")
                act.wait_ge(q.sem, q.at("sas", i))
                a.done(fn(nsa[0:NSM, 2, :], ps[0:NSM, 5, P:2 * P], ACT.Copy, scale=-1.0), "sas")
                act.wait_ge(q.sem, q.at("g1", i))
                fn(rhs[:, 1, 0:64], ps[:, 4, 0:64], ACT.Copy)
                a.done(fn(rhs[:, 1, 64:128], ps[:, 5, 0:64], ACT.Copy), "g1")
                act.wait_ge(q.sem, q.at("sa1", i))
                a.done(fn(nsa[:, 1, :], ps[:, 4, P:2 * P], ACT.Copy, scale=-1.0), "sa1")
                act.wait_ge(q.sem, q.at("y1", i))
                act.wait_ge(v.sem, v.at("dsp", i))
                fn(er[:, NPR:T], ps[:, 3, NPR:T], ACT.Copy)
                a.done(fn(sg, ps[:, 6, 0:T], ACT.Copy), "ys")
                act.wait_ge(v.sem, v.at("d", i))
                a.done(fn(csm, ekap, ACT.Square), "sq")
                act.wait_ge(v.sem, v.at("ve", i))
                a.done(fn(ek, ek, ACT.Sqrt), "groot")

        @block.vector
        def _(dve):
            ts, tt, stt = nc.vector.tensor_scalar, nc.vector.tensor_tensor, nc.vector.scalar_tensor_tensor
            dve.sem_inc(v.sem, v.n)
            dxs = dx[:, NPR + 1:XW].rearrange("p (b l) -> p b l", b=NB)[:, :, 0:NL]
            now = lambda x: x[:, 1 + NPR:XW].rearrange("p (b l) -> p b l", b=NB)[:, :, 1:1 + NL]

            def mix(x, out, mu):
                stt(out=out[:, 0:NPR], in0=dx[:, 0:NPR], scalar=mu, in1=x[:, 1:1 + NPR], op0=ALU.mult, op1=ALU.add)
                return stt(out=seq(out), in0=dxs, scalar=mu, in1=now(x), op0=ALU.mult, op1=ALU.add)
            ts(half[:, 0:KH], param[:, PARAM_AT["w0"]:PARAM_AT["w0"] + KH], 0.5, None, ALU.mult)
            ts(half[:, KH:2 * KH], param[:, PARAM_AT["a0"]:PARAM_AT["a0"] + KH], 0.5, None, ALU.mult)
            tt(dx[:, 0:XW - 1], rwx[:, 24, 0:XW - 1], rwx[:, 24, 1:XW], ALU.subtract).then_inc(dxd, 1)
            dve.wait_ge(dxd, 1)
            mix(rwx[:, 24, :], lora, par("mu", 24)).then_inc(mixed, 1)
            dve.wait_ge(mixed, 1)
            with dve.Fori(0, N) as i:
                W = lambda s: dve.wait_ge(v.sem, v.at(s, i))
                WQ = lambda s: dve.wait_ge(q.sem, q.at(s, i))
                WA = lambda s: dve.wait_ge(a.sem, a.at(s, i))
                before = None
                for n, out, off in (("k", k, 8), ("r", r, 0), ("v", v_, 16)):
                    if before:
                        W(before)
                    before = f"us_{n}"
                    x = rwx[:, bass.ds(i + off, 1), :].rearrange("p o x -> p (o x)")
                    v.done(tt(dx[:, 0:XW - 1], x[:, 0:XW - 1], x[:, 1:XW], ALU.subtract), f"dx_{n}")
                    W(f"dx_{n}")
                    v.done(mix(x, out, par("mu", i + off)), f"us_{n}")
                    if n == "k":
                        W("us_k")
                        v.done(ts(kk, k, par("k_k", i), None, ALU.mult), "kkr")
                WA("tz")
                v.done(ts(sg, sg, 0.5, 0.5, ALU.mult, ALU.add), "sg")
                WA("ta")
                v.done(ts(a_, a_, 0.5, 0.5, ALU.mult, ALU.add), "a")
                W("sg")
                v.done(nc.vector.tensor_tensor_scan(er, K("run_rw"), sg, 0.0, ALU.mult, ALU.add), "cs")
                W("cs")
                v.done(nc.vector.tensor_copy(cen[:, :], er[:, 63:NPR:P]), "cen")
                W("cen")
                for c in H:
                    ins = ts(er[:, c * P:(c + 1) * P], er[:, c * P:(c + 1) * P], cen[:, c:c + 1], None, ALU.subtract)
                v.done(ins, "csc")
                W("csc")
                v.done(tt(csm, er, sg, ALU.subtract), "csm")
                WQ("ss")
                v.done(ts(ek, ps[:, 4, 0:T], 1e-24, None, ALU.max), "ssm")
                WA("root")
                v.done(nc.vector.reciprocal(ek, ek), "rec")
                W("rec")
                v.done(tt(kk, kk, ek, ALU.mult), "kk")
                i2 = i * 2

                def merge(d, b):
                    WQ(f"U{d}{b}")
                    WA(f"G{d}{b}")
                    if b == 1:
                        dve.wait_ge(g_.sem, g_.at("m0", i) if d else g_.at("m1", i - 1))
                    o = gtmp[:, :] if b else mrg[:, bass.ds(i2 + d, 1), :].rearrange("p o t -> p (o t)")
                    v.done(stt(out=o, in0=gate, scalar=1.0, in1=ps[:, (1, 7)[b], 0:T], op0=ALU.add, op1=ALU.mult), f"m{d}{b}")
                merge(0, 0)
                WA("ec")
                W("kk")
                v.done(tt(kr[:, 0, :], kk, ekap, ALU.mult), "kap")
                v.done(tt(kr[:, 1, :], r, er, ALU.mult), "rt")
                v.done(tt(rkk, kk, a_, ALU.mult), "b")
                W("b")
                v.done(tt(kb[:, 1, :], rkk, ek, ALU.mult), "bt")
                v.done(ts(a_, a_, 1.0, par("k_a", i), ALU.subtract, ALU.mult), "ka")
                W("ka")
                v.done(stt(out=k, in0=a_, scalar=1.0, in1=k, op0=ALU.add, op1=ALU.mult), "kp")
                W("kp")
                v.done(tt(kb[:, 0, :], k, ek, ALU.mult), "kt")
                v.done(stt(out=rkk, in0=r, scalar=par("r_k", i), in1=k, op0=ALU.mult, op1=ALU.mult), "rkk")
                merge(0, 1)
                for x in H:
                    for h in H:
                        WQ(f"bk{x}{h}")
                        out = (kkm, bbm)[x][:, h, :, :, :].rearrange("p c x t -> p c (x t)")
                        v.done(tt(out, ps[:, 3 + 2 * x + h, :].rearrange("p (c n) -> p c n", c=2),
                                  K("lt_le").unsqueeze(1).to_broadcast([P, 2, 256]), ALU.mult), f"bk{x}{h}")
                for h in H:
                    WQ(f"sk{h}")
                    v.done(tt(sk[:, h, :, :, :].rearrange("p x y t -> p x (y t)"),
                              ps[0:NSM, 2 + h, 0:128].rearrange("p (x n) -> p x n", x=2),
                              K("seq_lt_le", NSM).unsqueeze(1).to_broadcast([NSM, 2, 64]), ALU.mult), f"sk{h}")
                for h in H:
                    WQ(f"w{h}")
                    if h:
                        W("w0")
                    v.done(tt(wtmp.rearrange("p (b n) -> p b n", b=NB), ps[0:64, 4 + h, :].rearrange("p (b n) -> p b n", b=NB),
                              K("of_seq", 64).unsqueeze(2).to_broadcast([64, NB, 64]), ALU.mult), f"wm{h}")
                    W(f"wm{h}")
                    v.done(nc.vector.tensor_reduce(s0t[:, h, :], wtmp.rearrange("p (b n) -> p n b", b=NB), AX.X, ALU.add), f"w{h}")
                j4 = lambda x: x.rearrange("p (j t) -> p j t", j=4)
                h2 = lambda x: x.rearrange("p (h t) -> p h t", h=2)
                for l in LV:
                    if l == 0:
                        one4 = K("ident").unsqueeze(1).to_broadcast([P, 4, P])
                        one2 = K("ident", NSM)[:, 0:NSM].unsqueeze(1).to_broadcast([NSM, 2, NSM])
                        dve.wait_ge(g_.sem, g_.at("sx0", i))
                        v.done(tt(um, one4, xm[:, 0, :, :], ALU.subtract), "u0")
                        WQ("z0")
                        v.done(tt(tm, one4, j4(ps[:, 6, :]), ALU.subtract), "t0")
                        v.done(tt(su[:, :, :], one2, sxm[:, 0, :, :], ALU.subtract), "su0")
                        WQ("sz0")
                        v.done(tt(st_[:, :, :], one2, h2(ps[0:NSM, 4, 0:64]), ALU.subtract), "st0")
                        continue
                    if l < 6:
                        WQ(f"t{l}")
                        v.done(tt(tm, tm, j4(ps[:, 2, :]), ALU.subtract), f"t{l}")
                    WQ(f"u{l}")
                    v.done(tt(um, um, j4(ps[:, 3, :]), ALU.subtract), f"u{l}")
                    if l == 1:
                        WQ("su1")
                        v.done(tt(su[:, :, :], su[:, :, :], h2(ps[0:NSM, 5, 0:64]), ALU.subtract), "su1")
                    if l == 3:
                        merge(1, 0)
                WQ("s0")
                v.done(ts(st0[:, :], ps[:, 2, 0:64], er[:, P - 1:P], ec[:, 1:2], ALU.mult, ALU.mult), "s0")
                WQ("s1")
                v.done(tt(st1[:, :], ps[:, 2, 0:64], st0[:, :], ALU.add), "s1a")
                W("s1a")
                v.done(ts(st1[:, :], st1[:, :], er[:, NPR - 1:NPR], None, ALU.mult), "s1")
                WQ("ds")
                v.done(tt(sts[:, :, :], sts[:, :, :], ps[:, 5, :].rearrange("p (b n) -> p b n", b=NB), ALU.add), "ds")
                W("ds")
                v.done(tt(sts[:, :, :], sts[:, :, :], seq(er)[:, :, NL - 1:NL].to_broadcast([P, NB, 64]), ALU.mult), "dsp")
                merge(1, 1)
                WA("ys")
                v.done(tt(sg[:, NPR:T], sg[:, NPR:T], er[:, NPR:T], ALU.add), "ysum")
                W("ysum")
                WQ("mean")
                v.done(tt(ekap, sg, ps[:, 3, 0:T], ALU.subtract), "d")
                WQ("var")
                v.done(ts(ek, ps[:, 2, 0:T], GN_EPS, None, ALU.add), "ve")
                WA("groot")
                v.done(nc.vector.reciprocal(ek, ek), "grec")
                W("grec")
                v.done(stt(out=ekap, in0=ekap, scalar=par("gn_w", i), in1=ek, op0=ALU.mult, op1=ALU.mult), "y")
                v.done(tt(csm, v_, ps[:, 4, 0:T], ALU.mult), "bon")
                W("bon")
                v.done(stt(out=rwx[:, bass.ds(i, 1), 0:T].rearrange("p o t -> p (o t)"), in0=ekap, scalar=par("gn_b", i),
                           in1=csm, op0=ALU.add, op1=ALU.add), "o")

        @block.gpsimd
        def _(pool):
            tt = nc.gpsimd.tensor_tensor
            pool.sem_inc(g_.sem, g_.n)

            def spread(out, src):
                return tt(out, src.unsqueeze(1).to_broadcast([NSM, NB, P]),
                          K("of_seq", NSM).unsqueeze(2).to_broadcast([NSM, NB, P]), ALU.mult)
            with pool.Fori(0, N) as i:
                bb = bbm[:, :, :, 0, :].rearrange("p h c t -> p (h c) t")
                for l in LV:
                    if l == 0:
                        pool.wait_ge(v.sem, v.at("bk11", i))
                    if l >= 2:
                        pool.wait_ge(q.sem, q.at(f"z{l - 2}", i))
                        if l == 2:
                            pool.wait_ge(v.sem, v.at("u0", i))
                    g_.done(tt(xm[:, l % 2, :, :], bb, K(f"level{LEVELS[l]}").unsqueeze(1).to_broadcast([P, 4, P]), ALU.mult), f"x{l}")
                    if l < 2:
                        if l == 0:
                            pool.wait_ge(v.sem, v.at("sk1", i))
                        g_.done(tt(sxm[:, l, :, :], sk[:, :, 1, 0, :],
                                   K(f"seq_level{LEVELS[l]}", NSM).unsqueeze(1).to_broadcast([NSM, 2, NSM]), ALU.mult), f"sx{l}")
                    if l == 2:
                        pool.wait_ge(a.sem, a.at("tr2", i))
                        g_.done(spread(vx[:, :, :], tok[0:NSM, 2, 0:P]), "vx")
                    if l == 3:
                        pool.wait_ge(v.sem, v.at("m01", i))
                        m = mrg[:, bass.ds(i * 2, 1), :].rearrange("p o t -> p (o t)")
                        g_.done(tt(m, m, gtmp[:, :], ALU.add), "m0")
                pool.wait_ge(a.sem, a.at("sas", i))
                g_.done(spread(nx[:, :, :], nsa[0:NSM, 2, :]), "nx")
                pool.wait_ge(v.sem, v.at("m11", i))
                m = mrg[:, bass.ds(i * 2 + 1, 1), :].rearrange("p o t -> p (o t)")
                g_.done(tt(m, m, gtmp[:, :], ALU.add), "m1")


class Norm:

    def __init__(self, nc, ctx, name, src, out, gain, bank, width, tmp):
        self.nc, self.src, self.out, self.gain, self.bank, self.width = nc, src, out, gain, bank, width
        self.sq, self.rstd = tmp[:, 0:2, 0:width], tmp[:, 2, 0:width]
        new = lambda n: ctx.enter_context(nc.semaphore(f"{name}_{n}"))
        self.squared = new("squared")
        self.summed = new("summed")
        self.mean, self.rooted = new("mean"), new("root")
        self.inverse = new("inverse")
        self.done = new("done")

    def act(self, act):
        for k in range(KD):
            if k >= 2:
                act.wait_ge(self.summed, k - 1)
            self.nc.scalar.activation(self.sq[:, k % 2, :], self.src[:, k, :], ACT.Square).then_inc(self.squared, 1)
        act.wait_ge(self.mean, 1)
        self.nc.scalar.activation(self.rstd, self.rstd, ACT.Sqrt).then_inc(self.rooted, 1)

    def pe(self, pe, ps, ones):
        for k in range(KD):
            pe.wait_ge(self.squared, k + 1)
            self.nc.tensor.matmul(ps[:, self.bank, 0:self.width], ones, self.sq[:, k % 2, :], start=(k == 0),
                                  stop=(k == KD - 1)).then_inc(self.summed, 1)

    def dve(self, dve, ps):
        dve.wait_ge(self.summed, KD)
        self.nc.vector.tensor_scalar(self.rstd, ps[:, self.bank, 0:self.width], 1.0 / D, RMS_EPS, ALU.mult, ALU.add
                                     ).then_inc(self.mean, 1)
        dve.wait_ge(self.rooted, 1)
        self.nc.vector.reciprocal(self.rstd, self.rstd).then_inc(self.inverse, 1)
        dve.wait_ge(self.inverse, 1)
        for k in range(KD):
            self.nc.vector.scalar_tensor_tensor(out=self.out[:, k, :], in0=self.src[:, k, :], scalar=self.gain(k),
                                                in1=self.rstd, op0=ALU.mult, op1=ALU.mult).then_inc(self.done, 1)


def stage_merge(nc, ctx0, A, O, env):
    ring, xn, mrg, ps, const, K, par, rwx, rounded = (env[k] for k in "ring xn mrg ps const K par rwx rounded".split())
    res = xn
    with ExitStack() as ctx:
        sem = lambda n: ctx.enter_context(nc.semaphore(n))
        gate = ctx.enter_context(nc.sbuf_tensor("gate", [P, 2, T], F32))
        up = ctx.enter_context(nc.sbuf_tensor("up", [P, 2, T], F32))
        x_h, x_l = rounded("gx_high", [P, KD, T], "o_ml"), rounded("gx_rest", [P, KD, T], "xn")
        r_h = ctx.enter_context(nc.sbuf_tensor("gr_high", [P, KH, T], F32R))
        r_l = rounded("gr_rest", [P, KH, XW], "rwx")[:, :, 0:T]
        m_h, m_l = rounded("gm_high", [P, KD, T], "rwx", KH * XW), rounded("gm_rest", [P, KD, T], "mrg")
        wide_h = ctx.enter_context(nc.sbuf_tensor("gw_high", [P, 2, KD, P], F32R))
        half_h = ctx.enter_context(nc.sbuf_tensor("gu_high", [P, 2, KH, P], F32R))
        rest = rounded("gw_rest", [P, 4, SLOT], "ring")
        slots = [sem(f"g_slot{s}") for s in range(4)]
        oslots = [sem(f"g_oslot{s}") for s in range(4)]
        again = sem("g_again")
        N = KH // 2
        xh, xl, rh, rl, mh, ml = (sem(f"g_{n}") for n in ("xh", "xl", "rh", "rl", "mh", "ml"))
        wh, wl, w_used, uh, ul, u_used = (sem(f"g_{n}") for n in ("wh", "wl", "wused", "uh", "ul", "uused"))
        q = Steps(ctx, nc, "g_pe", [f"{x}{d}" for d in range(4) for x in "GU"])
        a = Steps(ctx, nc, "g_act", [f"G{d}" for d in range(4)])
        v = Steps(ctx, nc, "g_dve", [f"{x}{d}" for d in range(4) for x in "um"])
        for s_ in (q, a, v):
            s_.lap = 1
        q2 = Steps(ctx, nc, "g_pe2", [f"o{b}" for b in range(8)])
        v2 = Steps(ctx, nc, "g_dve2", [f"o{b}" for b in range(8)])
        block = ctx.enter_context(nc.Block())

        def tile(t, i):
            return t[bass.ds(i, 1), :, :].rearrange("o p n -> (o p) n")

        def gate_cols(t, n):
            return t[:, 2 * (n // 2 % 2), :].rearrange("p (k n) -> p k n", k=KD)[:, :, (n % 2) * P:(n % 2 + 1) * P]

        def up_cols(t, n):
            return t[:, 2 * (n // 2 % 2) + 1, 0:2048].rearrange("p (k n) -> p k n", k=KH)[:, :, (n % 2) * P:(n % 2 + 1) * P]

        def out_cols(t, j):
            return t[:, j // 2 % 4, :].rearrange("p (k n) -> p k n", k=KD)[:, :, (j % 2) * P:(j % 2 + 1) * P]

        def turns(eng, turn):
            turn(0, True, False)
            with eng.Fori(1, N - 1) as i:
                turn(i, False, False)
            turn(N - 1, False, True)

        @block.sync
        def _(sp):
            with sp.Fori(0, N) as i:
                for s in range(2):
                    sp.wait_ge(q.sem, q.at(f"G{2 * s + 1}", i - 1))
                    sp.dma_start(ring[:, 2 * s, :], tile(A["w_gate"][0], i * 2 + s)).then_inc(slots[2 * s], 16)
                    sp.wait_ge(q.sem, q.at(f"U{2 * s + 1}", i - 1))
                    sp.dma_start(ring[:, 2 * s + 1, 0:2048], tile(A["w_up_rw"], i * 2 + s)).then_inc(slots[2 * s + 1], 16)
            for u in range(8):
                if u < 4:
                    sp.wait_ge(q.sem, q.at(f"{'GU'[u % 2]}{2 * (u // 2) + 1}", N - 1))
                else:
                    sp.wait_ge(q2.sem, q2.at(f"o{2 * (u - 4) + 1}"))
                sp.dma_start(ring[:, u % 4, :], A["w_out"][u, :, :]).then_inc(oslots[u % 4], 16)
                if u == 2:
                    sp.dma_start(res[:, :, :], A["xT"][:, :, :]).then_inc(again, 16)

        @block.tensor
        def _(pe):
            mm = nc.tensor.matmul
            pe.sem_inc(q.sem, q.n)

            def product(bank, n, high, low, x_high, x_low, used, low_ready, ready=None):
                for k in range(n):
                    if ready:
                        for s in ready:
                            pe.wait_ge(s, k + 1)
                    mm(ps[:, bank, 0:T], high[:, k, :], x_high[:, k, :], start=(k == 0), stop=False)
                    ins = mm(ps[:, bank, 0:T], high[:, k, :], x_low[:, k, :], start=False, stop=False)
                ins.then_inc(used, 1)
                pe.wait_ge(*low_ready)
                for k in range(n):
                    ins = mm(ps[:, bank, 0:T], low[:, k, :], x_high[:, k, :], start=False, stop=(k == n - 1))
                return ins

            def turn(i, first, last):
                for d in range(4):
                    pe.wait_ge(wh, i * 4 + d + 1)
                    pe.wait_ge(a.sem, a.at(f"G{d - 2}", i) if d >= 2 else a.at(f"G{d + 2}", i - 1))
                    q.done(product(d % 2, KD, wide_h[:, d % 2], gate_cols(rest, d), x_h, x_l, w_used, (wl, i * 4 + d + 1),
                                   (xh, xl) if first and d == 0 else None), f"G{d}")
                    pe.wait_ge(uh, i * 4 + d + 1)
                    pe.wait_ge(v.sem, v.at(f"u{d - 2}", i) if d >= 2 else v.at(f"u{d + 2}", i - 1))
                    q.done(product(2 + d % 2, KH, half_h[:, d % 2], up_cols(rest, d), r_h, r_l, u_used, (ul, i * 4 + d + 1),
                                   (rh, rl) if first and d == 0 else None), f"U{d}")
            turns(pe, turn)
            for j in range(KD):
                pe.wait_ge(wh, KD + j + 1)
                if j >= 4:
                    pe.wait_ge(v2.sem, v2.at(f"o{(j - 4) % 8}", (j - 4) // 8))
                q2.done(product(4 + j % 4, KD, wide_h[:, j % 2], out_cols(rest, j), m_h, m_l, w_used, (wl, KD + j + 1),
                                (mh, ml) if j == 0 else None), f"o{j % 8}")

        @block.scalar
        def _(act):
            copy = lambda out, src: nc.scalar.activation(out, src, ACT.Copy)
            act.sem_inc(a.sem, a.n)

            def split_gate(n, i):
                if n % 2 == 0:
                    act.wait_ge(slots[2 * (n // 2 % 2)], i * 16 + 16 * (n // 4 + 1))
                if not (isinstance(i, int) and i * 4 + n < 2):
                    act.wait_ge(w_used, i * 4 + n - 1)
                    act.wait_ge(wl, i * 4 + n - 1)
                copy(wide_h[:, n % 2, :, :], gate_cols(ring, n)).then_inc(wh, 1)

            def split_up(n, i):
                if n % 2 == 0:
                    act.wait_ge(slots[2 * (n // 2 % 2) + 1], i * 16 + 16 * (n // 4 + 1))
                if not (isinstance(i, int) and i * 4 + n < 2):
                    act.wait_ge(u_used, i * 4 + n - 1)
                    act.wait_ge(ul, i * 4 + n - 1)
                copy(half_h[:, n % 2, :, :], up_cols(ring, n)).then_inc(uh, 1)

            def split_out(j):
                act.wait_ge(oslots[j // 2 % 4], 16 * (j // 8 + 1))
                act.wait_ge(w_used, KD + j - 1)
                act.wait_ge(wl, KD + j - 1)
                copy(wide_h[:, j % 2, :, :], out_cols(ring, j)).then_inc(wh, 1)

            def turn(i, first, last):
                for d in range(4):
                    if not (last and d == 3):
                        split_gate(d + 1, i)
                        split_up(d + 1, i)
                    else:
                        split_out(0)
                    act.wait_ge(q.sem, q.at(f"G{d}", i))
                    act.wait_ge(v.sem, v.at(f"u{d - 2}", i) if d >= 2 else v.at(f"u{d + 2}", i - 1))
                    a.done(nc.scalar.activation(gate[:, d % 2, :], ps[:, d % 2, 0:T], ACT.Sigmoid), f"G{d}")
            for k in range(KD):
                copy(x_h[:, k, :], xn[:, k, :]).then_inc(xh, 1)
            split_gate(0, 0)
            for k in range(KH):
                copy(r_h[:, k, :], rwx[:, k, 0:T]).then_inc(rh, 1)
            split_up(0, 0)
            turns(act, turn)
            for k in range(KD):
                if k % 4 == 0:
                    act.wait_ge(v.sem, v.at("m3", k // 4))
                copy(m_h[:, k, :], mrg[:, k, :]).then_inc(mh, 1)
            for j in range(1, KD):
                split_out(j)

        @block.vector
        def _(dve):
            tt = nc.vector.tensor_tensor
            dve.sem_inc(v.sem, v.n)

            def rest_gate(n, i):
                dve.wait_ge(wh, i * 4 + n + 1)
                tt(gate_cols(rest, n), gate_cols(ring, n), wide_h[:, n % 2, :, :], ALU.subtract).then_inc(wl, 1)

            def rest_up(n, i):
                dve.wait_ge(uh, i * 4 + n + 1)
                tt(up_cols(rest, n), up_cols(ring, n), half_h[:, n % 2, :, :], ALU.subtract).then_inc(ul, 1)

            def rest_out(j):
                dve.wait_ge(wh, KD + j + 1)
                tt(out_cols(rest, j), out_cols(ring, j), wide_h[:, j % 2, :, :], ALU.subtract).then_inc(wl, 1)

            def turn(i, first, last):
                for d in range(4):
                    if not (last and d == 3):
                        rest_gate(d + 1, i)
                        rest_up(d + 1, i)
                    else:
                        rest_out(0)
                    dve.wait_ge(q.sem, q.at(f"U{d}", i))
                    dve.wait_ge(a.sem, a.at(f"G{d}", i))
                    dve.wait_ge(v.sem, v.at(f"m{d - 2}", i) if d >= 2 else v.at(f"m{d + 2}", i - 1))
                    v.done(tt(up[:, d % 2, :], gate[:, d % 2, :], ps[:, 2 + d % 2, 0:T], ALU.mult), f"u{d}")
                    dve.wait_ge(v.sem, v.at(f"u{d}", i))
                    m = mrg[:, bass.ds(i * 4 + d, 1), :].rearrange("p o t -> p (o t)")
                    v.done(nc.vector.scalar_tensor_tensor(out=m, in0=m, scalar=0.5, in1=up[:, d % 2, :],
                                                          op0=ALU.mult, op1=ALU.add), f"m{d}")
            for k in range(KD):
                dve.wait_ge(xh, k + 1)
                tt(x_l[:, k, :], xn[:, k, :], x_h[:, k, :], ALU.subtract).then_inc(xl, 1)
            rest_gate(0, 0)
            for k in range(KH):
                dve.wait_ge(rh, k + 1)
                tt(r_l[:, k, :], rwx[:, k, 0:T], r_h[:, k, :], ALU.subtract).then_inc(rl, 1)
            rest_up(0, 0)
            turns(dve, turn)
            for k in range(KD):
                dve.wait_ge(mh, k + 1)
                tt(m_l[:, k, :], mrg[:, k, :], m_h[:, k, :], ALU.subtract).then_inc(ml, 1)
            dve.wait_ge(again, 16)
            for j in range(KD):
                if j + 1 < KD:
                    rest_out(j + 1)
                dve.wait_ge(q2.sem, q2.at(f"o{j % 8}", j // 8))
                v2.done(tt(res[:, j, :], res[:, j, :], ps[:, 4 + j % 4, 0:T], ALU.add), f"o{j % 8}")


def stage_cross(nc, ctx0, A, O, env):
    ring, res, xn, ps, const, K, par = (env[k] for k in "ring xn mrg ps const K par".split())
    with ExitStack() as ctx:
        sem = lambda n: ctx.enter_context(nc.semaphore(n))
        sb = lambda n, s: ctx.enter_context(nc.sbuf_tensor(n, s, F32))
        kc = sb("kc", [P, XH, NB, MEM])
        mem = sb("mem", [P, KD, MEM])
        vc = [sb("vc", [P, NB, XH, P]),
              mem[:, :, :].rearrange("p k m -> p (k m)").rearrange("p (b h d) -> p b h d", b=NB, h=XH)]
        mkt = sb("mkt", [P, XH, MEM])
        mv = sb("mv", [P, 2, XH * P])
        qt = sb("qt", [P, XH, T])
        ot = sb("ot", [P, XH, T])
        tmp, tmp2 = sb("ntmp", [P, 3, T]), sb("ntmp2", [P, 3, T])
        pr = tmp[:, :, 0:MEM]
        sT = sb("sT", [P, 2, P])
        pt = sb("pt", [P, 2, 2, P])
        mx, sm = sb("mx", [P, 9]), sb("sm", [P, 9])
        scale = float(P) ** -0.5
        nm = Norm(nc, ctx, "xm", mem, mem, lambda k: par("g_mem", k), 7, MEM, tmp)
        nx_ = Norm(nc, ctx, "xx", res, xn, lambda k: par("g_xa", k), 6, T, tmp2)
        memory, kc_in, vc_in = sem("x_memory"), sem("x_kc"), sem("x_vc")
        vc_in1 = sem("x_vc1")
        slots = [sem(f"x_slot{s}") for s in range(4)]
        stored = sem("x_stored")
        order = [(h, c) for h in range(XH) for c in range(2)] + [None]
        J = range(9)
        SCORE_BANKS = (0, 1, 6)
        pe_steps = [f"k{h}" for h in range(XH)] + [f"v{j}" for j in range(4)] + [f"q{h}" for h in range(XH)]
        AHEAD = 2
        ahead = lambda n, j: [f"{n}{j + AHEAD}"] if j + AHEAD < 9 else []
        pe_steps += ["s0", "s1"] + sum([ahead("s", j) + (["sT"] if j == 4 else []) + [f"t{j}"] + ([f"o{j - 1}"] if j else []) for j in J], []) + ["o8"]
        q = Steps(ctx, nc, "x_pe", pe_steps + [f"w{j}" for j in range(KD)])
        a = Steps(ctx, nc, "x_act", [f"k{h}" for h in range(XH)] + [f"v{m}" for m in range(2)] + [f"q{h}" for h in range(XH)]
                  + ["e0"] + sum([([f"e{j + 1}"] if j < 8 else []) + [f"t{j}"] + (["sT"] if j == 4 else []) + ([f"o{j - 1}"] if j else []) for j in J], []) + ["o8"])
        v = Steps(ctx, nc, "x_dve", ["mx0", "nb0", "mx1", "nb1"] + sum([ahead("mx", j) + ahead("nb", j) + [f"r{j}", f"p{j}"] for j in J], []) + [f"w{j}" for j in range(KD)])
        block = ctx.enter_context(nc.Block())

        @block.sync
        def _(sp):
            sp.dma_start(mem[:, :, :], A["memT"][:, :, :]).then_inc(memory, 16)
            for s, n in enumerate(("w_xk", "w_xv")):
                for u in range(2):
                    sp.dma_start(ring[:, 2 * s + u, :], A[n][u, :, :]).then_inc(slots[2 * s + u], 16)
            sp.dma_start(kc[:, :, :, :], A["kc"][:, :, :, :]).then_inc(kc_in, 16)
            for u in range(2):
                sp.wait_ge(q.sem, q.at(f"k{2 * u + 1}"))
                sp.dma_start(ring[:, u, :], A["w_xq"][u, :, :]).then_inc(slots[u], 16)
            sp.dma_start(vc[0][:, :, :, :], A["vc"][:, 0, :, :, :]).then_inc(vc_in, 16)
            sp.wait_ge(q.sem, q.at("v3"))
            sp.dma_start(vc[1], A["vc"][:, 1, :, :, :]).then_inc(vc_in1, 16)
            for u in range(2):
                sp.wait_ge(q.sem, q.at(f"v{2 * u + 1}"))
                sp.dma_start(ring[:, 2 + u, :], A["w_xo"][u, :, :]).then_inc(slots[2 + u], 16)
            sp.wait_ge(a.sem, a.at("v1"))
            sp.dma_start(O["mk"][:, :, :], mkt[:, :, :]).then_inc(stored, 16)
            sp.dma_start(O["mv"][:, :, :], mv[:, :, :]).then_inc(stored, 16)
            sp.wait_ge(stored, 32)

        @block.tensor
        def _(pe):
            mm, ident = nc.tensor.matmul, K("ident")
            w = [ring[:, s, :].rearrange("p (k n) -> p k n", k=KD) for s in range(4)]
            nm.pe(pe, ps, K("ones"))
            nx_.pe(pe, ps, K("ones"))
            for h in range(XH):
                if h % 2 == 0:
                    pe.wait_ge(slots[h // 2], 16)
                for k in range(KD):
                    if h == 0:
                        pe.wait_ge(nm.done, k + 1)
                    ins = mm(ps[:, h, 0:MEM], w[h // 2][:, k, (h % 2) * P:(h % 2 + 1) * P], mem[:, k, :],
                             start=(k == 0), stop=(k == KD - 1))
                q.done(ins, f"k{h}")
            for u in range(2):
                pe.wait_ge(slots[2 + u], 16)
                for m in range(2):
                    for k in range(KD):
                        ins = mm(ps[:, 4 + m, u * 256:(u + 1) * 256], mem[:, k, m * P:(m + 1) * P], w[2 + u][:, k, :],
                                 start=(k == 0), stop=(k == KD - 1))
                    q.done(ins, f"v{2 * u + m}")
            for h in range(XH):
                if h % 2 == 0:
                    pe.wait_ge(slots[h // 2], 32)
                pe.wait_ge(a.sem, a.at(f"k{h}"))
                for k in range(KD):
                    if h == 0:
                        pe.wait_ge(nx_.done, k + 1)
                    ins = mm(ps[:, h, 0:T], w[h // 2][:, k, (h % 2) * P:(h % 2 + 1) * P], xn[:, k, :],
                             start=(k == 0), stop=(k == KD - 1))
                q.done(ins, f"q{h}")
            pe.wait_ge(kc_in, 16)
            pe.wait_ge(nm.mean, 1)
            pe.wait_ge(a.sem, a.at(f"q{XH - 1}"))
            decode = [(m, h, b) for m in range(2) for h in range(XH) for b in range(NB)]

            def decode_scores(part):
                for m, h, b in decode[13 * part:13 * part + 13]:
                    n = m * P + h * NSM + b * NL
                    ins = mm(ps[:, 7, n:n + NL], kc[:, h, b, m * P:(m + 1) * P], qt[:, h, NPR + b * NL:NPR + (b + 1) * NL],
                             start=True, stop=True)
                if part == 4:
                    q.done(ins, "sT")

            def scores(j):
                bank = SCORE_BANKS[j % 3]
                if j >= 3:
                    pe.wait_ge(a.sem, a.at(f"e{j - 3}"))
                if order[j] is None:
                    pe.wait_ge(a.sem, a.at("sT"))
                    for m in range(2):
                        ins = nc.tensor.transpose(ps[:, bank, m * P:(m + 1) * P], sT[:, m, :], ident)
                else:
                    h, c = order[j]
                    ins = mm(ps[:, bank, 0:MEM], qt[:, h, c * P:(c + 1) * P], mkt[:, h, :], start=True, stop=True)
                q.done(ins, f"s{j}")

            def values(j):
                pe.wait_ge(a.sem, a.at(f"t{j}"))
                if j >= 2:
                    pe.wait_ge(a.sem, a.at(f"o{j - 2}"))
                o = ps[:, 4 + j % 2, 0:P]
                if order[j] is None:
                    pe.wait_ge(vc_in, 16)
                    pe.wait_ge(vc_in1, 16)
                    for h in range(XH):
                        for b in range(NB):
                            n = h * NSM + b * NL
                            for m in range(2):
                                ins = mm(o[:, n:n + NL], vc[m][:, b, h, :], pt[:, j % 2, m, n:n + NL], start=(m == 0), stop=(m == 1))
                else:
                    h, c = order[j]
                    for m in range(2):
                        ins = mm(o, mv[:, m, h * P:(h + 1) * P], pt[:, j % 2, m, :], start=(m == 0), stop=(m == 1))
                q.done(ins, f"o{j}")
            for j in range(AHEAD):
                scores(j)
            for j in J:
                if j + AHEAD < 9:
                    scores(j + AHEAD)
                if j < 5:
                    decode_scores(j)
                pe.wait_ge(v.sem, v.at(f"p{j}"))
                if j >= 2:
                    pe.wait_ge(a.sem, a.at(f"t{j - 2}"))
                for m in range(2):
                    ins = nc.tensor.transpose(ps[:, 2 + j % 2, m * P:(m + 1) * P], pr[:, j % 3, m * P:(m + 1) * P], ident)
                q.done(ins, f"t{j}")
                if j >= 1:
                    values(j - 1)
            values(8)
            pe.wait_ge(a.sem, a.at("o8"))
            for j in range(KD):
                u, c = j // 8, (j % 8) * P
                wo = ring[:, 2 + u, :].rearrange("p (k n) -> p k n", k=XH)
                pe.wait_ge(slots[2 + u], 32)
                if j >= 4:
                    pe.wait_ge(v.sem, v.at(f"w{j - 4}"))
                for k in range(XH):
                    ins = mm(ps[:, j % 4, 0:T], wo[:, k, c:c + P], ot[:, k, :], start=(k == 0), stop=(k == XH - 1))
                q.done(ins, f"w{j}")

        @block.scalar
        def _(act):
            fn = nc.scalar.activation
            act.wait_ge(memory, 16)
            nm.act(act)
            nx_.act(act)
            for h in range(XH):
                act.wait_ge(q.sem, q.at(f"k{h}"))
                a.done(fn(mkt[:, h, :], ps[:, h, 0:MEM], ACT.Copy), f"k{h}")
            for m in range(2):
                act.wait_ge(q.sem, q.at(f"v{2 + m}"))
                a.done(fn(mv[:, m, :], ps[:, 4 + m, :], ACT.Copy), f"v{m}")
            for h in range(XH):
                act.wait_ge(q.sem, q.at(f"q{h}"))
                a.done(fn(qt[:, h, :], ps[:, h, 0:T], ACT.Copy), f"q{h}")

            def exponentials(j):
                act.wait_ge(v.sem, v.at(f"nb{j}"))
                if j >= 3:
                    act.wait_ge(q.sem, q.at(f"t{j - 3}"))
                a.done(fn(pr[:, j % 3, :], ps[:, SCORE_BANKS[j % 3], 0:MEM], ACT.Exp, bias=mx[:, j:j + 1], scale=scale,
                          accum_out=sm[:, j:j + 1]), f"e{j}")

            def results(j):
                act.wait_ge(q.sem, q.at(f"o{j}"))
                if order[j] is None:
                    ins = fn(ot[:, :, NPR:T], ps[:, 4 + j % 2, 0:P].rearrange("p (h n) -> p h n", h=XH), ACT.Copy)
                else:
                    h, c = order[j]
                    ins = fn(ot[:, h, c * P:(c + 1) * P], ps[:, 4 + j % 2, 0:P], ACT.Copy)
                a.done(ins, f"o{j}")
            exponentials(0)
            for j in J:
                if j < 8:
                    exponentials(j + 1)
                act.wait_ge(q.sem, q.at(f"t{j}"))
                if j >= 2:
                    act.wait_ge(q.sem, q.at(f"o{j - 2}"))
                a.done(fn(pt[:, j % 2, :, :], ps[:, 2 + j % 2, 0:2 * P].rearrange("p (m n) -> p m n", m=2), ACT.Copy), f"t{j}")
                if j == 4:
                    act.wait_ge(q.sem, q.at("sT"))
                    a.done(fn(sT[:, :, :], ps[:, 7, 0:2 * P].rearrange("p (m n) -> p m n", m=2), ACT.Copy), "sT")
                if j >= 1:
                    results(j - 1)
            results(8)

        @block.vector
        def _(dve):
            nm.dve(dve, ps)
            nx_.dve(dve, ps)

            def maxima(j):
                dve.wait_ge(q.sem, q.at(f"s{j}"))
                v.done(nc.vector.tensor_reduce(mx[:, j:j + 1], ps[:, SCORE_BANKS[j % 3], 0:MEM], AX.X, ALU.max), f"mx{j}")
                dve.wait_ge(v.sem, v.at(f"mx{j}"))
                v.done(nc.vector.tensor_scalar(mx[:, j:j + 1], mx[:, j:j + 1], -scale, None, ALU.mult), f"nb{j}")
            for j in range(AHEAD):
                maxima(j)
            for j in J:
                if j + AHEAD < 9:
                    maxima(j + AHEAD)
                dve.wait_ge(a.sem, a.at(f"e{j}"))
                v.done(nc.vector.reciprocal(sm[:, j:j + 1], sm[:, j:j + 1]), f"r{j}")
                dve.wait_ge(v.sem, v.at(f"r{j}"))
                v.done(nc.vector.tensor_scalar(pr[:, j % 3, :], pr[:, j % 3, :], sm[:, j:j + 1], None, ALU.mult), f"p{j}")
            for j in range(KD):
                dve.wait_ge(q.sem, q.at(f"w{j}"))
                v.done(nc.vector.tensor_tensor(res[:, j, :], res[:, j, :], ps[:, j % 4, 0:T], ALU.add), f"w{j}")


def stage_moe(nc, ctx0, A, O, env):
    ring, res, xn, ps, const, K, par = (env[k] for k in "ring xn mrg ps const K par".split())
    C, CAP, ROUNDS, PAIRS = 3, 64, -(-T // 64), NE // 2
    HID, NF = 2 * P, 2
    rows = [P, P, NSM]
    BANKS = (0, 1, 6, 7, 4, 5)
    with ExitStack() as ctx:
        sem = lambda n: ctx.enter_context(nc.semaphore(n))
        sb = lambda n, s, t=F32: ctx.enter_context(nc.sbuf_tensor(n, s, t))
        ring2 = sb("ring2", [P, 2, SLOT])
        x2t = sb("x2t", [P, C, D])
        tmp = sb("etmp", [P, 3, T])
        wr, br = sb("wr", [P, KD, 36]), sb("br", [P, 36])
        L = sb("L", [P, C, 36])
        ex, pen, gsum = sb("ex", [P, C, 4]), sb("pen", [P, C, 4]), sb("gsum", [P, C, 1])
        top, first = sb("top", [P, C, 2]), sb("first", [P, C, 2])
        gates, score = sb("gates", [P, C, 2]), sb("score", [P, C, NE])
        pick = [sb(f"pick{n}", [P, C, NE]) for n in range(2)]
        sel, rank = sb("sel", [P, C, NE]), sb("rank", [P, C, NE])
        comb = sb("comb", [P, C, ROUNDS * NE])
        pos = sb("pos", [P, C, ROUNDS * NE])
        count, over = sb("count", [P, 1]), sb("over", [P, ROUNDS - 1])
        turns_f, turns = sb("turns_f", [P, 1]), sb("turns", [P, 1], mybir.dt.int32)
        put = sb("put", [P, C, 2 * CAP])
        take = sb("take", [P, C, 2 * CAP])
        takeT, slot_gate = sb("takeT", [P, T]), sb("slot_gate", [P, 1])
        putT = sb("putT", [P, T], F32R)
        xg = sb("xg", [P, KD, 2 * CAP])
        sg, h = sb("sg", [P, HID]), sb("h", [P, HID])
        hT = sb("hT", [P, NF, 2 * CAP])
        y_h, y_l = (env["rounded"](n, [P, D], "mrg", w) for n, w in (("y_h", 0), ("y_l", D)))

        nm = Norm(nc, ctx, "en", res, xn, lambda k: par("g_moe", k), 7, T, tmp)
        nf = Norm(nc, ctx, "ef", res, xn, lambda k: par("g_final", k), 7, T, tmp)
        wr_in, stored = sem("e_wr"), sem("e_stored")
        last_pe, last = sem("e_last_pe"), sem("e_last")
        slot = [sem(f"e_slot{s}") for s in range(6)]
        ready = [ring[:, s, :] for s in range(4)] + [ring2[:, s, :] for s in range(2)]
        transposes = [(c, g) for c in range(C) for g in range(4)]
        qr = Steps(ctx, nc, "e_pe0", [f"r{c}" for c in range(C)] + [f"x{c}{g}" for c, g in transposes]
                   + [f"rank{c}" for c in range(C)] + ["count"] + [f"g{g}" for g in range(4)])
        ar = Steps(ctx, nc, "e_act0", [f"x{c}{g}" for c, g in transposes] + ["ex", "e2"] + [f"g{g}" for g in range(4)])
        router = (["zero"] + [f"r{c}" for c in range(C)] + ["gmax", "gdiff", "gsum", "pg", "geq", "gidx", "gfirst", "gone", "pen", "le"]
                  + sum([[f"top{n}", f"eq{n}", f"idx{n}", f"first{n}", f"one{n}"] + (["le2"] if n == 0 else []) for n in range(2)], [])
                  + ["dv", "e2p", "g1", "g1p", "g2", "sel", "c0"] + ["comb"] + [f"rank{c}" for c in range(C)]
                  + ["pos0", "pos1"] + ["pos"] + ["count", "over", "osum", "turns", "sel0"])
        vr = Steps(ctx, nc, "e_dve0", router)
        scattered = lambda k: max(0, (k - 3) * KD // (KD - 4))
        between = [range(scattered(k - 1), scattered(k)) for k in range(KD)]
        pe_steps = ["t"]
        for k in range(KD):
            pe_steps += [f"u{k // 8}"] * (k % 8 == 7) + [f"s{j}" for j in between[k]]
        q = Steps(ctx, nc, "e_pe", pe_steps + ["x0", "x1", "h", "x2", "x3"] + [f"d{n}" for n in range(4)])
        a = Steps(ctx, nc, "e_act", ["t", "g", "x0", "x1", "h", "x2", "x3"] + [f"y{n}" for n in range(4)])
        v = Steps(ctx, nc, "e_dve", ["sel"] + [f"s{k}" for k in range(KD)] + ["m", "h", "put", "y"])
        for s_ in (q, a, v):
            s_.lap = 1
        block = ctx.enter_context(nc.Block())

        def last_turn(eng):
            eng.wait_ge(vr.sem, vr.at("turns"))
            return eng.value_load(turns[0:1, 0:1], min_val=PAIRS - 1, max_val=PAIRS * ROUNDS - 1)

        @block.sync
        def _(sp):
            def load(j, i):
                for n in range(2):
                    if i is not None:
                        sp.wait_ge(q.sem, q.at(f"u{n}", i - 1))
                    for u in range(2):
                        sp.dma_start(ready[2 * n + u], A["w_egu"][bass.ds(j * 2 + u, 1), n, :, :].rearrange("o p n -> (o p) n")
                                     ).then_inc(slot[2 * n + u], 16)
                if i is not None:
                    sp.wait_ge(q.sem, q.at("d3", i - 1))
                for u in range(2):
                    sp.dma_start(ready[4 + u], A["w_ed"][bass.ds(j * 2 + u, 1), :, :].rearrange("o p n -> (o p) n")
                                 ).then_inc(slot[4 + u], 16)
            sp.dma_start(wr[:, :, :], A["w_router"][:, :, :]).then_inc(wr_in, 16)
            sp.dma_start(br[:, :], A["b_router"][:, :]).then_inc(wr_in, 16)
            load(0, None)
            with sp.Fori(1, last_turn(sp) + 1) as i:
                load(i % PAIRS, i)
            sp.wait_ge(nf.done, KD)
            sp.dma_start(O["y"][:, :, :], xn[:, :, :]).then_inc(stored, 16)
            sp.wait_ge(stored, 16)

        @block.tensor
        def _(pe):
            mm, ident = nc.tensor.matmul, K("ident")
            nm.pe(pe, ps, K("ones"))
            pe.wait_ge(wr_in, 32)
            for c in range(C):
                for k in range(KD):
                    if c == 0:
                        pe.wait_ge(nm.done, k + 1)
                    ins = mm(ps[0:rows[c], c, 0:36], xn[:, k, c * P:c * P + rows[c]], wr[:, k, :],
                             start=(k == 0), stop=(k == KD - 1))
                qr.done(ins, f"r{c}")
            for n, (c, g) in enumerate(transposes):
                if n >= 2:
                    pe.wait_ge(ar.sem, ar.at("x%d%d" % transposes[n - 2]))
                for k in range(4):
                    ins = nc.tensor.transpose(ps[0:rows[c], 4 + n % 2, k * P:(k + 1) * P],
                                              xn[:, g * 4 + k, c * P:c * P + rows[c]], ident)
                qr.done(ins, f"x{c}{g}")
            pe.wait_ge(vr.sem, vr.at("sel"))
            earlier, ones = K("lt_le", b=P), K("ones")
            for c in range(C):
                for e in range(c + 1):
                    left = (earlier if e == c else ones)[0:rows[e], 0:rows[c]]
                    ins = mm(ps[0:rows[c], c, 0:NE], left, sel[0:rows[e], e, :], start=(e == 0), stop=(e == c))
                qr.done(ins, f"rank{c}")
            for e in range(C):
                ins = mm(ps[:, 3, 0:NE], ones[0:rows[e], :], sel[0:rows[e], e, :], start=(e == 0), stop=(e == C - 1))
            qr.done(ins, "count")
            pe.wait_ge(ar.sem, ar.at("x23"))

            def scatter(k, i):
                if k >= len(BANKS):
                    pe.wait_ge(v.sem, v.at(f"s{k - len(BANKS)}", i + 1))
                o = ps[:, BANKS[k % len(BANKS)], 0:T]
                mm(o, y_h[:, k * P:(k + 1) * P], putT[:, :], start=True, stop=False)
                q.done(mm(o, y_l[:, k * P:(k + 1) * P], putT[:, :], start=False, stop=True), f"s{k}")

            def gather(g):
                for k in range(4 * g, 4 * g + 4):
                    for c in range(C):
                        ins = mm(ps[:, g % 2, (k % 4) * P:(k % 4 + 1) * P], x2t[0:rows[c], c, k * P:(k + 1) * P],
                                 put[0:rows[c], c, :], start=(c == 0), stop=(c == C - 1))
                return ins

            def turn(i, last):
                pe.wait_ge(a.sem, a.at("h", i - 1))
                for c in range(C):
                    ins = nc.tensor.transpose(ps[:, 3, c * P:c * P + rows[c]], take[0:rows[c], c, :],
                                              K("ident", rows[c], 0, rows[c]))
                q.done(ins, "t")
                for k in range(KD):
                    if k % 4 == 0:
                        pe.wait_ge(a.sem, a.at(f"x{k // 4}", i - 1))
                    for u in range(2):
                        s = 2 * (k // 8) + u
                        if k % 8 == 0:
                            pe.wait_ge(slot[s], i * 16 + 16)
                        w = ready[s].rearrange("p (k f) -> p k f", k=KD // 2)
                        ins = mm(ps[u * CAP:(u + 1) * CAP, 2, :], xg[:, k, u * CAP:(u + 1) * CAP], w[:, k % 8, :],
                                 start=(k == 0), stop=(k == KD - 1))
                    if k % 8 == 7:
                        q.done(ins, f"u{k // 8}")
                    for j in between[k]:
                        if j == 0:
                            pe.wait_ge(v.sem, v.at("y", i - 1))
                        scatter(j, i - 1)
                if not last:
                    pe.wait_ge(v.sem, v.at("sel", i))
                for g in range(4):
                    if g == 2:
                        pe.wait_ge(v.sem, v.at("h", i))
                        pe.wait_ge(a.sem, a.at("t", i))
                        for f in range(NF):
                            ins = nc.tensor.transpose(ps[:, 3, f * P:(f + 1) * P], h[:, f * P:(f + 1) * P], ident)
                        q.done(ins, "h")
                    if last:
                        q.left_out(pe, f"x{g}", i)
                        continue
                    if g >= 2:
                        pe.wait_ge(a.sem, a.at(f"x{g - 2}", i))
                    else:
                        pe.wait_ge(v.sem, v.at(f"s{12 + g}", i))
                    q.done(gather(g), f"x{g}")
                pe.wait_ge(a.sem, a.at("h", i))
                for u in range(2):
                    pe.wait_ge(slot[4 + u], i * 16 + 16)
                for n in range(4):
                    pe.wait_ge(v.sem, v.at(f"s{max(k for k in range(KD) if BANKS[k % len(BANKS)] == 4 + n)}", i))
                    for f in range(NF):
                        for u in range(2):
                            w = ready[4 + u].rearrange("p (f d) -> p f d", f=NF)
                            ins = mm(ps[u * CAP:(u + 1) * CAP, 4 + n, :], hT[:, f, u * CAP:(u + 1) * CAP],
                                     w[:, f, n * 512:(n + 1) * 512], start=(f == 0), stop=(f == NF - 1))
                    q.done(ins, f"d{n}")
            pe.wait_ge(vr.sem, vr.at("sel0"))
            for g in range(4):
                if g >= 2:
                    pe.wait_ge(ar.sem, ar.at(f"g{g - 2}"))
                qr.done(gather(g), f"g{g}")
            pe.wait_ge(ar.sem, ar.at("g3"))
            end = last_turn(pe)
            pe.sem_inc(q.sem, q.n)
            with pe.Fori(0, end) as i:
                turn(i, False)
            turn(end, True)
            pe.wait_ge(v.sem, v.at(f"s{KD - 1}", end))
            pe.wait_ge(v.sem, v.at("y", end))
            for k in range(KD):
                if k >= 4:
                    pe.wait_ge(last, k - 3)
                mm(ps[:, k % 4, 0:T], y_h[:, k * P:(k + 1) * P], putT[:, :], start=True, stop=False)
                mm(ps[:, k % 4, 0:T], y_l[:, k * P:(k + 1) * P], putT[:, :], start=False, stop=True).then_inc(last_pe, 1)
            nf.pe(pe, ps, K("ones"))

        @block.scalar
        def _(act):
            fn = nc.scalar.activation
            nm.act(act)
            for n, (c, g) in enumerate(transposes):
                act.wait_ge(qr.sem, qr.at(f"x{c}{g}"))
                ar.done(fn(x2t[0:rows[c], c, g * 512:(g + 1) * 512], ps[0:rows[c], 4 + n % 2, :], ACT.Copy), f"x{c}{g}")
            act.wait_ge(vr.sem, vr.at("gdiff"))
            ar.done(fn(ex[:, :, :], ex[:, :, :], ACT.Exp), "ex")
            act.wait_ge(vr.sem, vr.at("dv"))
            ar.done(fn(gates[:, :, 1:2], gates[:, :, 1:2], ACT.Exp), "e2")
            def place(g):
                return fn(xg[:, 4 * g:4 * g + 4, :].rearrange("p k s -> p (k s)"), ps[:, g % 2, :], ACT.Copy)

            def turn(i, last):
                act.wait_ge(q.sem, q.at("t", i))
                act.wait_ge(v.sem, v.at("y", i - 1))
                a.done(fn(takeT[:, :], ps[:, 3, 0:T], ACT.Copy, accum_out=slot_gate[:, :]), "t")
                act.wait_ge(q.sem, q.at("u1", i))
                act.wait_ge(v.sem, v.at("h", i - 1))
                a.done(fn(sg[:, :], ps[:, 2, 0:HID], ACT.Sigmoid), "g")
                for g in range(4):
                    if g == 2:
                        act.wait_ge(q.sem, q.at("h", i))
                        act.wait_ge(q.sem, q.at("d3", i - 1))
                        a.done(fn(hT[:, :, :].rearrange("p f s -> p (f s)"), ps[:, 3, 0:HID], ACT.Copy), "h")
                    if last:
                        a.left_out(act, f"x{g}", i)
                        continue
                    act.wait_ge(q.sem, q.at(f"x{g}", i))
                    a.done(place(g), f"x{g}")
                act.wait_ge(a.sem, a.at("t", i))
                for n in range(4):
                    act.wait_ge(q.sem, q.at(f"d{n}", i))
                    a.done(fn(y_h[:, n * 512:(n + 1) * 512], ps[:, 4 + n, :], ACT.Copy, scale=slot_gate[:, 0:1]), f"y{n}")
            for g in range(4):
                act.wait_ge(qr.sem, qr.at(f"g{g}"))
                ar.done(place(g), f"g{g}")
            end = last_turn(act)
            act.sem_inc(a.sem, a.n)
            with act.Fori(0, end) as i:
                turn(i, False)
            turn(end, True)
            act.wait_ge(last, KD)
            nf.act(act)

        @block.vector
        def _(dve):
            tt, ts, stt = nc.vector.tensor_tensor, nc.vector.tensor_scalar, nc.vector.scalar_tensor_tensor
            red = nc.vector.tensor_reduce

            def then(ins, step):
                vr.done(ins, step)
                dve.wait_ge(vr.sem, vr.at(step))
            nc.vector.memset(put[:, :, :], 0.0)
            nc.vector.memset(take[:, :, :], 0.0)
            then(nc.vector.memset(L[:, :, :], 0.0), "zero")
            nm.dve(dve, ps)
            dve.wait_ge(wr_in, 32)
            for c in range(C):
                dve.wait_ge(qr.sem, qr.at(f"r{c}"))
                then(tt(L[0:rows[c], c, :], ps[0:rows[c], c, 0:36], br[0:rows[c], :], ALU.add), f"r{c}")
            wide = lambda t, n: t.to_broadcast([P, C, n])
            number = K("expert_id").unsqueeze(1)
            lg = L[:, :, 0:4]
            then(red(top[:, :, 0:1], lg, AX.X, ALU.max), "gmax")
            then(tt(ex[:, :, :], lg, wide(top[:, :, 0:1], 4), ALU.subtract), "gdiff")
            dve.wait_ge(ar.sem, ar.at("ex"))
            then(red(gsum[:, :, :], ex[:, :, :], AX.X, ALU.add), "gsum")
            then(nc.vector.reciprocal(gsum[:, :, :], gsum[:, :, :]), "pg")
            then(tt(pen[:, :, :], lg, wide(top[:, :, 0:1], 4), ALU.is_ge), "geq")
            then(stt(out=pen[:, :, :], in0=pen[:, :, :], scalar=-1000.0, in1=number[:, :, 0:4].to_broadcast([P, C, 4]),
                     op0=ALU.mult, op1=ALU.add), "gidx")
            then(red(first[:, :, 0:1], pen[:, :, :], AX.X, ALU.min), "gfirst")
            then(tt(pen[:, :, :], pen[:, :, :], wide(first[:, :, 0:1], 4), ALU.is_equal), "gone")
            then(ts(pen[:, :, :], pen[:, :, :], 1e30, -1e30, ALU.mult, ALU.add), "pen")
            by_group = lambda t: t.rearrange("p c (g e) -> p c g e", g=4)
            for c in range(C):
                ins = tt(by_group(L[:, :, 4:36])[:, c], by_group(L[:, :, 4:36])[:, c],
                         pen[:, c, :].unsqueeze(2).to_broadcast([P, 4, 8]), ALU.add)
            then(ins, "le")
            le = L[:, :, 4:36]
            for n in range(2):
                then(red(top[:, :, n:n + 1], le, AX.X, ALU.max), f"top{n}")
                then(tt(score[:, :, :], le, wide(top[:, :, n:n + 1], NE), ALU.is_ge), f"eq{n}")
                then(stt(out=score[:, :, :], in0=score[:, :, :], scalar=-1000.0, in1=number.to_broadcast([P, C, NE]),
                         op0=ALU.mult, op1=ALU.add), f"idx{n}")
                then(red(first[:, :, n:n + 1], score[:, :, :], AX.X, ALU.min), f"first{n}")
                then(tt(pick[n][:, :, :], score[:, :, :], wide(first[:, :, n:n + 1], NE), ALU.is_equal), f"one{n}")
                if n == 0:
                    then(stt(out=le, in0=pick[0][:, :, :], scalar=-2e30, in1=le, op0=ALU.mult, op1=ALU.add), "le2")
            then(tt(gates[:, :, 1:2], top[:, :, 1:2], top[:, :, 0:1], ALU.subtract), "dv")
            dve.wait_ge(ar.sem, ar.at("e2"))
            then(ts(gates[:, :, 0:1], gates[:, :, 1:2], 1.0, None, ALU.add), "e2p")
            then(nc.vector.reciprocal(gates[:, :, 0:1], gates[:, :, 0:1]), "g1")
            then(tt(gates[:, :, 0:1], gates[:, :, 0:1], gsum[:, :, :], ALU.mult), "g1p")
            then(tt(gates[:, :, 1:2], gates[:, :, 1:2], gates[:, :, 0:1], ALU.mult), "g2")
            then(tt(sel[:, :, :], pick[0][:, :, :], pick[1][:, :, :], ALU.add), "sel")
            tt(pick[0][:, :, :], pick[0][:, :, :], wide(gates[:, :, 0:1], NE), ALU.mult)
            then(tt(pick[1][:, :, :], pick[1][:, :, :], wide(gates[:, :, 1:2], NE), ALU.mult), "c0")
            for r in range(ROUNDS):
                ins = tt(comb[:, :, r * NE:(r + 1) * NE], pick[0][:, :, :], pick[1][:, :, :], ALU.add)
            then(ins, "comb")
            for c in range(C):
                dve.wait_ge(qr.sem, qr.at(f"rank{c}"))
                ins = nc.vector.tensor_copy(rank[0:rows[c], c, :], ps[0:rows[c], c, 0:NE])
                then(ins, f"rank{c}")
            for c in range(C):
                ins = stt(out=rank[0:rows[c], c, :], in0=rank[0:rows[c], c, :], scalar=1.0, in1=sel[0:rows[c], c, :],
                          op0=ALU.add, op1=ALU.mult)
            then(ins, "pos0")
            for c in range(C):
                ins = ts(rank[0:rows[c], c, :], rank[0:rows[c], c, :], -1.0, None, ALU.add)
            then(ins, "pos1")
            for c in range(C):
                for r in range(ROUNDS):
                    ins = ts(pos[0:rows[c], c, r * NE:(r + 1) * NE], rank[0:rows[c], c, :], float(-r * CAP), None, ALU.add)
            then(ins, "pos")
            dve.wait_ge(qr.sem, qr.at("count"))
            then(red(count[:, :], ps[:, 3, 0:NE], AX.X, ALU.max), "count")
            for r in range(1, ROUNDS):
                ins = ts(over[:, r - 1:r], count[:, :], float(r * CAP), float(PAIRS), ALU.is_gt, ALU.mult)
            then(ins, "over")
            then(red(turns_f[:, :], over[:, :], AX.X, ALU.add), "osum")
            then(ts(turns[:, :], turns_f[:, :], float(PAIRS - 1), None, ALU.add), "turns")

            def select(i):
                for c in range(C):
                    for u in range(2):
                        at = lambda t: t[0:rows[c], c, bass.ds(i * 2 + u, 1)]
                        o = slice(u * CAP, (u + 1) * CAP)
                        ts(put[0:rows[c], c, o], K("slot_id", rows[c]), at(pos), None, ALU.is_equal)
                        ins = ts(take[0:rows[c], c, o], K("slot_id", rows[c]), at(pos), at(comb), ALU.is_equal, ALU.mult)
                return ins
            for o in (y_h, y_l, putT):
                ts(o[:, :], const[:, 0:o.shape[1]], 0.0, None, ALU.mult)
            then(select(0), "sel0")

            def turn(i, last):
                if last:
                    v.left_out(dve, "sel", i)
                else:
                    dve.wait_ge(q.sem, q.at("t", i))
                    v.done(select(i + 1), "sel")
                for k in range(KD):
                    dve.wait_ge(q.sem, q.at(f"s{k}", i))
                    v.done(tt(res[:, k, :], res[:, k, :], ps[:, BANKS[k % len(BANKS)], 0:T], ALU.add), f"s{k}")
                dve.wait_ge(a.sem, a.at("g", i))
                v.done(tt(sg[:, :], sg[:, :], ps[:, 2, 0:HID], ALU.mult), "m")
                dve.wait_ge(v.sem, v.at("m", i))
                dve.wait_ge(q.sem, q.at("h", i - 1))
                v.done(tt(h[:, :], sg[:, :], ps[:, 2, HID:2 * HID], ALU.mult), "h")
                dve.wait_ge(a.sem, a.at("t", i))
                v.done(ts(putT[:, :], takeT[:, :], 0.0, None, ALU.is_gt), "put")
                for n in range(4):
                    dve.wait_ge(a.sem, a.at(f"y{n}", i))
                    o = slice(n * 512, (n + 1) * 512)
                    ins = stt(out=y_l[:, o], in0=ps[:, 4 + n, :], scalar=slot_gate[:, 0:1], in1=y_h[:, o], op0=ALU.mult,
                              op1=ALU.subtract)
                v.done(ins, "y")
            end = last_turn(dve)
            dve.sem_inc(v.sem, v.n)
            with dve.Fori(0, end) as i:
                turn(i, False)
            turn(end, True)
            dve.wait_ge(v.sem, v.at(f"s{KD - 1}", end))
            for k in range(KD):
                dve.wait_ge(last_pe, k + 1)
                tt(res[:, k, :], res[:, k, :], ps[:, k % 4, 0:T], ALU.add).then_inc(last, 1)
            dve.wait_ge(last, KD)
            nf.dve(dve, ps)



def feature_cols(a):
    a = np.asarray(a)
    f = a.shape[-1]
    lead = a.shape[:-1]
    a = a.reshape(*lead, f // P, P)
    return np.ascontiguousarray(np.moveaxis(np.moveaxis(a, -1, 0), -1, 1))


def weight_units(w, width=256):
    k, n = w.shape
    return np.ascontiguousarray(w.reshape(k // P, P, n // width, width).transpose(2, 1, 0, 3)).reshape(n // width, P, -1)


def lay_out(i):
    g = {n: np.asarray(v) for n, v in i.items()}
    w = g["w_in"][0]
    x = np.concatenate([g["x_prompt"][0], g["x_sample"].reshape(NSM, D)], 0)
    a = {"const": CONST, "xT": feature_cols(x)}
    vec = dict(mu="rw_mu", w0="rw_w0", a0="rw_a0", k_k="rw_k_k", k_a="rw_k_a", r_k="rw_r_k", gn_w="rw_gn_w",
               gn_b="rw_gn_b", ml_gn="ml_gn_w", pool_scale="pool_scale", g_mix="g_mix", g_xa="g_xa", g_mem="g_mem",
               g_moe="g_moe", g_final="g_final")
    a["param"] = np.concatenate([g[vec[n]].reshape(-1, P).T for n, _ in PARAMS], 1)
    a["w_main"] = weight_units(np.concatenate([w[:, 0:3072], w[:, 3200:6272], w[:, 6280:7304], w[:, 3072:3200],
                                               w[:, 6272:6280], np.zeros((D, 120), np.float32)], 1))
    a["past"] = np.concatenate([feature_cols(g["state_rwkv_shift"][0]).reshape(P, -1),
                                feature_cols(g["state_pool"][0]).reshape(P, -1)], 1)
    small = np.zeros((P, 42), np.float32)
    small[:, 0:32] = g["state_mlstm_n"][0].transpose(2, 1, 0).reshape(P, 32)
    small[0:4, 32], small[0:4, 33] = g["ml_b_i"][0], g["ml_b_f"][0]
    small[0:4, 34:42] = g["state_mlstm_m"][0].T
    a["ml_small"] = small
    pairs = lambda w: weight_units(w)
    a["w_gate"] = np.stack([pairs(w[:, 7304 + b * D:7304 + (b + 1) * D]) for b in range(3)])
    a["w_up_rw"] = weight_units(g["w_up_rwkv"][0])
    a["w_out"] = weight_units(g["w_out"][0])
    a["memT"] = feature_cols(g["mem_prompt"][0])
    a["w_xk"], a["w_xv"], a["w_xq"] = (weight_units(g[n][0]) for n in ("xa_wk", "xa_wv", "xa_wq"))
    a["w_xo"] = weight_units(g["xa_wo"][0], 1024)
    a["w_router"] = feature_cols(np.concatenate([g["moe_wr1"][0], g["moe_wr2"][0]], 1).T)
    a["b_router"] = np.tile(np.concatenate([g["moe_br1"][0], g["moe_br2"][0]]), (P, 1))
    gu = np.concatenate([g["moe_wg"][0], g["moe_wu"][0]], 2).reshape(NE, 2, KH, P, 4 * P)
    a["w_egu"] = gu.transpose(0, 1, 3, 2, 4).reshape(NE, 2, P, SLOT)
    a["w_ed"] = g["moe_wd"][0].reshape(NE, 2, P, D).transpose(0, 2, 1, 3).reshape(NE, P, SLOT)
    a["kc"] = g["cache_mem_k"][0].transpose(3, 2, 0, 1)
    a["vc"] = g["cache_mem_v"][0].reshape(NB, 2, P, XH, P).transpose(2, 1, 0, 3, 4)
    a["w_up2"] = np.concatenate([pairs(g["w_up_mlstm"][0]), pairs(g["w_up_pool"][0])], 2)
    a["w_lora"] = np.concatenate([g["rw_w2"][0], g["rw_a2"][0]], 0).reshape(P, KH, P).transpose(1, 0, 2)
    a["rw_s"] = g["state_rwkv_s"][0].reshape(NB, KH, 2, 64, 64).transpose(1, 2, 4, 0, 3).reshape(KH, P, NB, 64)
    a["pool_w"] = g["pool_w"][0].reshape(4, 2, P, 256).transpose(2, 0, 1, 3)
    a["c_in"] = g["state_mlstm_c"][0].transpose(1, 2, 0, 3)
    return {n: np.ascontiguousarray(v) for n, v in a.items()}


OUTS = {"y": (P, KD, T), "mk": (P, XH, MEM), "mv": (P, 2, XH * P), "rw_p": (KH, P, 64), "rw_s": (KH, P, NB, 64), "ml_n": (P, MLH, 9), "ml_m": (MLH, T), "shift": (P, RWT, 9), "pool": (P, KH, 9, BUF), "ml_cp": (MLH, P, DV),
        "ml_cs": (MLH, P, NB, DV)}


def feature_rows(a):
    a = np.moveaxis(a, (0, 1), (-1, -2))
    return np.ascontiguousarray(a).reshape(*a.shape[:-2], -1)


def give_back(o):
    shift = feature_rows(o["shift"])
    pool = feature_rows(o["pool"])
    n = o["ml_n"].transpose(2, 1, 0)
    m = o["ml_m"]
    mk = o["mk"].transpose(2, 1, 0)[None, None]
    mv = o["mv"].transpose(1, 0, 2).reshape(1, 1, MEM, XH, P)
    rw_p = o["rw_p"].reshape(KH, 2, 64, 64).transpose(0, 1, 3, 2).reshape(1, 1, 16, 64, 64)
    rw_s = o["rw_s"].reshape(KH, 2, 64, NB, 64).transpose(3, 0, 1, 4, 2).reshape(1, NB, 16, 64, 64)
    y = feature_rows(o["y"])
    return (y[None, 0:NPR], y[NPR:T].reshape(NB, NL, D), rw_p, shift[None, 0:1], o["ml_cp"][None, None], n[None, 0:1], m[:, NPR - 1][None, None], pool[None, 0:1],
            mk, mv, rw_s, shift[None, 1:9], o["ml_cs"].transpose(2, 0, 1, 3)[None], n[None, 1:9],
            np.ascontiguousarray(m[:, NPR + NL - 1::NL].T)[None], pool[None, 1:9])


def kernel(**inputs):
    import concourse.bacc as bacc
    from concourse.bass_utils import run_bass_kernel_spmd

    nc = bacc.Bacc("TRN2", target_bir_lowering=False, num_devices=1)
    arrays = lay_out(inputs)
    A = {n: nc.dram_tensor(f"in_{n}", a.shape, F32, kind="ExternalInput").ap() for n, a in arrays.items()}
    O = {n: nc.dram_tensor(f"out_{n}", s, F32, kind="ExternalOutput").ap() for n, s in OUTS.items()}
    program(nc, A, O)
    r = run_bass_kernel_spmd(nc, [{f"in_{n}": a for n, a in arrays.items()}], core_ids=[0])
    return give_back({n: r.results[0][f"out_{n}"] for n in OUTS})
```
